# Optimizing a Trainium2 kernel written in Bass

```python
import math
import jax, jax.numpy as jnp
from jax import lax
import numpy as np

D_MODEL = 1024
BATCH = 1
SEQ = 256
DEPTH = 2

CHUNK = 64
Q_BLOCK = 128
D_MIX = D_MODEL
CONV_CH = D_MIX // 4
CONV_WIDTH = 31
DIFF_HEADS = 4
DIFF_DV = D_MIX // 8
DIFF_DH = DIFF_DV // 2
GLA_HEADS = 4
GLA_DV = D_MIX // 16
GLA_DK = GLA_DV // 2
GLA_GATE_RANK = 16
GLA_TAU = 16.0
ROPE_THETA = 500000.0
ROT_DIMS = DIFF_DH // 4
D_FF = 2816
N_EXPERTS = 8
TOP_K = 2
D_FF_EXPERT = 3584
EXPERT_BLOCK = 256
PLE_DIM = 256
EPS = 1e-6

DIFF_QK = DIFF_HEADS * 2 * DIFF_DH
DIFF_V = DIFF_HEADS * DIFF_DV
GLA_QK = GLA_HEADS * GLA_DK
GLA_V = GLA_HEADS * GLA_DV
IN_SPLITS = (CONV_CH, CONV_CH, DIFF_QK, DIFF_QK, DIFF_V, GLA_QK, GLA_QK, GLA_V, GLA_V, GLA_GATE_RANK)
D_IN = CONV_CH * 2 + DIFF_QK * 2 + DIFF_V + GLA_QK * 2 + GLA_V * 2 + GLA_GATE_RANK

kernel_name = "hybrid_conv_diffattn_gla_moe_trunk"

def rmsnorm(x, g):
    xf = x.astype(jnp.float32)
    y = xf * lax.rsqrt(jnp.mean(xf * xf, axis=-1, keepdims=True) + EPS)
    return (y * g.astype(jnp.float32)).astype(x.dtype)

def layernorm(x, g, b):
    xf = x.astype(jnp.float32)
    mu = jnp.mean(xf, axis=-1, keepdims=True)
    var = jnp.mean(jnp.square(xf - mu), axis=-1, keepdims=True)
    y = (xf - mu) * lax.rsqrt(var + EPS)
    return (y * g.astype(jnp.float32) + b.astype(jnp.float32)).astype(x.dtype)

def rope_partial(x, cos, sin):
    half = ROT_DIMS // 2
    bshape = (x.shape[1],) + (1,) * (x.ndim - 3) + (half,)
    c = cos.reshape(bshape)
    s = sin.reshape(bshape)
    xf = x.astype(jnp.float32)
    x1 = xf[..., :half]
    x2 = xf[..., half:ROT_DIMS]
    out = jnp.concatenate([x1 * c - x2 * s, x2 * c + x1 * s, xf[..., ROT_DIMS:]], axis=-1)
    return out.astype(x.dtype)

def conformer_conv(a, g, w, b, ln_g, ln_b):
    u = a * jax.nn.sigmoid(g)
    y = lax.conv_general_dilated(u, w[:, None, :].astype(u.dtype), window_strides=(1,),
                                 padding=[(CONV_WIDTH - 1, 0)],
                                 dimension_numbers=('NWC', 'WIO', 'NWC'),
                                 feature_group_count=CONV_CH) + b
    return jax.nn.silu(layernorm(y, ln_g, ln_b))

def diff_attention(q, k, v, lam, subln_g, lam_init):
    bsz, seq = q.shape[0], q.shape[1]
    nqb = seq // Q_BLOCK
    qb = jnp.moveaxis(q.reshape(bsz, nqb, Q_BLOCK, DIFF_HEADS, 2, DIFF_DH), 1, 0)
    k_chunk = jnp.arange(seq) // CHUNK
    scale = DIFF_DH ** -0.5

    def one_block(args):
        q_blk, bi = args
        s = jnp.einsum('bqhcd,bkhcd->bhcqk', q_blk, k).astype(jnp.float32) * scale
        q_chunk = (bi * Q_BLOCK + jnp.arange(Q_BLOCK)) // CHUNK
        allowed = k_chunk[None, :] <= q_chunk[:, None]
        s = jnp.where(allowed, s, -jnp.inf)
        pr = jax.nn.softmax(s, axis=-1)
        a = pr[:, :, 0] - lam * pr[:, :, 1]
        return jnp.einsum('bhqk,bkhv->bqhv', a.astype(v.dtype), v)

    o = lax.map(one_block, (qb, jnp.arange(nqb)))
    o = jnp.moveaxis(o, 0, 1).reshape(bsz, seq, DIFF_HEADS, DIFF_DV)
    o = rmsnorm(o, subln_g) * (1.0 - lam_init)
    return o.reshape(bsz, seq, DIFF_V)

def gla_mixer(q, k, v, r, gz, w_g2, b_g, norm_g):
    bsz, seq = q.shape[0], q.shape[1]
    nc = seq // CHUNK
    dt = v.dtype
    shp = (bsz, nc, CHUNK, GLA_HEADS)
    log_a = jax.nn.log_sigmoid((gz @ w_g2 + b_g).astype(jnp.float32)) / GLA_TAU
    log_a = log_a.reshape(shp + (GLA_DK,))
    qc = q.astype(jnp.float32).reshape(shp + (GLA_DK,)) * (GLA_DK ** -0.5)
    kc = k.astype(jnp.float32).reshape(shp + (GLA_DK,))
    vc = v.astype(jnp.float32).reshape(shp + (GLA_DV,))
    cum = jnp.cumsum(log_a, axis=2)
    tot = cum[:, :, -1]
    kv = jnp.einsum('bnchk,bnchv->nbhkv', kc * jnp.exp(tot[:, :, None] - cum), vc)
    decay = jnp.moveaxis(jnp.exp(tot), 1, 0)

    def step(state, inp):
        d, kv_c = inp
        state = d[..., None] * state + kv_c
        return state, state

    init = jnp.zeros((bsz, GLA_HEADS, GLA_DK, GLA_DV), jnp.float32)
    _, states = lax.scan(step, init, (decay, kv))
    o = jnp.einsum('bnchk,nbhkv->bnchv', qc, states).reshape(bsz, seq, GLA_HEADS, GLA_DV)
    gate = jax.nn.silu(r.astype(jnp.float32)).reshape(bsz, seq, GLA_HEADS, GLA_DV)
    o = rmsnorm(o, norm_g) * gate
    return o.reshape(bsz, seq, GLA_V).astype(dt)

def swiglu(h, w_gu, w_down):
    g, u = jnp.split(h @ w_gu, 2, axis=-1)
    return (jax.nn.silu(g) * u) @ w_down

def moe_swiglu(h, router_w, w_gu, w_down):
    bsz, seq, d = h.shape
    t = bsz * seq
    xf = h.reshape(t, d)
    logits = (xf @ router_w).astype(jnp.float32)
    top_val, top_idx = lax.top_k(logits, TOP_K)
    gates = jax.nn.softmax(top_val, axis=-1)
    flat_e = top_idx.reshape(-1)
    flat_tok = jnp.repeat(jnp.arange(t, dtype=jnp.int32), TOP_K)
    flat_w = gates.reshape(-1)
    order = jnp.argsort(flat_e, stable=True)
    sorted_e = flat_e[order]
    counts = jnp.bincount(flat_e, length=N_EXPERTS)
    padded = ((counts + EXPERT_BLOCK - 1) // EXPERT_BLOCK) * EXPERT_BLOCK
    pend = jnp.cumsum(padded)
    pstart = pend - padded
    ustart = jnp.cumsum(counts) - counts
    n_assign = t * TOP_K
    dest = pstart[sorted_e] + jnp.arange(n_assign) - ustart[sorted_e]
    m_rows = n_assign + N_EXPERTS * EXPERT_BLOCK
    row_tok = jnp.zeros((m_rows,), jnp.int32).at[dest].set(flat_tok[order])
    row_w = jnp.zeros((m_rows,), jnp.float32).at[dest].set(flat_w[order])
    nb = m_rows // EXPERT_BLOCK
    block_e = jnp.minimum(jnp.searchsorted(pend, jnp.arange(nb) * EXPERT_BLOCK, side='right'),
                          N_EXPERTS - 1)
    xs = xf[row_tok].reshape(nb, EXPERT_BLOCK, d)

    def expert_block(args):
        xb, e = args
        return swiglu(xb, w_gu[e], w_down[e])

    ys = lax.map(expert_block, (xs, block_e)).reshape(m_rows, d)
    out = jnp.zeros((t, d), jnp.float32).at[row_tok].add(ys.astype(jnp.float32) * row_w[:, None])
    return out.astype(h.dtype).reshape(bsz, seq, d)

def setup_inputs(seed: int = 0) -> dict:
    key = jax.random.key(seed)
    ks = jax.random.split(key, 24)
    n_dense = (DEPTH + 1) // 2
    n_moe = DEPTH // 2

    def nrm(k, shape, s):
        return jax.random.normal(k, shape, jnp.float32) * s

    return {
        "x": nrm(ks[0], (BATCH, SEQ, D_MODEL), 1.0),
        "p": nrm(ks[1], (DEPTH, BATCH, SEQ, PLE_DIM), 1.0),
        "norm_mix_g": 1.0 + nrm(ks[2], (DEPTH, D_MODEL), 0.02),
        "w_in": nrm(ks[3], (DEPTH, D_MODEL, D_IN), D_MODEL ** -0.5),
        "conv_w": nrm(ks[4], (DEPTH, CONV_WIDTH, CONV_CH), CONV_WIDTH ** -0.5),
        "conv_b": nrm(ks[5], (DEPTH, CONV_CH), 0.02),
        "conv_ln_g": 1.0 + nrm(ks[6], (DEPTH, CONV_CH), 0.02),
        "conv_ln_b": nrm(ks[7], (DEPTH, CONV_CH), 0.02),
        "diff_lambda": nrm(ks[8], (DEPTH, 4, DIFF_DH), 0.1),
        "diff_subln_g": 1.0 + nrm(ks[9], (DEPTH, DIFF_DV), 0.02),
        "gla_w_gate2": nrm(ks[10], (DEPTH, GLA_GATE_RANK, GLA_QK), GLA_GATE_RANK ** -0.5),
        "gla_b_gate": nrm(ks[11], (DEPTH, GLA_QK), 0.1),
        "gla_norm_g": 1.0 + nrm(ks[12], (DEPTH, GLA_DV), 0.02),
        "w_out": nrm(ks[13], (DEPTH, D_MIX, D_MODEL), D_MIX ** -0.5),
        "norm_ffn_g": 1.0 + nrm(ks[14], (DEPTH, D_MODEL), 0.02),
        "ffn_w_gu": nrm(ks[15], (n_dense, D_MODEL, 2 * D_FF), D_MODEL ** -0.5),
        "ffn_w_down": nrm(ks[16], (n_dense, D_FF, D_MODEL), D_FF ** -0.5),
        "router_w": nrm(ks[17], (n_moe, D_MODEL, N_EXPERTS), D_MODEL ** -0.5),
        "moe_w_gu": nrm(ks[18], (n_moe, N_EXPERTS, D_MODEL, 2 * D_FF_EXPERT), D_MODEL ** -0.5),
        "moe_w_down": nrm(ks[19], (n_moe, N_EXPERTS, D_FF_EXPERT, D_MODEL), D_FF_EXPERT ** -0.5),
        "ple_w_up": nrm(ks[20], (DEPTH, PLE_DIM, D_MODEL), PLE_DIM ** -0.5),
        "ple_w_gate": nrm(ks[21], (DEPTH, D_MODEL, D_MODEL), D_MODEL ** -0.5),
        "ple_norm_g": 1.0 + nrm(ks[22], (DEPTH, D_MODEL), 0.02),
        "final_norm_g": 1.0 + nrm(ks[23], (D_MODEL,), 0.02),
    }

def reference(x, p, norm_mix_g, w_in, conv_w, conv_b, conv_ln_g, conv_ln_b, diff_lambda,
              diff_subln_g, gla_w_gate2, gla_b_gate, gla_norm_g, w_out, norm_ffn_g,
              ffn_w_gu, ffn_w_down, router_w, moe_w_gu, moe_w_down, ple_w_up, ple_w_gate,
              ple_norm_g, final_norm_g):
    bsz, seq, _ = x.shape
    pos = jnp.arange(seq, dtype=jnp.float32)
    inv_freq = ROPE_THETA ** (-jnp.arange(0, ROT_DIMS, 2, dtype=jnp.float32) / ROT_DIMS)
    ang = pos[:, None] * inv_freq[None, :]
    cos, sin = jnp.cos(ang), jnp.sin(ang)
    split_at = [int(v) for v in np.cumsum(IN_SPLITS)[:-1]]

    h = x
    for i in range(DEPTH):
        hn = rmsnorm(h, norm_mix_g[i])
        z = hn @ w_in[i]
        (c_a, c_g, d_q, d_k, d_v, g_q, g_k, g_v, g_r, g_z) = jnp.split(z, split_at, axis=-1)

        y_conv = conformer_conv(c_a, c_g, conv_w[i], conv_b[i], conv_ln_g[i], conv_ln_b[i])

        lam_init = 0.8 - 0.6 * math.exp(-0.3 * i)
        lp = diff_lambda[i].astype(jnp.float32)
        lam = jnp.exp(jnp.sum(lp[0] * lp[1])) - jnp.exp(jnp.sum(lp[2] * lp[3])) + lam_init
        dq = rope_partial(d_q.reshape(bsz, seq, DIFF_HEADS, 2, DIFF_DH), cos, sin)
        dk = rope_partial(d_k.reshape(bsz, seq, DIFF_HEADS, 2, DIFF_DH), cos, sin)
        dv = d_v.reshape(bsz, seq, DIFF_HEADS, DIFF_DV)
        y_diff = diff_attention(dq, dk, dv, lam, diff_subln_g[i], lam_init)

        y_gla = gla_mixer(g_q, g_k, g_v, g_r, g_z, gla_w_gate2[i], gla_b_gate[i], gla_norm_g[i])

        h = h + jnp.concatenate([y_conv, y_diff, y_gla], axis=-1) @ w_out[i]

        hn = rmsnorm(h, norm_ffn_g[i])
        if i % 2 == 0:
            h = h + swiglu(hn, ffn_w_gu[i // 2], ffn_w_down[i // 2])
        else:
            h = h + moe_swiglu(hn, router_w[i // 2], moe_w_gu[i // 2], moe_w_down[i // 2])

        gate = jax.nn.sigmoid(rmsnorm(h, ple_norm_g[i]) @ ple_w_gate[i])
        h = h + gate * (p[i] @ ple_w_up[i])

    return rmsnorm(h, final_norm_g)


_drawn_inputs = setup_inputs


def setup_inputs(seed=0):
    import zlib

    import numpy as np

    out = dict(_drawn_inputs(seed))
    spreads = {}
    factors = {'conv_ln_b': 3.114,
     'ple_norm_g': 58.032,
     'final_norm_g': 24.14,
     'conv_ln_g': 2.895,
     'gla_norm_g': 5.317,
     'diff_subln_g': 4.987,
     'norm_ffn_g': 3.624}
    for name, (base, spread) in spreads.items():
        noise = np.random.default_rng([zlib.crc32(name.encode()), seed]).standard_normal(out[name].shape)
        drawn = base * np.exp(spread * noise) if base else spread * noise
        out[name] = __import__('jax').numpy.asarray(drawn.astype(out[name].dtype))
    for name, factor in factors.items():
        out[name] = (out[name] * factor).astype(out[name].dtype)
    return out
```

```python
import math
from contextlib import ExitStack

import numpy as np

import concourse.bass as bass
from concourse import mybir

P = 128
F32 = mybir.dt.float32
F32R = mybir.dt.float32r
I32 = mybir.dt.int32
ALU = mybir.AluOpType
ACT = mybir.ActivationFunctionType
AX = mybir.AxisListType

D = 1024
SEQ = 256
DEPTH = 2
TT = SEQ // P
KC = D // P
CHUNK = 64
CONV_CH = 256
TAPS = 31
HEADS = 4
DH = 64
DV = 128
GLA_HEADS = 4
GLA_DK = 32
GLA_DV = 64
RANK = 16
TAU = 16.0
ROT = 16
D_FF = 2816
N_EXP = 8
D_FE = 3584
PLE = 256
EPS = 1e-6

C_A, C_G, C_DQ, C_DK, C_DV = 0, 256, 512, 1024, 1536
C_GQ, C_GK, C_GV, C_GR, C_GZ = 2048, 2176, 2304, 2560, 2816
D_IN = 2832
IN_BLOCKS = [(c, min(c + 512, D_IN)) for c in range(0, 2560, 512)] + [(2560, D_IN)]

RING = 6
SPLIT = 3
TILE = 2048

V_MIX, V_FFN, V_PLE, V_CB, V_LG, V_LB, V_SUB, V_GLA, V_TAP = 0, 8, 16, 24, 26, 28, 30, 31, 32
V_ROWS = V_TAP + 2 * TAPS

FB = 256
N_FB = D_FF // FB
MB = 512
N_MB = D_FE // MB
T_IN = [0, 54]
T_OUT = [12, 66]
T_FFN = 16
T_UP = [49, 70]
T_GATE = [50, 71]
T_MOE = 71
E_TILES = 6 * N_MB
assert T_FFN + 3 * N_FB == T_UP[0] and E_TILES % RING == 0

K_ID, K_IOTA, K_RANK, K_REV, K_ONES, K_MEAN = (P * i for i in range(6))
K_MASK = 6 * P
K_BD = K_MASK + TT * SEQ
K_COS = K_BD + 256
K_SIN = K_COS + TT * 8
K_HALF = K_SIN + TT * 8
K_TIE = K_HALF + 2
K_END = K_TIE + 64


def constants():
    c = np.zeros((P, K_END), np.float32)
    i = np.arange(P)
    c[:, K_ID:K_ID + P] = np.eye(P)
    c[:, K_IOTA:K_IOTA + P] = i[None, :]
    c[:, K_RANK:K_RANK + P] = i[:, None] < i[None, :]
    c[:, K_REV:K_REV + P] = (i[:, None] > i[None, :]) & (i[:, None] // CHUNK == i[None, :] // CHUNK)
    c[:, K_ONES:K_ONES + P] = 1.0
    c[:, K_MEAN:K_MEAN + P] = 1.0 / CONV_CH
    k = np.arange(SEQ)
    for t in range(TT):
        q = t * P + i
        c[:, K_MASK + t * SEQ:K_MASK + (t + 1) * SEQ] = np.where(
            k[None, :] // CHUNK <= q[:, None] // CHUNK, 0.0, -1e30)
    c[:, K_BD:K_BD + 256] = i[:, None] // GLA_DK == np.arange(256)[None, :] // GLA_DV
    freq = np.float32(500000.0) ** (-np.arange(0, ROT, 2, dtype=np.float32) / np.float32(ROT))
    ang = np.arange(SEQ, dtype=np.float32)[:, None] * freq[None, :].astype(np.float32)
    for t in range(TT):
        c[:, K_COS + 8 * t:K_COS + 8 * t + 8] = np.cos(ang[t * P:(t + 1) * P])
        c[:, K_SIN + 8 * t:K_SIN + 8 * t + 8] = np.sin(ang[t * P:(t + 1) * P])
    c[:, K_HALF] = i < CHUNK
    c[:, K_HALF + 1] = i >= CHUNK
    e = np.arange(N_EXP)
    c[:, K_TIE:K_TIE + 64] = (e[None, :] < e[:, None]).reshape(1, 64)
    return c


def build(nc, x, p, norm_mix_g, w_in, conv_w, conv_b, conv_ln_g, conv_ln_b, diff_lambda, diff_subln_g,
          gla_w_gate2, gla_b_gate, gla_norm_g, w_out, norm_ffn_g, ffn_w_gu, ffn_w_down, router_w,
          moe_w_gu, moe_w_down, ple_w_up, ple_w_gate, ple_norm_g, final_norm_g, consts, out):
    with ExitStack() as ctx:
        def sb(name, shape, dt=F32):
            return ctx.enter_context(nc.sbuf_tensor(name, [P] + shape, dt))

        def sem(name):
            return ctx.enter_context(nc.semaphore(name))

        raw = sb("raw", [RING, TILE])
        w_hi = sb("w_hi", [SPLIT, TILE], F32R)
        w_lo = sb("w_lo", [SPLIT, TILE], F32R)
        cst = sb("cst", [K_END])
        h = sb("h", [TT, D])
        xn = sb("xn", [TT, D])
        x_hi = sb("x_hi", [KC, SEQ], F32R)
        x_lo = sb("x_lo", [KC, SEQ], F32R)
        z = sb("z", [TT, D_IN])
        uT = sb("uT", [2, TAPS - 1 + SEQ])
        yc = sb("yc", [2, SEQ])
        ysq = sb("ysq", [2, SEQ])
        probs = sb("probs", [2 * HEADS, SEQ])
        aT = sb("aT", [TT, HEADS * P])
        vcol = sb("vcol", [DEPTH, V_ROWS])
        lam_mul = sb("lam_mul", [DEPTH, 2, DH])
        lam_exp = sb("lam_exp", [DEPTH, 2])
        neg_lam = sb("neg_lam", [DEPTH])
        w_g2 = sb("w_g2", [DEPTH, P])
        b_gate = sb("b_gate", [DEPTH, P])
        gqT = sb("gqT", [SEQ])
        gzT = sb("gzT", [SEQ])
        decay = sb("decay", [4])
        kx_half = sb("kx_half", [TT, 2, P])
        kv = sb("kv", [2, 256])
        state = sb("state", [4, 256])
        pt = sb("pt", [DEPTH, TT, PLE])
        p_hi = sb("p_hi", [2, SEQ], F32R)
        p_lo = sb("p_lo", [2, SEQ], F32R)
        ff_hi = sb("ff_hi", [512], F32R)
        ff_lo = sb("ff_lo", [512], F32R)
        zeros = sb("zeros", [512], F32R)
        rw = sb("rw", [KC, N_EXP])
        rw_hi = sb("rw_hi", [KC, N_EXP], F32R)
        rw_lo = sb("rw_lo", [KC, N_EXP], F32R)
        small = sb("small", [64])
        eps_t = sb("eps_t", [1])
        logit = sb("logit", [TT, N_EXP])
        chosen = sb("chosen", [TT, N_EXP])
        e_gate = sb("e_gate", [TT, 1 + 2 * N_EXP])
        slot_of = sb("slot_of", [TT, 1 + 2 * N_EXP])
        passes_t = sb("passes_t", [1], I32)
        pickT = sb("pickT", [SEQ], F32R)
        vrows = kx_half[:, :, :, :].rearrange("p t a n -> p (t a) n")[:, 0:DEPTH, :]
        lam_row = kv[:, :, :].rearrange("p l (a n) -> p l a n", a=4)
        qT = xn[:, 0, :].rearrange("p (j n) -> p j n", j=HEADS)
        kT = xn[:, 1, :].rearrange("p (j n) -> p j n", j=HEADS)
        on, osq = z[:, 0, C_DQ:C_DK], z[:, 1, C_DQ:C_DK]
        log_a, g_exp = (z[:, 0, i:i + 256].rearrange("p (t n) -> p t n", t=TT) for i in (0, 256))
        g_pre, g_abs = (z[:, 1, i:i + 256].rearrange("p (t n) -> p t n", t=TT) for i in (0, 256))
        silu_g, ff = z[:, 0, 0:512], z[:, 1, 0:512]
        g_row = z[:, 0, 512:512 + D]
        pick = z[:, 1, 512:768].rearrange("p (t n) -> p t n", t=TT)
        cmp_a, cmp_b = (z[:, 1, i:i + 128].rearrange("p (t n) -> p t n", t=TT) for i in (768, 896))
        up = probs[:, :, :].rearrange("p (t a) n -> p t (a n)", t=TT)
        gate = aT
        rot = state[:, :, :].rearrange("p i (t g n) -> p i t g n", t=TT, g=16)
        xe_hi, xe_lo = (a[:, 0:4, :].rearrange("p k (m n) -> p (k m) n", m=2) for a in (x_hi, x_lo))
        y_hi, y_lo = (a[:, 4:8, :].rearrange("p k n -> p (k n)") for a in (x_hi, x_lo))
        ps = ctx.enter_context(nc.psum_tensor("ps", [P, 8, 512], F32))

        ident = cst[:, K_ID:K_ID + P]
        sumsq, std, rstd = small[:, 0:2], small[:, 2:4], small[:, 4:6]
        neg_max, row_sum, row_inv = small[:, 8:16], small[:, 16:24], small[:, 24:32]
        o_ss, o_std, o_inv = small[:, 32:36], small[:, 36:40], small[:, 40:44]
        g_ss, g_std, g_inv = small[:, 44:52], small[:, 52:60], small[:, 8:16]
        top, gsum, count_max = small[:, 60:62], small[:, 62:64], small[:, 6:7]

        raw_landed = [sem(f"raw_landed{i}") for i in range(RING)]
        up_landed = [sem(f"up_landed{i}") for i in range(RING)]
        hi_ready, lo_ready, tile_used = sem("hi_ready"), sem("lo_ready"), sem("tile_used")
        x_landed, cst_landed, vec_landed = sem("x_landed"), sem("cst_landed"), sem("vec_landed")
        misc_landed, grow_landed, frow_landed = sem("misc_landed"), sem("grow_landed"), sem("frow_landed")
        dve_step, act_step = sem("dve_step"), sem("act_step")
        vecT_ready, vec_ready, setup_done = sem("vecT_ready"), sem("vec_ready"), sem("setup_done")
        sumsq_ready, std_ready, xn_ready = sem("sumsq_ready"), sem("std_ready"), sem("xn_ready")
        xnT_ready, xhi_ready, xlo_ready = sem("xnT_ready"), sem("xhi_ready"), sem("xlo_ready")
        h_updated = sem("h_updated")
        z_ready, u_ready, uT_ready, uT_copied = sem("z_ready"), sem("u_ready"), sem("uT_ready"), sem("uT_copied")
        tap_done, rope_done = sem("tap_done"), sem("rope_done")
        qkT_ready, qT_copied, kT_copied = sem("qkT_ready"), sem("qT_copied"), sem("kT_copied")
        mean_ready, yc_ready, ysq_ready, var_ready = sem("mean_ready"), sem("yc_ready"), sem("ysq_ready"), sem("var_ready")
        ystd_ready, yn_ready, y_ready = sem("ystd_ready"), sem("yn_ready"), sem("y_ready")
        scores_ready, neg_max_ready, exp_ready = sem("scores_ready"), sem("neg_max_ready"), sem("exp_ready")
        masked_ready, a_ready, aT_ready, aT_copied = sem("masked_ready"), sem("a_ready"), sem("aT_ready"), sem("aT_copied")
        o_ready, osq_ready, oss_ready, ostd_ready = sem("o_ready"), sem("osq_ready"), sem("oss_ready"), sem("ostd_ready")
        on_ready, onT_ready = sem("on_ready"), sem("onT_ready")
        gT_ready, gT_copied, gpre_ready, gbias_ready = sem("gT_ready"), sem("gT_copied"), sem("gpre_ready"), sem("gbias_ready")
        gln_ready, la_ready, rev_ready, gexp_ready = sem("gln_ready"), sem("la_ready"), sem("rev_ready"), sem("gexp_ready")
        kx_ready, kv_ready, kv_masked, state_ready = sem("kx_ready"), sem("kv_ready"), sem("kv_masked"), sem("state_ready")
        go_ready, gsq_ready, gss_ready, gstd_ready = sem("go_ready"), sem("gsq_ready"), sem("gss_ready"), sem("gstd_ready")
        gon_ready, gonT_ready = sem("gon_ready"), sem("gonT_ready")
        mixhi_ready, mixlo_ready = sem("mixhi_ready"), sem("mixlo_ready")
        pT_ready, phi_ready, plo_ready, up_ready, gate_ready = (
            sem("pT_ready"), sem("phi_ready"), sem("plo_ready"), sem("up_ready"), sem("gate_ready"))
        f_silu, f_act, f_T, f_hi, f_lo = sem("f_silu"), sem("f_act"), sem("f_T"), sem("f_hi"), sem("f_lo")
        logit_ready, rank_ready, lexp_ready, chosen_ready = sem("logit_ready"), sem("rank_ready"), sem("lexp_ready"), sem("chosen_ready")
        passes_ready, xg_ready, rw_hi_ready, rw_lo_ready = (
            sem("passes_ready"), sem("xg_ready"), sem("rw_hi_ready"), sem("rw_lo_ready"))
        m_pick, m_gathered, m_xhi, m_xlo = sem("m_pick"), sem("m_gathered"), sem("m_xhi"), sem("m_xlo")
        m_pickT, m_pickT_copied = sem("m_pickT"), sem("m_pickT_copied")
        m_silu, m_act, m_T, m_hi, m_lo = sem("m_silu"), sem("m_act"), sem("m_T"), sem("m_hi"), sem("m_lo")
        m_yhi, m_ylo, m_scattered, m_added = sem("m_yhi"), sem("m_ylo"), sem("m_scattered"), sem("m_added")
        out_landed, out_ready = sem("out_landed"), sem("out_ready")

        def nth(c, r):
            return c + 1 if r is None else r * RING + (c + 1)

        def load_tile(sp, c, r, dst_of, src):
            if c >= RING or r is not None:
                sp.wait_ge(lo_ready, nth(c - RING, r))
            sp.dma_start(dst_of(raw[:, c % RING, :]), src).then_inc(raw_landed[c % RING], 16)

        def split_hi(act, c, r=None):
            f = c - T_FFN
            if 0 <= f < 3 * N_FB - 1 and (f < 2 or (f - 2) % 3 != 2):
                if r is None:
                    act.wait_ge(up_landed[c % RING], 16 * (f // RING + 1))
                else:
                    act.wait_ge(up_landed[c % RING], r * 16 + 16 * (f // RING + 1))
            if r is None:
                act.wait_ge(raw_landed[c % RING], 16 * (c // RING + 1))
            else:
                act.wait_ge(raw_landed[c % RING], r * 16 + 16 * (c // RING + 1))
            if c >= SPLIT or r is not None:
                act.wait_ge(tile_used, nth(c - SPLIT, r))
            w = tile_width(c)
            nc.scalar.activation(w_hi[:, c % SPLIT, 0:w], raw[:, c % RING, 0:w], ACT.Copy).then_inc(hi_ready, 1)

        def split_lo(dve, c, r=None):
            dve.wait_ge(hi_ready, nth(c, r))
            w = tile_width(c)
            nc.vector.tensor_tensor(w_lo[:, c % SPLIT, 0:w], raw[:, c % RING, 0:w],
                                    w_hi[:, c % SPLIT, 0:w].bitcast(F32), ALU.subtract).then_inc(lo_ready, 1)

        def tile_width(c):
            last = any(c in (t + 10, t + 11) for t in T_IN)
            return 4 * (IN_BLOCKS[-1][1] - IN_BLOCKS[-1][0]) if last else TILE

        def products(acc, xh, xl, wh, wl, start, stop):
            nc.tensor.matmul(acc, xh, wh, start=start, stop=False)
            nc.tensor.matmul(acc, xh, wl, start=False, stop=False)
            return nc.tensor.matmul(acc, xl, wh, start=False, stop=stop)

        H_BEFORE = {1: 2, 2: 3, 3: 5, 4: 7, 6: 9}
        MIX_PARTS = 6
        Z_DONE = [2, 3, 4, 5, 6, 8]
        halves = lambda t: t.rearrange("p (k n) -> p k n", k=4)
        doubles = lambda t: t.rearrange("p (k n) -> p k n", k=2)
        block = ctx.enter_context(nc.Block())

        @block.sync
        def _(sp):
            def rows(c, r, w, cols):
                n = cols[1] - cols[0]
                load_tile(sp, c, r, lambda t: t[:, 0:4 * n].rearrange("p (k n) -> p k n", k=4),
                          w[:, :, cols[0]:cols[1]])

            def in_proj(l):
                w = w_in[l].rearrange("(k p) n -> p k n", p=P)
                for b, cols in enumerate(IN_BLOCKS):
                    for half in range(2):
                        rows(T_IN[l] + 2 * b + half, None, w[:, 4 * half:4 * half + 4, :], cols)

            def square(first, r, w):
                w = w.rearrange("(k p) n -> p k n", p=P)
                for b in range(2):
                    for half in range(2):
                        rows(first + 2 * b + half, r, w[:, 4 * half:4 * half + 4, :], (512 * b, 512 * b + 512))

            def up_proj(l):
                load_tile(sp, T_UP[l], None, doubles, ple_w_up[l].rearrange("(k p) n -> p k n", p=P))

            f_gu = ffn_w_gu[0].rearrange("(k p) (s n) -> p k s n", p=P, s=2)
            f_down = ffn_w_down[0].rearrange("(k p) n -> p k n", p=P)

            def ffn_gu(c, r, b):
                for half in range(2):
                    load_tile(sp, c + half, r, lambda t: t.rearrange("p (k s n) -> p k s n", k=4, s=2)[:, :, 0, :],
                              f_gu[:, 4 * half:4 * half + 4, 0, bass.ds(b * FB, FB)])
                    dst = raw[:, (c + half) % RING, :].rearrange("p (k s n) -> p k s n", k=4, s=2)[:, :, 1, :]
                    sp.dma_start(dst, f_gu[:, 4 * half:4 * half + 4, 1, bass.ds(b * FB, FB)]
                                 ).then_inc(up_landed[(c + half) % RING], 16)

            def ffn_down(c, r, b):
                load_tile(sp, c, r, doubles, f_down[:, bass.ds(b * 2, 2), :])

            in_proj(0)
            square(T_OUT[0], None, w_out[0])
            ffn_gu(T_FFN, None, 0)
            with sp.Fori(0, (N_FB - 1) // 2) as i:
                for s in range(2):
                    ffn_gu(T_FFN + 2 + 3 * s, i, i * 2 + (1 + s))
                    ffn_down(T_FFN + 4 + 3 * s, i, i * 2 + s)
            c = T_UP[0] - 1
            load_tile(sp, c, None, lambda t: doubles(t)[:, 0, :], f_down[:, 2 * N_FB - 2, :])
            sp.dma_start(doubles(raw[:, c % RING, :])[:, 1, :], f_down[:, 2 * N_FB - 1, :]).then_inc(up_landed[c % RING], 16)
            up_proj(0)
            square(T_GATE[0], None, ple_w_gate[0])
            in_proj(1)
            square(T_OUT[1], None, w_out[1])
            up_proj(1)

            e_gu = moe_w_gu[0].rearrange("e (k p) n -> e p k n", p=P)
            e_down = moe_w_down[0].rearrange("e (k p) n -> e p k n", p=P)

            def expert_gu(c, r, e, b):
                for s in range(2):
                    for half in range(2):
                        load_tile(sp, c + 2 * s + half, r, halves,
                                  e_gu[bass.ds(e, 1), :, 4 * half:4 * half + 4, bass.ds(b * MB + s * D_FE, MB)]
                                  .rearrange("e p k n -> p (e k) n"))

            def expert_down(c, r, e, b):
                for half in range(2):
                    load_tile(sp, c + half, r, doubles,
                              e_down[bass.ds(e, 1), :, bass.ds(b * 4 + 2 * half, 2), :]
                              .rearrange("e p k n -> p (e k) n"))

            def experts(first):
                with sp.Fori(0, N_EXP) as e:
                    r0 = e * N_MB + first * N_MB
                    expert_gu(T_MOE, r0, e, 0)
                    with sp.Fori(1, N_MB) as b:
                        r = r0 + b - 1
                        expert_gu(T_MOE + 4, r, e, b)
                        expert_down(T_MOE + 8, r, e, b - 1)
                    expert_down(T_MOE + 4, r0 + (N_MB - 1), e, N_MB - 1)

            experts(0)
            sp.wait_ge(passes_ready, 1)
            passes = sp.value_load(passes_t[0:1, 0:1], min_val=1, max_val=2)
            with sp.If(passes > 1):
                experts(N_EXP)
            square(T_GATE[1], passes * (N_EXP * N_MB), ple_w_gate[1])

            sp.wait_ge(out_ready, 1)
            sp.dma_start(out[0].rearrange("(t p) n -> p t n", p=P), xn[:, :, :]).then_inc(out_landed, 16)
            sp.wait_ge(out_landed, 16)

        N_VEC_DMAS = 10

        @block.gpsimd
        def _(pool):
            pool.dma_start(cst[:, :], consts).then_inc(cst_landed, 16)
            for l in range(DEPTH):
                for first, src in ((V_MIX, norm_mix_g), (V_FFN, norm_ffn_g), (V_PLE, ple_norm_g), (V_CB, conv_b),
                                   (V_LG, conv_ln_g), (V_LB, conv_ln_b), (V_SUB, diff_subln_g)):
                    n = src.shape[1] // P
                    pool.dma_start(vrows[first:first + n, l, :],
                                   src[l].rearrange("(r n) -> r n", n=P)).then_inc(vec_landed, 16)
                for half in range(2):
                    pool.dma_start(vrows[V_GLA:V_GLA + 1, l, half * GLA_DV:(half + 1) * GLA_DV],
                                   gla_norm_g[l:l + 1, :]).then_inc(vec_landed, 16)
                pool.dma_start(vrows[V_TAP:V_TAP + 2 * TAPS, l, :],
                               conv_w[l].rearrange("a (r n) -> (a r) n", n=P)).then_inc(vec_landed, 16)
            for l in range(DEPTH):
                pool.dma_start(lam_row[:, l, :, :].rearrange("p a n -> p (a n)"),
                               diff_lambda[l:l + 1].rearrange("o a n -> o (a n)").broadcast_to([P, 4 * DH])
                               ).then_inc(misc_landed, 16)
                pool.dma_start(w_g2[0:RANK, l, :], gla_w_gate2[l]).then_inc(misc_landed, 16)
                pool.dma_start(b_gate[:, l, :], gla_b_gate[l:l + 1, :].broadcast_to([P, P])).then_inc(misc_landed, 16)
                pool.dma_start(pt[:, l, :, :], p[l, 0].rearrange("(t p) n -> p t n", p=P)).then_inc(misc_landed, 16)
            pool.dma_start(rw[:, :, :], router_w[0].rearrange("(k p) n -> p k n", p=P)).then_inc(misc_landed, 16)
            pool.wait_ge(mixlo_ready, 4 * DEPTH)
            pool.dma_start(g_row[:, :], norm_ffn_g[1:2, :].broadcast_to([P, D])).then_inc(grow_landed, 16)
            pool.wait_ge(xg_ready, 2)
            pool.dma_start(g_row[:, :], final_norm_g.rearrange("(a n) -> a n", a=1).broadcast_to([P, D])
                           ).then_inc(frow_landed, 16)

        N_MISC = 4 * DEPTH + 1

        @block.scalar
        def _(act):
            steps = [0]

            def link(ins):
                steps[0] += 1
                ins.then_inc(act_step, 1)
                act.wait_ge(act_step, steps[0])

            nc.scalar.dma_start(h[:, :, :], x[0].rearrange("(t p) n -> p t n", p=P)).then_inc(x_landed, 16)

            def norm_start(q):
                if q in H_BEFORE:
                    act.wait_ge(h_updated, H_BEFORE[q])
                for t in range(TT):
                    nc.scalar.activation(xn[:, t, :], h[:, t, :], ACT.Square,
                                         accum_out=sumsq[:, t:t + 1]).then_inc(sumsq_ready, 1)
                act.wait_ge(sumsq_ready, 2 * q + 2)
                nc.scalar.activation(std, sumsq, ACT.Sqrt, bias=eps_t[:, 0:1], scale=1.0 / D).then_inc(std_ready, 1)

            def norm_split(q, l, first):
                for k in range(KC):
                    act.wait_ge(xnT_ready, 4 * q + k // 2 + 1)
                    nc.scalar.activation(x_hi[:, k, :], ps[:, 4 + k // 2, (k % 2) * SEQ:(k % 2 + 1) * SEQ], ACT.Copy,
                                         scale=vcol[:, l, first + k:first + k + 1]).then_inc(xhi_ready, 1)

            def in_proj(l):
                for b, (c0, c1) in enumerate(IN_BLOCKS):
                    c = T_IN[l] + 2 * b
                    split_hi(act, c + 3)
                    act.wait_ge(tile_used, c + 2)
                    s = 2 * (b % 2)
                    if b == 0:
                        nc.scalar.activation(z[:, :, 0:C_G], ps[:, s:s + 2, 0:C_G], ACT.Copy).then_inc(z_ready, 1)
                        nc.scalar.activation(z[:, :, C_G:c1], ps[:, s:s + 2, C_G:c1], ACT.Sigmoid).then_inc(z_ready, 1)
                    elif c0 == C_GR:
                        nc.scalar.activation(z[:, :, c0:C_GZ], ps[:, s:s + 2, 0:C_GZ - c0], ACT.Silu).then_inc(z_ready, 1)
                        nc.scalar.activation(z[:, :, C_GZ:c1], ps[:, s:s + 2, C_GZ - c0:c1 - c0], ACT.Copy).then_inc(z_ready, 1)
                    else:
                        nc.scalar.activation(z[:, :, c0:c1], ps[:, s:s + 2, :], ACT.Copy).then_inc(z_ready, 1)
                    split_hi(act, c + 4)
                    if b == 2:
                        act.wait_ge(uT_ready, l + 1)
                        nc.scalar.activation(uT[:, :, TAPS - 1:], ps[:, 4, :].rearrange("p (j n) -> p j n", j=2),
                                             ACT.Copy).then_inc(uT_copied, 1)

            def exps(l, t):
                act.wait_ge(neg_max_ready, TT * l + t + 1)
                for i in range(2 * HEADS):
                    nc.scalar.activation(probs[:, i, 0:P * (t + 1)], probs[:, i, 0:P * (t + 1)], ACT.Exp,
                                         bias=neg_max[:, i:i + 1], accum_out=row_sum[:, i:i + 1]).then_inc(exp_ready, 1)

            def probs_T(l, t):
                for kt in range(t + 1):
                    act.wait_ge(aT_ready, TT * l + t + 1)
                    nc.scalar.activation(aT[:, kt, :], ps[:, 4 + kt, :], ACT.Copy).then_inc(aT_copied, 1)

            def o_square(l, t):
                act.wait_ge(o_ready, TT * l + t + 1)
                nc.scalar.activation(osq[:, :], ps[:, 6, :], ACT.Square).then_inc(osq_ready, 1)

            def o_std_(l, t):
                act.wait_ge(oss_ready, TT * l + t + 1)
                nc.scalar.activation(o_std, o_ss, ACT.Sqrt, bias=eps_t[:, 0:1], scale=1.0 / DV).then_inc(ostd_ready, 1)

            def o_split(l, t):
                act.wait_ge(onT_ready, TT * l + t + 1)
                nc.scalar.activation(x_hi[:, 2:6, t * P:(t + 1) * P], ps[:, 4, :].rearrange("p (j n) -> p j n", j=4),
                                     ACT.Copy, scale=vcol[:, l, V_SUB:V_SUB + 1]).then_inc(mixhi_ready, 1)

            def mixer(l):
                for t in range(TT):
                    act.wait_ge(qkT_ready, 4 * l + t + 1)
                    nc.scalar.activation(qT[:, :, t * P:(t + 1) * P], ps[:, 4 + t, :].rearrange("p (j n) -> p j n", j=4),
                                         ACT.Copy).then_inc(qT_copied, 1)
                act.wait_ge(yc_ready, l + 1)
                nc.scalar.activation(ysq[:, :, :], yc[:, :, :], ACT.Square).then_inc(ysq_ready, 1)
                act.wait_ge(var_ready, l + 1)
                nc.scalar.activation(ysq[:, 0, :], ps[:, 7, SEQ:2 * SEQ], ACT.Sqrt, bias=eps_t[:, 0:1]).then_inc(ystd_ready, 1)
                act.wait_ge(gT_ready, l + 1)
                nc.scalar.activation(gqT[:, :], ps[:, 7, 0:SEQ], ACT.Copy, scale=GLA_DK ** -0.5).then_inc(gT_copied, 1)
                nc.scalar.activation(gzT[0:RANK, :], ps[0:RANK, 7, SEQ:2 * SEQ], ACT.Copy).then_inc(gT_copied, 1)
                exps(l, 0)
                act.wait_ge(yn_ready, l + 1)
                for j in range(2):
                    nc.scalar.activation(yc[:, j, :], yc[:, j, :], ACT.Silu, bias=vcol[:, l, V_LB + j:V_LB + j + 1],
                                         scale=vcol[:, l, V_LG + j:V_LG + j + 1]).then_inc(y_ready, 1)
                act.wait_ge(y_ready, 2 * l + 2)
                nc.scalar.activation(x_hi[:, 0:2, :], yc[:, :, :], ACT.Copy).then_inc(mixhi_ready, 1)
                act.wait_ge(gbias_ready, l + 1)
                link(nc.scalar.activation(g_abs[:, :, :], g_pre[:, :, :], ACT.Abs))
                link(nc.scalar.activation(g_abs[:, :, :], g_abs[:, :, :], ACT.Exp, scale=-1.0))
                nc.scalar.activation(g_abs[:, :, :], g_abs[:, :, :], ACT.Ln, bias=1.0).then_inc(gln_ready, 1)
                probs_T(l, 0)
                act.wait_ge(rev_ready, l + 1)
                nc.scalar.activation(g_exp[:, :, :], ps[:, 7, 0:SEQ].rearrange("p (t n) -> p t n", t=2), ACT.Exp,
                                     scale=1.0 / TAU).then_inc(gexp_ready, 1)
                nc.scalar.activation(decay[:, :], ps[:, 7, SEQ:SEQ + 4], ACT.Exp, scale=1.0 / TAU).then_inc(gexp_ready, 1)
                exps(l, 1)
                o_square(l, 0)
                o_std_(l, 0)
                o_split(l, 0)
                probs_T(l, 1)
                act.wait_ge(go_ready, l + 1)
                nc.scalar.activation(osq[:, :], ps[:, 7, :], ACT.Square).then_inc(gsq_ready, 1)
                act.wait_ge(gss_ready, l + 1)
                nc.scalar.activation(g_std, g_ss, ACT.Sqrt, bias=eps_t[:, 0:1], scale=1.0 / GLA_DV).then_inc(gstd_ready, 1)
                o_square(l, 1)
                o_std_(l, 1)
                act.wait_ge(gonT_ready, l + 1)
                nc.scalar.activation(x_hi[:, 6:8, :], ps[:, 7, :].rearrange("p (j n) -> p j n", j=2), ACT.Copy,
                                     scale=vcol[:, l, V_GLA:V_GLA + 1]).then_inc(mixhi_ready, 1)
                o_split(l, 1)
                act.wait_ge(pT_ready, l + 1)
                nc.scalar.activation(p_hi[:, :, :], ps[:, 5, :].rearrange("p (j n) -> p j n", j=2), ACT.Copy).then_inc(phi_ready, 1)

            def up_copy(l):
                act.wait_ge(tile_used, T_UP[l] + 1)
                nc.scalar.activation(up[:, :, :], ps[:, 0:4, :].rearrange("p (t m) n -> p t (m n)", t=2),
                                     ACT.Copy).then_inc(up_ready, 1)

            def ple_gate(l, r):
                for b in range(2):
                    c = T_GATE[l] + 2 * b
                    if l == 0:
                        split_hi(act, c + 3)
                    elif b == 0:
                        split_hi(act, c + 3, r)
                    act.wait_ge(tile_used, nth(c + 1, r))
                    if b == 1:
                        act.wait_ge(h_updated, 5 * l + 4 - l)
                    nc.scalar.activation(gate[:, :, :], ps[:, 2 * b:2 * b + 2, :], ACT.Sigmoid).then_inc(gate_ready, 1)
                    if l == 0:
                        split_hi(act, c + 4)

            act.wait_ge(setup_done, 1)
            act.wait_ge(x_landed, 16)
            norm_start(0)
            act.wait_ge(vecT_ready, 1)
            nc.scalar.activation(vcol[:, :, :], ps[:, 0:2, 0:V_ROWS], ACT.Copy).then_inc(vec_ready, 1)
            act.wait_ge(vec_ready, 1)
            for c in range(3):
                split_hi(act, c)
            for l in range(DEPTH):
                if l:
                    norm_start(3)
                norm_split(3 * l, l, V_MIX)
                in_proj(l)
                if l == 0:
                    act.wait_ge(setup_done, 3)
                    nc.scalar.activation(lam_exp[:, :, :], lam_exp[:, :, :], ACT.Exp).then_inc(vec_ready, 1)
                mixer(l)
                for c in range(T_OUT[l], T_OUT[l] + 4):
                    split_hi(act, c + 3)
                if l == 0:
                    norm_start(1)
                    norm_split(1, 0, V_FFN)

                    def ffn_gate():
                        nc.scalar.activation(silu_g[:, :].rearrange("p (t n) -> p t n", t=2), ps[:, 0:2, 0:FB],
                                             ACT.Silu).then_inc(f_silu, 1)

                    def ffn_T(b):
                        act.wait_ge(f_T, b + 1)
                        nc.scalar.activation(ff_hi[:, :], ps[:, 2, :], ACT.Copy).then_inc(f_hi, 1)

                    act.wait_ge(tile_used, T_FFN + 2)
                    ffn_gate()
                    with act.Fori(0, (N_FB - 1) // 2) as i:
                        for s in range(2):
                            c = T_FFN + 2 + 3 * s
                            split_hi(act, c + 1, i)
                            split_hi(act, c + 2, i)
                            ffn_T(i * 2 + s)
                            split_hi(act, c + 3, i)
                            act.wait_ge(tile_used, nth(c + 1, i))
                            ffn_gate()
                    split_hi(act, T_UP[0])
                    split_hi(act, T_UP[0] + 1)
                    ffn_T(N_FB - 1)
                    split_hi(act, T_UP[0] + 2)
                    norm_start(2)
                    split_hi(act, T_UP[0] + 3)
                    up_copy(0)
                    norm_split(2, 0, V_PLE)
                    ple_gate(0, None)

            up_copy(1)
            split_hi(act, T_UP[1] + 3)
            norm_start(4)
            norm_split(4, 1, V_FFN)
            nc.scalar.activation(rw_hi[:, :, :], rw[:, :, :], ACT.Copy).then_inc(rw_hi_ready, 1)
            act.wait_ge(chosen_ready, 1)
            nc.scalar.activation(e_gate[:, :, 1:1 + N_EXP], e_gate[:, :, 1:1 + N_EXP], ACT.Exp).then_inc(lexp_ready, 1)
            act.wait_ge(passes_ready, 1)
            passes = act.value_load(passes_t[0:1, 0:1], min_val=1, max_val=2)

            def expert_rows_hi(n):
                for half in range(2):
                    act.wait_ge(m_gathered, n * 2 + (half + 1))
                    nc.scalar.activation(xe_hi[:, 4 * half:4 * half + 4, :],
                                         ps[:, 6 + half, :].rearrange("p (k n) -> p k n", k=4), ACT.Copy).then_inc(m_xhi, 1)

            def expert_out_hi(r):
                act.wait_ge(tile_used, nth(T_MOE - 1, r))
                for half in range(2):
                    nc.scalar.activation(y_hi[:, 512 * half:512 * half + 512], ps[:, 4 + half, :],
                                         ACT.Copy).then_inc(m_yhi, 1)

            expert_rows_hi(0)
            with act.Fori(0, passes) as ps_i:
                with act.Fori(0, N_EXP) as e:
                    n = ps_i * N_EXP + e
                    r0 = n * N_MB

                    def gate_of(c, r):
                        act.wait_ge(tile_used, nth(c, r))
                        nc.scalar.activation(silu_g[:, :], ps[:, 0, :], ACT.Silu).then_inc(m_silu, 1)

                    def upper_T(m):
                        act.wait_ge(m_T, m)
                        nc.scalar.activation(ff_hi[:, :], ps[:, 2, :], ACT.Copy).then_inc(m_hi, 1)

                    expert_out_hi(r0)
                    split_hi(act, T_MOE + 3, r0)
                    gate_of(T_MOE + 1, r0)
                    split_hi(act, T_MOE + 4, r0)
                    split_hi(act, T_MOE + 5, r0)
                    with act.Fori(1, N_MB) as b:
                        r = r0 + b - 1
                        split_hi(act, T_MOE + 6, r)
                        upper_T(r0 + b)
                        split_hi(act, T_MOE + 7, r)
                        gate_of(T_MOE + 5, r)
                        for c in range(8, 12):
                            split_hi(act, T_MOE + c, r)
                    r1 = r0 + N_MB
                    upper_T(r1)
                    split_hi(act, T_MOE + 0, r1)
                    expert_rows_hi(n + 1)
                    act.wait_ge(m_pickT, n + 1)
                    nc.scalar.activation(pickT[:, :], ps[:, 3, 0:SEQ], ACT.Copy).then_inc(m_pickT_copied, 1)
                    split_hi(act, T_MOE + 1, r1)
                    split_hi(act, T_MOE + 2, r1)
            expert_out_hi(passes * (N_EXP * N_MB))
            act.wait_ge(m_added, passes * (2 * N_EXP) + 2)
            norm_start(5)
            norm_split(5, 1, V_PLE)
            ple_gate(1, passes * (N_EXP * N_MB))
            norm_start(6)

        @block.vector
        def _(dve):
            steps = [0]

            def link(ins):
                steps[0] += 1
                ins.then_inc(dve_step, 1)
                dve.wait_ge(dve_step, steps[0])

            def norm_scale(q):
                dve.wait_ge(std_ready, q + 1)
                link(nc.vector.reciprocal(rstd, std))
                for t in range(TT):
                    nc.vector.tensor_scalar(xn[:, t, :], h[:, t, :], rstd[:, t:t + 1], None, ALU.mult).then_inc(xn_ready, 1)

            def norm_split(q, l, first):
                for k in range(KC):
                    dve.wait_ge(xhi_ready, 8 * q + 2 * (k // 2) + 2)
                    nc.vector.scalar_tensor_tensor(
                        out=x_lo[:, k, :], in0=ps[:, 4 + k // 2, (k % 2) * SEQ:(k % 2 + 1) * SEQ],
                        scalar=vcol[:, l, first + k:first + k + 1], in1=x_hi[:, k, :].bitcast(F32),
                        op0=ALU.mult, op1=ALU.subtract).then_inc(xlo_ready, 1)

            def taps(l, first, last):
                for n in range(first, min(last, 2 * TAPS)):
                    tap, j = n // 2, n % 2
                    w = vcol[:, l, V_TAP + n:V_TAP + n + 1]
                    src = uT[:, j, tap:tap + SEQ]
                    if tap == 0:
                        ins = nc.vector.tensor_scalar(yc[:, j, :], src, w, vcol[:, l, V_CB + j:V_CB + j + 1],
                                                      ALU.mult, ALU.add)
                    else:
                        dve.wait_ge(tap_done, 2 * TAPS * l + n - 1)
                        ins = nc.vector.scalar_tensor_tensor(out=yc[:, j, :], in0=src, scalar=w, in1=yc[:, j, :],
                                                             op0=ALU.mult, op1=ALU.add)
                    ins.then_inc(tap_done, 1)

            def rope(l):
                dve.wait_ge(z_ready, 8 * l + Z_DONE[2])
                qk = z[:, :, C_DQ:C_DV].rearrange("p t (g d) -> p t g d", d=DH)
                x1, x2 = qk[:, :, :, 0:8], qk[:, :, :, 8:16]
                cos = cst[:, K_COS:K_COS + 16].rearrange("p (t o n) -> p t o n", t=2, o=1).broadcast_to([P, TT, 16, 8])
                sin = cst[:, K_SIN:K_SIN + 16].rearrange("p (t o n) -> p t o n", t=2, o=1).broadcast_to([P, TT, 16, 8])
                for i, (a, b) in enumerate(((x1, cos), (x2, sin), (x2, cos), (x1, sin))):
                    for t in range(TT):
                        ins = nc.vector.tensor_tensor(rot[:, i, t], a[:, t], b[:, t], ALU.mult)
                        if i == 3 and t == 1:
                            link(ins)
                        else:
                            link(ins)
                for t in range(TT):
                    nc.vector.tensor_tensor(x1[:, t], rot[:, 0, t], rot[:, 1, t], ALU.subtract).then_inc(rope_done, 1)
                    nc.vector.tensor_tensor(x2[:, t], rot[:, 2, t], rot[:, 3, t], ALU.add).then_inc(rope_done, 1)

            def in_proj(l):
                n = 0
                for b in range(len(IN_BLOCKS)):
                    c = T_IN[l] + 2 * b
                    split_lo(dve, c + 3)
                    if b >= 3:
                        taps(l, n, n + 10)
                        n += 10
                    if b == 1:
                        dve.wait_ge(z_ready, 8 * l + Z_DONE[0])
                        nc.vector.tensor_tensor(z[:, :, 0:C_G], z[:, :, 0:C_G], z[:, :, C_G:2 * C_G],
                                                ALU.mult).then_inc(u_ready, 1)
                    split_lo(dve, c + 4)
                    if b == 3:
                        rope(l)
                    if b == 2:
                        dve.wait_ge(uT_copied, l + 1)
                    if b >= 2:
                        taps(l, n, n + 10)
                        n += 10
                taps(l, n, 2 * TAPS)

            def mask_scores(l, t):
                dve.wait_ge(scores_ready, TT * l + t + 1)
                n = P * (t + 1)
                mask = cst[:, K_MASK + t * SEQ:K_MASK + t * SEQ + n].rearrange("p (o n) -> p o n", o=1).broadcast_to([P, HEADS, n])
                for c in range(2):
                    s = ps[:, 2 * c:2 * c + 2, :].rearrange("p b (i n) -> p (b i) n", i=2)[:, :, 0:n]
                    nc.vector.scalar_tensor_tensor(out=probs[:, HEADS * c:HEADS * c + HEADS, 0:n], in0=s,
                                                   scalar=DH ** -0.5, in1=mask, op0=ALU.mult,
                                                   op1=ALU.add).then_inc(masked_ready, 1)
                dve.wait_ge(masked_ready, 2 * TT * l + 2 * t + 2)
                nc.vector.tensor_reduce(neg_max, probs[:, :, 0:n], AX.X, ALU.max, negate=True).then_inc(neg_max_ready, 1)

            def differences(l, t):
                n = P * (t + 1)
                dve.wait_ge(exp_ready, 2 * HEADS * (TT * l + t + 1))
                link(nc.vector.reciprocal(row_inv, row_sum))
                link(nc.vector.tensor_scalar(row_inv[:, HEADS:], row_inv[:, HEADS:], neg_lam[:, l:l + 1], None, ALU.mult))
                for i in range(HEADS):
                    link(nc.vector.tensor_scalar(probs[:, HEADS + i, 0:n], probs[:, HEADS + i, 0:n],
                                                 row_inv[:, HEADS + i:HEADS + i + 1], None, ALU.mult))
                    nc.vector.scalar_tensor_tensor(out=probs[:, i, 0:n], in0=probs[:, i, 0:n], scalar=row_inv[:, i:i + 1],
                                                   in1=probs[:, HEADS + i, 0:n], op0=ALU.mult,
                                                   op1=ALU.add).then_inc(a_ready, 1)

            def o_sums(l, t):
                dve.wait_ge(osq_ready, TT * l + t + 1)
                nc.vector.tensor_reduce(o_ss, osq[:, :].rearrange("p (j n) -> p j n", j=HEADS), AX.X,
                                        ALU.add).then_inc(oss_ready, 1)

            def o_scale(l, t):
                dve.wait_ge(ostd_ready, TT * l + t + 1)
                link(nc.vector.reciprocal(o_inv, o_std))
                nc.vector.tensor_tensor(on[:, :].rearrange("p (j n) -> p j n", j=HEADS),
                                        ps[:, 6, :].rearrange("p (j n) -> p j n", j=HEADS),
                                        o_inv.rearrange("p (j o) -> p j o", o=1).broadcast_to([P, HEADS, DV]),
                                        ALU.mult).then_inc(on_ready, 1)

            def lower_mix(l, part, chunks, src, scale, cols=slice(0, SEQ)):
                dve.wait_ge(mixhi_ready, 4 * l + part + 1)
                hi = x_hi[:, chunks, cols].bitcast(F32)
                if scale is None:
                    ins = nc.vector.tensor_tensor(x_lo[:, chunks, cols], src, hi, ALU.subtract)
                else:
                    ins = nc.vector.scalar_tensor_tensor(out=x_lo[:, chunks, cols], in0=src, scalar=scale, in1=hi,
                                                         op0=ALU.mult, op1=ALU.subtract)
                ins.then_inc(mixlo_ready, 1)

            def mixer(l):
                for t in range(TT):
                    dve.wait_ge(qkT_ready, 4 * l + 2 + t + 1)
                    nc.vector.tensor_copy(kT[:, :, t * P:(t + 1) * P],
                                          ps[:, 6 + t, :].rearrange("p (j n) -> p j n", j=4)).then_inc(kT_copied, 1)
                dve.wait_ge(mean_ready, l + 1)
                both = lambda a: a.rearrange("p (o n) -> p o n", o=1).broadcast_to([P, 2, SEQ])
                nc.vector.tensor_tensor(yc[:, :, :], yc[:, :, :], both(ps[:, 7, 0:SEQ]), ALU.subtract).then_inc(yc_ready, 1)
                mask_scores(l, 0)
                dve.wait_ge(ystd_ready, l + 1)
                link(nc.vector.reciprocal(ysq[:, 1, :], ysq[:, 0, :]))
                nc.vector.tensor_tensor(yc[:, :, :], yc[:, :, :], both(ysq[:, 1, :]), ALU.mult).then_inc(yn_ready, 1)
                lower_mix(l, 0, slice(0, 2), yc[:, :, :], None)
                dve.wait_ge(gpre_ready, l + 1)
                nc.vector.tensor_tensor(g_pre[:, :, :], ps[:, 7, 0:SEQ].rearrange("p (t n) -> p t n", t=2),
                                        b_gate[:, l, :].rearrange("p (o n) -> p o n", o=1).broadcast_to([P, TT, P]),
                                        ALU.add).then_inc(gbias_ready, 1)
                differences(l, 0)
                dve.wait_ge(gln_ready, l + 1)
                nc.vector.scalar_tensor_tensor(out=log_a[:, :, :], in0=g_pre[:, :, :], scalar=0.0, in1=g_abs[:, :, :],
                                               op0=ALU.min, op1=ALU.subtract).then_inc(la_ready, 1)
                dve.wait_ge(aT_ready, TT * l + 1)
                mask_scores(l, 1)
                dve.wait_ge(gexp_ready, 2 * l + 2)
                link(nc.vector.tensor_tensor(z[:, :, C_GK:C_GV], z[:, :, C_GK:C_GV], g_exp[:, :, :], ALU.mult))
                for half in range(2):
                    nc.vector.tensor_scalar(kx_half[:, :, half, :], z[:, :, C_GK:C_GV], cst[:, K_HALF + half:K_HALF + half + 1],
                                            None, ALU.mult).then_inc(kx_ready, 1)
                o_sums(l, 0)
                o_scale(l, 0)
                for c in range(4):
                    if c % 2 == 0:
                        dve.wait_ge(kv_ready, 2 * l + c // 2 + 1)
                        nc.vector.tensor_tensor(
                            state[:, c:c + 2, :] if c == 0 else kv[:, :, :],
                            ps[:, 7, :].rearrange("p (j n) -> p j n", j=2),
                            cst[:, K_BD:K_BD + 256].rearrange("p (o n) -> p o n", o=1).broadcast_to([P, 2, 256]),
                            ALU.mult).then_inc(kv_masked, 1)
                        dve.wait_ge(kv_masked, 2 * l + c // 2 + 1)
                    if c:
                        nc.vector.scalar_tensor_tensor(
                            out=state[:, c, :], in0=state[:, c - 1, :], scalar=decay[:, c:c + 1],
                            in1=state[:, 1, :] if c == 1 else kv[:, c % 2, :], op0=ALU.mult,
                            op1=ALU.add).then_inc(state_ready, 1)
                        dve.wait_ge(state_ready, 3 * l + c)
                lower_mix(l, 1, slice(2, 6), ps[:, 4, :].rearrange("p (j n) -> p j n", j=4), vcol[:, l, V_SUB:V_SUB + 1],
                          slice(0, P))
                differences(l, 1)
                dve.wait_ge(gsq_ready, l + 1)
                heads = lambda a: a.rearrange("p (j n) -> p j n", n=GLA_DV)
                nc.vector.tensor_reduce(g_ss, heads(osq[:, :]), AX.X, ALU.add).then_inc(gss_ready, 1)
                dve.wait_ge(gstd_ready, l + 1)
                link(nc.vector.reciprocal(g_inv, g_std))
                link(nc.vector.tensor_tensor(heads(silu_g[:, :]), heads(ps[:, 7, :]),
                                             g_inv.rearrange("p (j o) -> p j o", o=1).broadcast_to([P, 8, GLA_DV]), ALU.mult))
                nc.vector.tensor_tensor(silu_g[:, :].rearrange("p (t n) -> p t n", t=2),
                                        silu_g[:, :].rearrange("p (t n) -> p t n", t=2), z[:, :, C_GR:C_GZ],
                                        ALU.mult).then_inc(gon_ready, 1)
                o_sums(l, 1)
                o_scale(l, 1)
                lower_mix(l, 2, slice(6, 8), ps[:, 7, :].rearrange("p (j n) -> p j n", j=2), vcol[:, l, V_GLA:V_GLA + 1])
                lower_mix(l, 3, slice(2, 6), ps[:, 4, :].rearrange("p (j n) -> p j n", j=4), vcol[:, l, V_SUB:V_SUB + 1],
                          slice(P, SEQ))
                dve.wait_ge(phi_ready, l + 1)
                nc.vector.tensor_tensor(p_lo[:, :, :], ps[:, 5, :].rearrange("p (j n) -> p j n", j=2),
                                        p_hi[:, :, :].bitcast(F32), ALU.subtract).then_inc(plo_ready, 1)

            def out_proj(l):
                for b in range(2):
                    c = T_OUT[l] + 2 * b
                    split_lo(dve, c + 3)
                    dve.wait_ge(tile_used, c + 2)
                    hb = h[:, :, 512 * b:512 * b + 512]
                    nc.vector.tensor_tensor(hb, hb, ps[:, 2 * b:2 * b + 2, :], ALU.add).then_inc(h_updated, 1)
                    split_lo(dve, c + 4)

            def ple_add(l, r):
                for b in range(2):
                    c = T_GATE[l] + 2 * b
                    if l == 0 or b == 0:
                        split_lo(dve, c + 3, r)
                    dve.wait_ge(gate_ready, 2 * l + b + 1)
                    link(nc.vector.tensor_tensor(gate[:, :, :], gate[:, :, :], up[:, :, 512 * b:512 * b + 512], ALU.mult))
                    hb = h[:, :, 512 * b:512 * b + 512]
                    nc.vector.tensor_tensor(hb, hb, gate[:, :, :], ALU.add).then_inc(h_updated, 1)
                    if l == 0:
                        split_lo(dve, c + 4)

            def lambdas():
                dve.wait_ge(misc_landed, 16 * N_MISC)
                for l in range(DEPTH):
                    link(nc.vector.tensor_tensor(lam_mul[:, l, :, :], lam_row[:, l, 0::2, :], lam_row[:, l, 1::2, :],
                                                 ALU.mult))
                    nc.vector.tensor_reduce(lam_exp[:, l, :], lam_mul[:, l, :, :], AX.X, ALU.add).then_inc(setup_done, 1)
                dve.wait_ge(vec_ready, 2)
                for l in range(DEPTH):
                    lam_init = 0.8 - 0.6 * math.exp(-0.3 * l)
                    link(nc.vector.scalar_tensor_tensor(out=neg_lam[:, l:l + 1], in0=lam_exp[:, l, 1:2], scalar=-lam_init,
                                                        in1=lam_exp[:, l, 0:1], op0=ALU.add, op1=ALU.subtract))
                    link(nc.vector.tensor_scalar(vcol[:, l, V_SUB:V_SUB + 1], vcol[:, l, V_SUB:V_SUB + 1],
                                                 1.0 - lam_init, None, ALU.mult))

            nc.vector.memset(eps_t[:, :], EPS).then_inc(setup_done, 1)
            link(nc.vector.memset(e_gate[:, :, :], 0.0))
            link(nc.vector.memset(slot_of[:, :, :], 0.0))
            link(nc.vector.memset(uT[:, :, :], 0.0))
            link(nc.vector.memset(zeros[:, :].bitcast(F32), 0.0))
            norm_scale(0)
            for c in range(3):
                split_lo(dve, c)
            for l in range(DEPTH):
                if l:
                    norm_scale(3)
                norm_split(3 * l, l, V_MIX)
                in_proj(l)
                if l == 0:
                    lambdas()
                mixer(l)
                out_proj(l)
                if l == 0:
                    norm_scale(1)
                    norm_split(1, 0, V_FFN)

                    def ffn_mult(b):
                        dve.wait_ge(f_silu, b + 1)
                        nc.vector.tensor_tensor(ff[:, :].rearrange("p (t n) -> p t n", t=2),
                                                silu_g[:, :].rearrange("p (t n) -> p t n", t=2), ps[:, 0:2, FB:2 * FB],
                                                ALU.mult).then_inc(f_act, 1)

                    def ffn_T(b):
                        dve.wait_ge(f_hi, b + 1)
                        nc.vector.tensor_tensor(ff_lo[:, :], ps[:, 2, :], ff_hi[:, :].bitcast(F32),
                                                ALU.subtract).then_inc(f_lo, 1)

                    ffn_mult(0)
                    with dve.Fori(0, (N_FB - 1) // 2) as i:
                        for s in range(2):
                            c = T_FFN + 2 + 3 * s
                            split_lo(dve, c + 1, i)
                            split_lo(dve, c + 2, i)
                            ffn_T(i * 2 + s)
                            split_lo(dve, c + 3, i)
                            ffn_mult(i * 2 + (1 + s))
                    split_lo(dve, T_UP[0])
                    split_lo(dve, T_UP[0] + 1)
                    ffn_T(N_FB - 1)
                    split_lo(dve, T_UP[0] + 2)
                    dve.wait_ge(tile_used, T_UP[0])
                    hv = h[:, :, :].rearrange("p t n -> p (t n)")
                    nc.vector.tensor_tensor(hv, hv, ps[:, 4:8, :].rearrange("p b n -> p (b n)"), ALU.add).then_inc(h_updated, 1)
                    norm_scale(2)
                    split_lo(dve, T_UP[0] + 3)
                    norm_split(2, 0, V_PLE)
                    ple_add(0, None)

            split_lo(dve, T_UP[1] + 3)
            norm_scale(4)
            norm_split(4, 1, V_FFN)
            dve.wait_ge(rw_hi_ready, 1)
            nc.vector.tensor_tensor(rw_lo[:, :, :], rw[:, :, :], rw_hi[:, :, :].bitcast(F32), ALU.subtract).then_inc(rw_lo_ready, 1)
            dve.wait_ge(xnT_ready, 4 * 5)
            dve.wait_ge(grow_landed, 16)
            for t in range(TT):
                nc.vector.tensor_tensor(xn[:, t, :], xn[:, t, :], g_row[:, :], ALU.mult).then_inc(xg_ready, 1)
            dve.wait_ge(logit_ready, 1)
            link(nc.vector.tensor_copy(logit[:, :, :], ps[:, 0, 0:TT * N_EXP].rearrange("p (t e) -> p t e", t=2)))
            for t in range(TT):
                own = logit[:, t, :].rearrange("p (e o) -> p e o", o=1).broadcast_to([P, N_EXP, N_EXP])
                other = logit[:, t, :].rearrange("p (o e) -> p o e", o=1).broadcast_to([P, N_EXP, N_EXP])
                sq = lambda a: a.rearrange("p (a b) -> p a b", a=N_EXP)
                link(nc.vector.tensor_tensor(sq(cmp_a[:, t, :]), own, other, ALU.is_lt))
                link(nc.vector.tensor_tensor(sq(cmp_b[:, t, :]), own, other, ALU.is_equal))
                link(nc.vector.tensor_tensor(cmp_b[:, t, :], cmp_b[:, t, :], cst[:, K_TIE:K_TIE + 64], ALU.mult))
                link(nc.vector.tensor_tensor(cmp_a[:, t, :], cmp_a[:, t, :], cmp_b[:, t, :], ALU.add))
                link(nc.vector.tensor_reduce(chosen[:, t, :], sq(cmp_a[:, t, :]), AX.X, ALU.add))
                link(nc.vector.tensor_reduce(top[:, t:t + 1], logit[:, t, :], AX.X, ALU.max))
                link(nc.vector.tensor_scalar(e_gate[:, t, 1:1 + N_EXP], logit[:, t, :], top[:, t:t + 1], None, ALU.subtract))
            nc.vector.tensor_scalar(chosen[:, :, :], chosen[:, :, :], 1.5, None, ALU.is_lt).then_inc(chosen_ready, 1)
            dve.wait_ge(chosen_ready, 1)
            dve.wait_ge(lexp_ready, 1)
            eg = e_gate[:, :, 1:1 + N_EXP]
            link(nc.vector.tensor_tensor(eg, eg, chosen[:, :, :], ALU.mult))
            link(nc.vector.tensor_reduce(gsum, eg, AX.X, ALU.add))
            link(nc.vector.reciprocal(gsum, gsum))
            for t in range(TT):
                link(nc.vector.tensor_scalar(e_gate[:, t, 1 + N_EXP:], eg[:, t, :], gsum[:, t:t + 1], None, ALU.mult))
                link(nc.vector.tensor_copy(eg[:, t, :], e_gate[:, t, 1 + N_EXP:]))
            dve.wait_ge(rank_ready, 1)
            for t in range(TT):
                link(nc.vector.scalar_tensor_tensor(out=slot_of[:, t, 0:N_EXP], in0=ps[:, 1, t * N_EXP:(t + 1) * N_EXP],
                                                    scalar=1.0, in1=chosen[:, t, :], op0=ALU.add, op1=ALU.mult))
                link(nc.vector.tensor_scalar(slot_of[:, t, N_EXP:2 * N_EXP], slot_of[:, t, 0:N_EXP], -1.0 - P, None, ALU.add))
                link(nc.vector.tensor_scalar(slot_of[:, t, 0:N_EXP], slot_of[:, t, 0:N_EXP], -1.0, None, ALU.add))
            link(nc.vector.tensor_reduce(count_max, ps[:, 1, 2 * N_EXP:3 * N_EXP], AX.X, ALU.max))
            nc.vector.tensor_scalar(passes_t[:, :], count_max, P + 0.5, 1.0, ALU.is_gt, ALU.add).then_inc(passes_ready, 1)
            dve.wait_ge(passes_ready, 1)
            nc.vector.memset(pickT[:, :].bitcast(F32), 0.0).then_inc(m_pickT_copied, 1)
            for free in (m_act, m_lo):
                dve.sem_inc(free, 1)

            def picks(n):
                for t in range(TT):
                    nc.vector.tensor_scalar(pick[:, t, :], cst[:, K_IOTA:K_IOTA + P], slot_of[:, t, bass.ds(n, 1)], None,
                                            ALU.is_equal).then_inc(m_pick, 1)

            def expert_rows_lo(n):
                for half in range(2):
                    dve.wait_ge(m_xhi, n * 2 + (half + 1))
                    nc.vector.tensor_tensor(xe_lo[:, 4 * half:4 * half + 4, :],
                                            ps[:, 6 + half, :].rearrange("p (k n) -> p k n", k=4),
                                            xe_hi[:, 4 * half:4 * half + 4, :].bitcast(F32),
                                            ALU.subtract).then_inc(m_xlo, 1)

            def expert_out_lo(n):
                for half in range(2):
                    dve.wait_ge(m_yhi, n * 2 + (half + 1))
                    cols = slice(512 * half, 512 * half + 512)
                    nc.vector.tensor_tensor(y_lo[:, cols], ps[:, 4 + half, :], y_hi[:, cols].bitcast(F32),
                                            ALU.subtract).then_inc(m_ylo, 1)

            def add_rows(n):
                for t, bank in ((1, 4), (0, 6)):
                    dve.wait_ge(m_scattered, n * 2 + (2 - t))
                    nc.vector.scalar_tensor_tensor(
                        out=h[:, t, :], in0=ps[:, bank:bank + 2, :].rearrange("p b n -> p (b n)"),
                        scalar=e_gate[:, t, bass.ds(n, 1)], in1=h[:, t, :], op0=ALU.mult,
                        op1=ALU.add).then_inc(m_added, 1)

            picks(0)
            passes = dve.value_load(passes_t[0:1, 0:1], min_val=1, max_val=2)
            expert_rows_lo(0)
            with dve.Fori(0, passes) as ps_i:
                with dve.Fori(0, N_EXP) as e:
                    n = ps_i * N_EXP + e
                    r0 = n * N_MB

                    def mult(m, c, r):
                        dve.wait_ge(tile_used, nth(c, r))
                        dve.wait_ge(m_silu, m)
                        nc.vector.tensor_tensor(ff[:, :], silu_g[:, :], ps[:, 1, :], ALU.mult).then_inc(m_act, 1)

                    def lower_T(m):
                        dve.wait_ge(m_hi, m)
                        nc.vector.tensor_tensor(ff_lo[:, :], ps[:, 2, :], ff_hi[:, :].bitcast(F32),
                                                ALU.subtract).then_inc(m_lo, 1)

                    expert_out_lo(n)
                    for c in range(3, 6):
                        split_lo(dve, T_MOE + c, r0)
                    mult(r0 + 1, T_MOE + 3, r0)
                    add_rows(n)
                    dve.wait_ge(m_pickT, n + 1)
                    picks(n + 1)
                    with dve.Fori(1, N_MB) as b:
                        r = r0 + b - 1
                        split_lo(dve, T_MOE + 6, r)
                        lower_T(r0 + b)
                        for c in range(7, 11):
                            split_lo(dve, T_MOE + c, r)
                        mult(r0 + b + 1, T_MOE + 7, r)
                        split_lo(dve, T_MOE + 11, r)
                    r1 = r0 + N_MB
                    lower_T(r1)
                    split_lo(dve, T_MOE + 0, r1)
                    expert_rows_lo(n + 1)
                    split_lo(dve, T_MOE + 1, r1)
                    split_lo(dve, T_MOE + 2, r1)
            expert_out_lo(passes * N_EXP)
            add_rows(passes * N_EXP)
            norm_scale(5)
            norm_split(5, 1, V_PLE)
            ple_add(1, passes * (N_EXP * N_MB))
            dve.wait_ge(std_ready, 7)
            link(nc.vector.reciprocal(rstd, std))
            dve.wait_ge(frow_landed, 16)
            for t in range(TT):
                ins = nc.vector.scalar_tensor_tensor(out=xn[:, t, :], in0=h[:, t, :], scalar=rstd[:, t:t + 1],
                                                     in1=g_row[:, :], op0=ALU.mult, op1=ALU.mult)
                if t == 0:
                    link(ins)
            ins.then_inc(out_ready, 1)

        @block.tensor
        def _(pe):
            def transpose(dst, src, n=P):
                return nc.tensor.transpose(dst, src, ident[0:n, 0:n])

            def norm_T(q):
                pe.wait_ge(xn_ready, 2 * q + 2)
                for k in range(KC):
                    for t in range(TT):
                        ins = transpose(ps[:, 4 + k // 2, (k % 2) * SEQ + t * P:(k % 2) * SEQ + (t + 1) * P],
                                        xn[:, t, k * P:(k + 1) * P])
                    if k % 2:
                        ins.then_inc(xnT_ready, 1)

            def tile(c, r=None):
                pe.wait_ge(lo_ready, nth(c, r))
                return w_hi[:, c % SPLIT, :], w_lo[:, c % SPLIT, :]

            def columns(c, r, bank, width, half):
                wh, wl = tile(c, r)
                wh, wl = (w[:, 0:4 * width].rearrange("p (k n) -> p k n", k=4) for w in (wh, wl))
                for kk in range(4):
                    k = 4 * half + kk
                    for t in range(TT):
                        ins = products(ps[:, bank + t, 0:width], x_hi[:, k, t * P:(t + 1) * P],
                                       x_lo[:, k, t * P:(t + 1) * P], wh[:, kk, :], wl[:, kk, :],
                                       k == 0, k == KC - 1)
                ins.then_inc(tile_used, 1)

            def rows_tile(c, r, bank, xh, xl, start, stop):
                wh, wl = tile(c, r)
                wh, wl = (w.rearrange("p (k m n) -> p k m n", k=2, m=2) for w in (wh, wl))
                for k in range(2):
                    for t in range(TT):
                        for m in range(2):
                            ins = products(ps[:, bank + 2 * t + m, :], xh[:, k, t * P:(t + 1) * P],
                                           xl[:, k, t * P:(t + 1) * P], wh[:, k, m, :], wl[:, k, m, :],
                                           start and k == 0, stop and k == 1)
                ins.then_inc(tile_used, 1)

            def in_proj(l):
                pe.wait_ge(xlo_ready, 8 * (3 * l + 1))
                for b, (c0, c1) in enumerate(IN_BLOCKS):
                    if b >= 2:
                        pe.wait_ge(z_ready, 8 * l + Z_DONE[b - 2])
                    for half in range(2):
                        columns(T_IN[l] + 2 * b + half, None, 2 * (b % 2), c1 - c0, half)
                    if b == 2:
                        pe.wait_ge(u_ready, l + 1)
                        for j in range(2):
                            for t in range(TT):
                                ins = transpose(ps[:, 4, j * SEQ + t * P:j * SEQ + (t + 1) * P],
                                                z[:, t, j * P:(j + 1) * P])
                        ins.then_inc(uT_ready, 1)

            def scores(l, t):
                if t:
                    pe.wait_ge(masked_ready, 2 * TT * l + 2)
                else:
                    pe.wait_ge(z_ready, 8 * l + 8)
                    pe.wait_ge(qT_copied, 2 * l + 2)
                    pe.wait_ge(kT_copied, 2 * l + 2)
                n = P * (t + 1)
                for c in range(2):
                    for i in range(HEADS):
                        ins = nc.tensor.matmul(ps[:, 2 * c + i // 2, (i % 2) * SEQ:(i % 2) * SEQ + n],
                                               qT[c * DH:(c + 1) * DH, i, t * P:(t + 1) * P],
                                               kT[c * DH:(c + 1) * DH, i, 0:n], start=True, stop=True)
                ins.then_inc(scores_ready, 1)

            def probs_T(l, t):
                pe.wait_ge(a_ready, HEADS * (TT * l + t + 1))
                for kt in range(t + 1):
                    for i in range(HEADS):
                        ins = transpose(ps[:, 4 + kt, i * P:(i + 1) * P], probs[:, i, kt * P:(kt + 1) * P])
                ins.then_inc(aT_ready, 1)

            def values(l, t):
                pe.wait_ge(aT_copied, 3 * l + (1 if t == 0 else 3))
                if t:
                    pe.wait_ge(on_ready, TT * l + 1)
                for i in range(HEADS):
                    for kt in range(t + 1):
                        ins = nc.tensor.matmul(ps[:, 6, i * DV:(i + 1) * DV], aT[:, kt, i * P:(i + 1) * P],
                                               z[:, kt, C_DV + i * DV:C_DV + (i + 1) * DV],
                                               start=kt == 0, stop=kt == t)
                ins.then_inc(o_ready, 1)

            def o_T(l, t):
                pe.wait_ge(on_ready, TT * l + t + 1)
                for i in range(HEADS):
                    ins = transpose(ps[:, 4, i * P:(i + 1) * P], on[:, i * DV:(i + 1) * DV])
                ins.then_inc(onT_ready, 1)

            def mixer(l):
                pe.wait_ge(rope_done, 4 * (l + 1))
                pe.wait_ge(uT_copied, l + 1)
                for s, c0 in enumerate((C_DQ, C_DK)):
                    for t in range(TT):
                        for i in range(HEADS):
                            ins = transpose(ps[:, 4 + 2 * s + t, i * P:(i + 1) * P], z[:, t, c0 + i * P:c0 + (i + 1) * P])
                        ins.then_inc(qkT_ready, 1)
                pe.wait_ge(tap_done, 2 * TAPS * (l + 1))
                pe.wait_ge(kT_copied, 2 * l + 2)
                for j in range(2):
                    ins = nc.tensor.matmul(ps[:, 7, 0:SEQ], cst[:, K_MEAN:K_MEAN + P], yc[:, j, :], start=j == 0, stop=j == 1)
                ins.then_inc(mean_ready, 1)
                scores(l, 0)
                pe.wait_ge(ysq_ready, l + 1)
                for j in range(2):
                    ins = nc.tensor.matmul(ps[:, 7, SEQ:2 * SEQ], cst[:, K_MEAN:K_MEAN + P], ysq[:, j, :], start=j == 0, stop=j == 1)
                ins.then_inc(var_ready, 1)
                pe.wait_ge(ystd_ready, l + 1)
                for t in range(TT):
                    transpose(ps[:, 7, t * P:(t + 1) * P], z[:, t, C_GQ:C_GK])
                for t in range(TT):
                    ins = transpose(ps[0:RANK, 7, SEQ + t * P:SEQ + (t + 1) * P], z[:, t, C_GZ:D_IN])
                ins.then_inc(gT_ready, 1)
                pe.wait_ge(gT_copied, 2 * l + 2)
                for t in range(TT):
                    ins = nc.tensor.matmul(ps[:, 7, t * P:(t + 1) * P], gzT[0:RANK, t * P:(t + 1) * P], w_g2[0:RANK, l, :],
                                           start=True, stop=True)
                ins.then_inc(gpre_ready, 1)
                scores(l, 1)
                probs_T(l, 0)
                pe.wait_ge(la_ready, l + 1)
                for t in range(TT):
                    nc.tensor.matmul(ps[:, 7, t * P:(t + 1) * P], cst[:, K_REV:K_REV + P], log_a[:, t, :], start=True, stop=True)
                for t in range(TT):
                    ins = nc.tensor.matmul(ps[:, 7, SEQ + 2 * t:SEQ + 2 * t + 2], log_a[:, t, :], cst[:, K_HALF:K_HALF + 2],
                                           start=True, stop=True)
                ins.then_inc(rev_ready, 1)
                values(l, 0)
                for t in range(TT):
                    pe.wait_ge(kx_ready, 2 * l + 2)
                    if t:
                        pe.wait_ge(kv_masked, 2 * l + 1)
                    for half in range(2):
                        ins = nc.tensor.matmul(ps[:, 7, half * 256:half * 256 + 256], kx_half[:, t, half, :],
                                               z[:, t, C_GV:C_GR], start=True, stop=True)
                    ins.then_inc(kv_ready, 1)
                    if t == 0:
                        o_T(l, 0)
                pe.wait_ge(state_ready, 3 * (l + 1))
                for t in range(TT):
                    for half in range(2):
                        ins = nc.tensor.matmul(ps[half * CHUNK:(half + 1) * CHUNK, 7, t * 256:t * 256 + 256],
                                               gqT[:, t * P + half * CHUNK:t * P + (half + 1) * CHUNK],
                                               state[:, 2 * t + half, :], start=True, stop=True)
                ins.then_inc(go_ready, 1)
                pe.wait_ge(mixlo_ready, 4 * l + 2)
                probs_T(l, 1)
                values(l, 1)
                pe.wait_ge(gon_ready, l + 1)
                for j in range(2):
                    for t in range(TT):
                        ins = transpose(ps[:, 7, j * SEQ + t * P:j * SEQ + (t + 1) * P],
                                        silu_g[:, t * 256 + j * P:t * 256 + (j + 1) * P])
                ins.then_inc(gonT_ready, 1)
                o_T(l, 1)
                for j in range(2):
                    for t in range(TT):
                        ins = transpose(ps[:, 5, j * SEQ + t * P:j * SEQ + (t + 1) * P], pt[:, l, t, j * P:(j + 1) * P])
                ins.then_inc(pT_ready, 1)

            def square(first, r):
                for b in range(2):
                    for half in range(2):
                        columns(first + 2 * b + half, r, 2 * b, 512, half)

            def up_proj(l):
                pe.wait_ge(plo_ready, l + 1)
                rows_tile(T_UP[l], None, 0, p_hi, p_lo, True, True)

            pe.wait_ge(cst_landed, 16)
            pe.wait_ge(vec_landed, 16 * N_VEC_DMAS * DEPTH)
            for l in range(DEPTH):
                ins = transpose(ps[:, l, 0:V_ROWS], vrows[0:V_ROWS, l, :], V_ROWS)
            ins.then_inc(vecT_ready, 1)
            pe.wait_ge(vec_ready, 1)
            for l in range(DEPTH):
                norm_T(3 * l)
                in_proj(l)
                if l == 0:
                    pe.wait_ge(misc_landed, 16 * N_MISC)
                mixer(l)
                pe.wait_ge(mixlo_ready, 4 * (l + 1))
                square(T_OUT[l], None)
                if l == 0:
                    norm_T(1)
                    pe.wait_ge(xlo_ready, 16)

                    def gate_up(c, r):
                        for half in range(2):
                            columns(c + half, r, 0, 512, half)

                    def ffn_T(b):
                        pe.wait_ge(f_act, b + 1)
                        for k in range(2):
                            for t in range(TT):
                                ins = transpose(ps[:, 2, k * SEQ + t * P:k * SEQ + (t + 1) * P],
                                                ff[:, t * FB + k * P:t * FB + (k + 1) * P])
                        ins.then_inc(f_T, 1)

                    def down(c, r, b, stop):
                        pe.wait_ge(f_lo, b + 1)
                        rows_tile(c, r, 4, ff_hi[:, :].rearrange("p (k n) -> p k n", k=2),
                                  ff_lo[:, :].rearrange("p (k n) -> p k n", k=2), False, stop)

                    for b in range(4):
                        nc.tensor.matmul(ps[:, 4 + b, :], x_hi[:, 0, 0:P], zeros[:, :], start=True, stop=False)
                    gate_up(T_FFN, None)
                    ffn_T(0)
                    with pe.Fori(0, (N_FB - 1) // 2) as i:
                        for s in range(2):
                            b = i * 2 + (1 + s)
                            gate_up(T_FFN + 2 + 3 * s, i)
                            down(T_FFN + 4 + 3 * s, i, b - 1, False)
                            ffn_T(b)
                    down(T_UP[0] - 1, None, N_FB - 1, True)
                    up_proj(0)
                    norm_T(2)
                    pe.wait_ge(xlo_ready, 24)
                    pe.wait_ge(up_ready, 1)
                    square(T_GATE[0], None)
            pe.wait_ge(h_updated, 7)
            up_proj(1)
            norm_T(4)
            pe.wait_ge(xlo_ready, 8 * 5)
            pe.wait_ge(rw_lo_ready, 1)
            pe.wait_ge(up_ready, 2)
            for t in range(TT):
                n = 0
                for k in range(KC):
                    for a in (x_hi, x_lo):
                        for w in (rw_hi, rw_lo):
                            ins = nc.tensor.matmul(ps[:, 0, t * N_EXP:(t + 1) * N_EXP], a[:, k, t * P:(t + 1) * P],
                                                   w[:, k, :], start=n == 0, stop=n == 4 * KC - 1)
                            n += 1
            ins.then_inc(logit_ready, 1)
            pe.wait_ge(chosen_ready, 1)
            nc.tensor.matmul(ps[:, 1, 0:N_EXP], cst[:, K_RANK:K_RANK + P], chosen[:, 0, :], start=True, stop=True)
            nc.tensor.matmul(ps[:, 1, N_EXP:2 * N_EXP], cst[:, K_ONES:K_ONES + P], chosen[:, 0, :], start=True, stop=False)
            nc.tensor.matmul(ps[:, 1, N_EXP:2 * N_EXP], cst[:, K_RANK:K_RANK + P], chosen[:, 1, :], start=False, stop=True)
            nc.tensor.matmul(ps[:, 1, 2 * N_EXP:3 * N_EXP], cst[:, K_ONES:K_ONES + P], chosen[:, 0, :], start=True, stop=False)
            nc.tensor.matmul(ps[:, 1, 2 * N_EXP:3 * N_EXP], cst[:, K_ONES:K_ONES + P], chosen[:, 1, :], start=False,
                             stop=True).then_inc(rank_ready, 1)
            pe.wait_ge(xg_ready, 2)
            pe.wait_ge(passes_ready, 1)
            passes = pe.value_load(passes_t[0:1, 0:1], min_val=1, max_val=2)

            def gather(n):
                pe.wait_ge(m_pick, n * 2 + 2)
                for k in range(KC):
                    for t in range(TT):
                        ins = nc.tensor.matmul(ps[:, 6 + k // 4, (k % 4) * P:(k % 4 + 1) * P],
                                               xn[:, t, k * P:(k + 1) * P], pick[:, t, :], start=t == 0, stop=t == 1)
                    if k % 4 == 3:
                        ins.then_inc(m_gathered, 1)

            def scatter(n):
                pe.wait_ge(m_pickT_copied, n + 1)
                pe.wait_ge(m_ylo, n * 2 + 2)
                for t, bank in ((1, 4), (0, 6)):
                    for m in range(2):
                        cols = slice(512 * m, 512 * m + 512)
                        nc.tensor.matmul(ps[:, bank + m, :], pickT[:, t * P:(t + 1) * P], y_hi[:, cols],
                                         start=True, stop=False)
                        ins = nc.tensor.matmul(ps[:, bank + m, :], pickT[:, t * P:(t + 1) * P], y_lo[:, cols],
                                               start=False, stop=True)
                    ins.then_inc(m_scattered, 1)

            gather(0)
            with pe.Fori(0, passes) as ps_i:
                with pe.Fori(0, N_EXP) as e:
                    n = ps_i * N_EXP + e
                    r0 = n * N_MB

                    def gate_up(c, r, m):
                        pe.wait_ge(m_act, m + 1)
                        for s in range(2):
                            for half in range(2):
                                wh, wl = tile(c + 2 * s + half, r)
                                wh, wl = (w.rearrange("p (k n) -> p k n", k=4) for w in (wh, wl))
                                for kk in range(4):
                                    k = 4 * half + kk
                                    ins = products(ps[:, s, :], xe_hi[:, k, :], xe_lo[:, k, :], wh[:, kk, :], wl[:, kk, :],
                                                   k == 0, k == KC - 1)
                                ins.then_inc(tile_used, 1)

                    def act_T(m):
                        pe.wait_ge(m_act, m + 2)
                        pe.wait_ge(m_lo, m + 1)
                        for k in range(4):
                            ins = transpose(ps[:, 2, k * P:(k + 1) * P], ff[:, k * P:(k + 1) * P])
                        ins.then_inc(m_T, 1)

                    def down(c, r, m, stop):
                        pe.wait_ge(m_lo, m + 2)
                        for half in range(2):
                            wh, wl = tile(c + half, r)
                            wh, wl = (w.rearrange("p (k m n) -> p k m n", k=2, m=2) for w in (wh, wl))
                            for kk in range(2):
                                k = 2 * half + kk
                                for s in range(2):
                                    ins = products(ps[:, 4 + s, :], ff_hi[:, k * P:(k + 1) * P], ff_lo[:, k * P:(k + 1) * P],
                                                   wh[:, kk, s, :], wl[:, kk, s, :], False, stop and k == 3)
                            ins.then_inc(tile_used, 1)

                    pe.wait_ge(m_xlo, n * 2 + 2)
                    gate_up(T_MOE, r0, r0)
                    scatter(n)
                    for t in range(TT):
                        ins = transpose(ps[:, 3, t * P:(t + 1) * P], pick[:, t, :])
                    ins.then_inc(m_pickT, 1)
                    act_T(r0)
                    pe.wait_ge(m_added, n * 2 + 1)
                    for m in range(2):
                        nc.tensor.matmul(ps[:, 4 + m, :], xe_hi[:, 0, :], zeros[:, :], start=True, stop=False)
                    with pe.Fori(1, N_MB) as b:
                        r = r0 + b - 1
                        gate_up(T_MOE + 4, r, r0 + b)
                        down(T_MOE + 8, r, r, False)
                        act_T(r0 + b)
                    pe.wait_ge(m_added, n * 2 + 2)
                    gather(n + 1)
                    down(T_MOE + 4, r0 + (N_MB - 1), r0 + (N_MB - 1), True)
            scatter(passes * N_EXP)
            pe.wait_ge(m_added, passes * (2 * N_EXP) + 2)
            norm_T(5)
            pe.wait_ge(xlo_ready, 8 * 6)
            square(T_GATE[1], passes * (N_EXP * N_MB))


_INS = ["x", "p", "norm_mix_g", "w_in", "conv_w", "conv_b", "conv_ln_g", "conv_ln_b", "diff_lambda", "diff_subln_g",
        "gla_w_gate2", "gla_b_gate", "gla_norm_g", "w_out", "norm_ffn_g", "ffn_w_gu", "ffn_w_down", "router_w",
        "moe_w_gu", "moe_w_down", "ple_w_up", "ple_w_gate", "ple_norm_g", "final_norm_g"]


def kernel(**inputs):
    import concourse.bacc as bacc
    from concourse.bass_utils import run_bass_kernel_spmd

    nc = bacc.Bacc("TRN2", target_bir_lowering=False, num_devices=1)
    arrays, args = {}, []
    for name in _INS:
        arrays[name + "_d"] = np.ascontiguousarray(inputs[name])
    arrays["consts_d"] = constants()
    for name, a in arrays.items():
        args.append(nc.dram_tensor(name, a.shape, mybir.dt.from_np(a.dtype), kind="ExternalInput").ap())
    args.append(nc.dram_tensor("out_d", (1, SEQ, D), F32, kind="ExternalOutput").ap())
    build(nc, *args)
    r = run_bass_kernel_spmd(nc, [arrays], core_ids=[0])
    return r.results[0]["out_d"]
```

```python
import math
from contextlib import ExitStack

import numpy as np

import concourse.bass as bass
from concourse import mybir

P = 128
F32 = mybir.dt.float32
F32R = mybir.dt.float32r
I32 = mybir.dt.int32
ALU = mybir.AluOpType
ACT = mybir.ActivationFunctionType
AX = mybir.AxisListType

D = 1024
SEQ = 256
DEPTH = 2
TT = SEQ // P
KC = D // P
CHUNK = 64
CONV_CH = 256
TAPS = 31
HEADS = 4
DH = 64
DV = 128
GLA_HEADS = 4
GLA_DK = 32
GLA_DV = 64
RANK = 16
TAU = 16.0
ROT = 16
D_FF = 2816
N_EXP = 8
D_FE = 3584
PLE = 256
EPS = 1e-6

C_A, C_G, C_DQ, C_DK, C_DV = 0, 256, 512, 1024, 1536
C_GQ, C_GK, C_GV, C_GR, C_GZ = 2048, 2176, 2304, 2560, 2816
D_IN = 2832
IN_BLOCKS = [(c, min(c + 512, D_IN)) for c in range(0, 2560, 512)] + [(2560, D_IN)]

RING = 6
SPLIT = 3
TILE = 2048

V_MIX, V_FFN, V_PLE, V_CB, V_LG, V_LB, V_SUB, V_GLA, V_TAP = 0, 8, 16, 24, 26, 28, 30, 31, 32
V_ROWS = V_TAP + 2 * TAPS

FB = 256
N_FB = D_FF // FB
MB = 512
N_MB = D_FE // MB
T_IN = [0, 54]
T_OUT = [12, 66]
T_FFN = 16
T_UP = [49, 70]
T_GATE = [50, 71]
T_MOE = 71
E_TILES = 6 * N_MB
assert T_FFN + 3 * N_FB == T_UP[0] and E_TILES % RING == 0

K_ID, K_IOTA, K_RANK, K_REV, K_ONES, K_MEAN = (P * i for i in range(6))
K_MASK = 6 * P
K_BD = K_MASK + TT * SEQ
K_COS = K_BD + 256
K_SIN = K_COS + TT * 8
K_HALF = K_SIN + TT * 8
K_TIE = K_HALF + 2
K_END = K_TIE + 64


def constants():
    c = np.zeros((P, K_END), np.float32)
    i = np.arange(P)
    c[:, K_ID:K_ID + P] = np.eye(P)
    c[:, K_IOTA:K_IOTA + P] = i[None, :]
    c[:, K_RANK:K_RANK + P] = i[:, None] < i[None, :]
    c[:, K_REV:K_REV + P] = (i[:, None] > i[None, :]) & (i[:, None] // CHUNK == i[None, :] // CHUNK)
    c[:, K_ONES:K_ONES + P] = 1.0
    c[:, K_MEAN:K_MEAN + P] = 1.0 / CONV_CH
    k = np.arange(SEQ)
    for t in range(TT):
        q = t * P + i
        c[:, K_MASK + t * SEQ:K_MASK + (t + 1) * SEQ] = np.where(
            k[None, :] // CHUNK <= q[:, None] // CHUNK, 0.0, -1e30)
    c[:, K_BD:K_BD + 256] = i[:, None] // GLA_DK == np.arange(256)[None, :] // GLA_DV
    freq = np.float32(500000.0) ** (-np.arange(0, ROT, 2, dtype=np.float32) / np.float32(ROT))
    ang = np.arange(SEQ, dtype=np.float32)[:, None] * freq[None, :].astype(np.float32)
    for t in range(TT):
        c[:, K_COS + 8 * t:K_COS + 8 * t + 8] = np.cos(ang[t * P:(t + 1) * P])
        c[:, K_SIN + 8 * t:K_SIN + 8 * t + 8] = np.sin(ang[t * P:(t + 1) * P])
    c[:, K_HALF] = i < CHUNK
    c[:, K_HALF + 1] = i >= CHUNK
    e = np.arange(N_EXP)
    c[:, K_TIE:K_TIE + 64] = (e[None, :] < e[:, None]).reshape(1, 64)
    return c


def build(nc, x, p, norm_mix_g, w_in, conv_w, conv_b, conv_ln_g, conv_ln_b, diff_lambda, diff_subln_g,
          gla_w_gate2, gla_b_gate, gla_norm_g, w_out, norm_ffn_g, ffn_w_gu, ffn_w_down, router_w,
          moe_w_gu, moe_w_down, ple_w_up, ple_w_gate, ple_norm_g, final_norm_g, consts, out):
    with ExitStack() as ctx:
        def sb(name, shape, dt=F32):
            return ctx.enter_context(nc.sbuf_tensor(name, [P] + shape, dt))

        def sem(name):
            return ctx.enter_context(nc.semaphore(name))

        raw = sb("raw", [RING, TILE])
        w_hi = sb("w_hi", [SPLIT, TILE], F32R)
        w_lo = sb("w_lo", [SPLIT, TILE], F32R)
        cst = sb("cst", [K_END])
        h = sb("h", [TT, D])
        with nc.sbuf_tensor("xb_hi", [P, KC, SEQ], F32R) as xb_hi:
            pass
        xn = sb("xn", [TT, D])
        x_hi = sb("x_hi", [KC, SEQ], F32R)
        x_lo = sb("x_lo", [KC, SEQ], F32R)
        with (nc.sbuf_tensor("z_front", [P, C_DV], F32), nc.sbuf_tensor("xb_lo0", [P, 4, SEQ], F32R) as xb_lo0,
              nc.sbuf_tensor("z_mid", [P, D_IN - 4 * SEQ], F32), nc.sbuf_tensor("xb_lo1", [P, 4, SEQ], F32R) as xb_lo1):
            pass
        z = sb("z", [TT, D_IN])
        uT = sb("uT", [2, TAPS - 1 + SEQ])
        yc = sb("yc", [2, SEQ])
        ysq = sb("ysq", [2, SEQ])
        probs = sb("probs", [2 * HEADS, SEQ])
        aT = sb("aT", [TT, HEADS * P])
        vcol = sb("vcol", [DEPTH, V_ROWS])
        lam_mul = sb("lam_mul", [DEPTH, 2, DH])
        lam_exp = sb("lam_exp", [DEPTH, 2])
        neg_lam = sb("neg_lam", [DEPTH])
        w_g2 = sb("w_g2", [DEPTH, P])
        b_gate = sb("b_gate", [DEPTH, P])
        gqT = sb("gqT", [SEQ])
        gzT = sb("gzT", [SEQ])
        decay = sb("decay", [4])
        kx_half = sb("kx_half", [TT, 2, P])
        kv = sb("kv", [2, 256])
        state = sb("state", [4, 256])
        pt = sb("pt", [DEPTH, TT, PLE])
        p_hi = sb("p_hi", [2, SEQ], F32R)
        p_lo = sb("p_lo", [2, SEQ], F32R)
        ff_hi = sb("ff_hi", [512], F32R)
        ff_lo = sb("ff_lo", [512], F32R)
        zeros = sb("zeros", [512], F32R)
        rw = sb("rw", [KC, N_EXP])
        rw_hi = sb("rw_hi", [KC, N_EXP], F32R)
        rw_lo = sb("rw_lo", [KC, N_EXP], F32R)
        small = sb("small", [64])
        eps_t = sb("eps_t", [1])
        logit = sb("logit", [TT, N_EXP])
        chosen = sb("chosen", [TT, N_EXP])
        e_gate = sb("e_gate", [TT, 1 + 2 * N_EXP])
        slot_of = sb("slot_of", [TT, 1 + 2 * N_EXP])
        passes_t = sb("passes_t", [1], I32)
        pickT = sb("pickT", [SEQ], F32R)
        vrows = kx_half[:, :, :, :].rearrange("p t a n -> p (t a) n")[:, 0:DEPTH, :]
        lam_row = kv[:, :, :].rearrange("p l (a n) -> p l a n", a=4)
        qT = xn[:, 0, :].rearrange("p (j n) -> p j n", j=HEADS)
        kT = xn[:, 1, :].rearrange("p (j n) -> p j n", j=HEADS)
        on, osq = z[:, 0, C_DQ:C_DK], z[:, 1, C_DQ:C_DK]
        log_a, g_exp = (z[:, 0, i:i + 256].rearrange("p (t n) -> p t n", t=TT) for i in (0, 256))
        g_pre, g_abs = (z[:, 1, i:i + 256].rearrange("p (t n) -> p t n", t=TT) for i in (0, 256))
        silu_g, ff = z[:, 0, 0:512], z[:, 1, 0:512]
        g_row = z[:, 0, 512:512 + D]
        pick = z[:, 1, 512:768].rearrange("p (t n) -> p t n", t=TT)
        cmp_a, cmp_b = (z[:, 1, i:i + 128].rearrange("p (t n) -> p t n", t=TT) for i in (768, 896))
        up = probs[:, :, :].rearrange("p (t a) n -> p t (a n)", t=TT)
        gate = aT
        rot = state[:, :, :].rearrange("p i (t g n) -> p i t g n", t=TT, g=16)
        xe_hi, xe_lo = (a[:, 0:4, :].rearrange("p k (m n) -> p (k m) n", m=2) for a in (x_hi, x_lo))
        y_hi, y_lo = (a[:, 4:8, :].rearrange("p k n -> p (k n)") for a in (x_hi, x_lo))
        ps = ctx.enter_context(nc.psum_tensor("ps", [P, 8, 512], F32))

        def x_parts(q, k):
            if q in (2, 5):
                return x_hi[:, k, :], x_lo[:, k, :]
            if q in (0, 3):
                lower = (p_hi[:, :, :], p_lo[:, :, :], ff_hi[:, :].rearrange("p (k n) -> p k n", k=2),
                         ff_lo[:, :].rearrange("p (k n) -> p k n", k=2))[k // 2][:, k % 2, :]
            else:
                lower = (xb_lo0, xb_lo1)[k // 4][:, k % 4, :]
            return xb_hi[:, k, :], lower

        def xT(q, k):
            bank = k // 2 if q == 5 else 4 + k // 4 + 2 * (k % 4 // 2)
            return ps[:, bank, (k % 2) * SEQ:(k % 2 + 1) * SEQ]

        def h_half(q, half):
            return 2 * q - 1 + half

        ident = cst[:, K_ID:K_ID + P]
        sumsq, std, rstd = small[:, 0:2], small[:, 2:4], small[:, 4:6]
        neg_max, row_sum, row_inv = small[:, 8:16], small[:, 16:24], small[:, 24:32]
        o_ss, o_std, o_inv = small[:, 32:36], small[:, 36:40], small[:, 40:44]
        g_ss, g_std, g_inv = small[:, 44:52], small[:, 52:60], small[:, 8:16]
        top, gsum, count_max = small[:, 60:62], small[:, 62:64], small[:, 6:7]

        raw_landed = [sem(f"raw_landed{i}") for i in range(RING)]
        up_landed = [sem(f"up_landed{i}") for i in range(RING)]
        hi_ready, lo_ready, tile_used = sem("hi_ready"), sem("lo_ready"), sem("tile_used")
        x_landed, ident_landed, rest_landed, vec_landed = (
            sem("x_landed"), sem("ident_landed"), sem("rest_landed"), sem("vec_landed"))
        misc_landed, grow_landed, frow_landed = sem("misc_landed"), sem("grow_landed"), sem("frow_landed")
        dve_step, act_step = sem("dve_step"), sem("act_step")
        vecT_ready, vec_ready, setup_done = sem("vecT_ready"), sem("vec_ready"), sem("setup_done")
        sumsq_ready, std_ready, rstd_ready = sem("sumsq_ready"), sem("std_ready"), sem("rstd_ready")
        xnT_ready, xhi_ready, xlo_ready = sem("xnT_ready"), sem("xhi_ready"), sem("xlo_ready")
        h_updated = sem("h_updated")
        z_ready, u_ready, uT_ready, uT_copied = sem("z_ready"), sem("u_ready"), sem("uT_ready"), sem("uT_copied")
        tap_done, rope_done = sem("tap_done"), sem("rope_done")
        qkT_ready, qT_copied, kT_copied = sem("qkT_ready"), sem("qT_copied"), sem("kT_copied")
        mean_ready, yc_ready, ysq_ready, var_ready = sem("mean_ready"), sem("yc_ready"), sem("ysq_ready"), sem("var_ready")
        ystd_ready, yn_ready, y_ready = sem("ystd_ready"), sem("yn_ready"), sem("y_ready")
        scores_ready, neg_max_ready, exp_ready = sem("scores_ready"), sem("neg_max_ready"), sem("exp_ready")
        masked_ready, a_ready, aT_ready, aT_copied = sem("masked_ready"), sem("a_ready"), sem("aT_ready"), sem("aT_copied")
        o_ready, osq_ready, oss_ready, ostd_ready = sem("o_ready"), sem("osq_ready"), sem("oss_ready"), sem("ostd_ready")
        on_ready, onT_ready = sem("on_ready"), sem("onT_ready")
        gT_ready, gT_copied, gpre_ready, gbias_ready = sem("gT_ready"), sem("gT_copied"), sem("gpre_ready"), sem("gbias_ready")
        gln_ready, la_ready, rev_ready, gexp_ready = sem("gln_ready"), sem("la_ready"), sem("rev_ready"), sem("gexp_ready")
        kx_ready, kv_ready, kv_masked, state_ready = sem("kx_ready"), sem("kv_ready"), sem("kv_masked"), sem("state_ready")
        go_ready, gsq_ready, gss_ready, gstd_ready = sem("go_ready"), sem("gsq_ready"), sem("gss_ready"), sem("gstd_ready")
        gon_ready, gonT_ready = sem("gon_ready"), sem("gonT_ready")
        mixhi_ready, mixlo_ready = sem("mixhi_ready"), sem("mixlo_ready")
        pT_ready, phi_ready, plo_ready, up_ready, gate_ready = (
            sem("pT_ready"), sem("phi_ready"), sem("plo_ready"), sem("up_ready"), sem("gate_ready"))
        f_silu, f_act, f_T, f_hi, f_lo = sem("f_silu"), sem("f_act"), sem("f_T"), sem("f_hi"), sem("f_lo")
        logit_ready, rank_ready, lexp_ready, chosen_ready = sem("logit_ready"), sem("rank_ready"), sem("lexp_ready"), sem("chosen_ready")
        passes_ready, xg_ready, rw_hi_ready, rw_lo_ready = (
            sem("passes_ready"), sem("xg_ready"), sem("rw_hi_ready"), sem("rw_lo_ready"))
        m_pick, m_gathered, m_xhi, m_xlo = sem("m_pick"), sem("m_gathered"), sem("m_xhi"), sem("m_xlo")
        m_pickT, m_pickT_copied = sem("m_pickT"), sem("m_pickT_copied")
        m_silu, m_act, m_T, m_hi, m_lo = sem("m_silu"), sem("m_act"), sem("m_T"), sem("m_hi"), sem("m_lo")
        m_yhi, m_ylo, m_scattered, m_added = sem("m_yhi"), sem("m_ylo"), sem("m_scattered"), sem("m_added")
        out_landed, out_ready = sem("out_landed"), sem("out_ready")

        def nth(c, r):
            return c + 1 if r is None else r * RING + (c + 1)

        def load_tile(sp, c, r, dst_of, src):
            if c >= RING or r is not None:
                sp.wait_ge(lo_ready, nth(c - RING, r))
            sp.dma_start(dst_of(raw[:, c % RING, :]), src).then_inc(raw_landed[c % RING], 16)

        def split_hi(act, c, r=None):
            f = c - T_FFN
            if 0 <= f < 3 * N_FB - 1 and (f < 2 or (f - 2) % 3 != 2):
                if r is None:
                    act.wait_ge(up_landed[c % RING], 16 * (f // RING + 1))
                else:
                    act.wait_ge(up_landed[c % RING], r * 16 + 16 * (f // RING + 1))
            if r is None:
                act.wait_ge(raw_landed[c % RING], 16 * (c // RING + 1))
            else:
                act.wait_ge(raw_landed[c % RING], r * 16 + 16 * (c // RING + 1))
            if c >= SPLIT or r is not None:
                act.wait_ge(tile_used, nth(c - SPLIT, r))
            w = tile_width(c)
            nc.scalar.activation(w_hi[:, c % SPLIT, 0:w], raw[:, c % RING, 0:w], ACT.Copy).then_inc(hi_ready, 1)

        def split_lo(dve, c, r=None):
            dve.wait_ge(hi_ready, nth(c, r))
            w = tile_width(c)
            nc.vector.tensor_tensor(w_lo[:, c % SPLIT, 0:w], raw[:, c % RING, 0:w],
                                    w_hi[:, c % SPLIT, 0:w].bitcast(F32), ALU.subtract).then_inc(lo_ready, 1)

        def tile_width(c):
            last = any(c in (t + 10, t + 11) for t in T_IN)
            return 4 * (IN_BLOCKS[-1][1] - IN_BLOCKS[-1][0]) if last else TILE

        def products(acc, xh, xl, wh, wl, start, stop):
            nc.tensor.matmul(acc, xh, wh, start=start, stop=False)
            nc.tensor.matmul(acc, xh, wl, start=False, stop=False)
            return nc.tensor.matmul(acc, xl, wh, start=False, stop=stop)

        mix_part = lambda k: (x_hi[:, k, :], x_lo[:, k, :])
        MIX_PARTS = 6
        Z_DONE = [2, 3, 4, 5, 6, 8]
        halves = lambda t: t.rearrange("p (k n) -> p k n", k=4)
        doubles = lambda t: t.rearrange("p (k n) -> p k n", k=2)
        block = ctx.enter_context(nc.Block())

        @block.sync
        def _(sp):
            def rows(c, r, w, cols):
                n = cols[1] - cols[0]
                load_tile(sp, c, r, lambda t: t[:, 0:4 * n].rearrange("p (k n) -> p k n", k=4),
                          w[:, :, cols[0]:cols[1]])

            def in_proj(l):
                w = w_in[l].rearrange("(k p) n -> p k n", p=P)
                for b, cols in enumerate(IN_BLOCKS):
                    for half in range(2):
                        rows(T_IN[l] + 2 * b + half, None, w[:, 4 * half:4 * half + 4, :], cols)

            def square(first, r, w):
                w = w.rearrange("(k p) n -> p k n", p=P)
                for b in range(2):
                    for half in range(2):
                        rows(first + 2 * b + half, r, w[:, 4 * half:4 * half + 4, :], (512 * b, 512 * b + 512))

            def up_proj(l):
                load_tile(sp, T_UP[l], None, doubles, ple_w_up[l].rearrange("(k p) n -> p k n", p=P))

            f_gu = ffn_w_gu[0].rearrange("(k p) (s n) -> p k s n", p=P, s=2)
            f_down = ffn_w_down[0].rearrange("(k p) n -> p k n", p=P)

            def ffn_gu(c, r, b):
                for half in range(2):
                    load_tile(sp, c + half, r, lambda t: t.rearrange("p (k s n) -> p k s n", k=4, s=2)[:, :, 0, :],
                              f_gu[:, 4 * half:4 * half + 4, 0, bass.ds(b * FB, FB)])
                    dst = raw[:, (c + half) % RING, :].rearrange("p (k s n) -> p k s n", k=4, s=2)[:, :, 1, :]
                    sp.dma_start(dst, f_gu[:, 4 * half:4 * half + 4, 1, bass.ds(b * FB, FB)]
                                 ).then_inc(up_landed[(c + half) % RING], 16)

            def ffn_down(c, r, b):
                load_tile(sp, c, r, doubles, f_down[:, bass.ds(b * 2, 2), :])

            sp.dma_start(h[:, :, :], x[0].rearrange("(t p) n -> p t n", p=P)).then_inc(x_landed, 16)
            in_proj(0)
            square(T_OUT[0], None, w_out[0])
            ffn_gu(T_FFN, None, 0)
            with sp.Fori(0, (N_FB - 1) // 2) as i:
                for s in range(2):
                    ffn_gu(T_FFN + 2 + 3 * s, i, i * 2 + (1 + s))
                    ffn_down(T_FFN + 4 + 3 * s, i, i * 2 + s)
            c = T_UP[0] - 1
            load_tile(sp, c, None, lambda t: doubles(t)[:, 0, :], f_down[:, 2 * N_FB - 2, :])
            sp.dma_start(doubles(raw[:, c % RING, :])[:, 1, :], f_down[:, 2 * N_FB - 1, :]).then_inc(up_landed[c % RING], 16)
            up_proj(0)
            square(T_GATE[0], None, ple_w_gate[0])
            in_proj(1)
            square(T_OUT[1], None, w_out[1])
            up_proj(1)

            e_gu = moe_w_gu[0].rearrange("e (k p) n -> e p k n", p=P)
            e_down = moe_w_down[0].rearrange("e (k p) n -> e p k n", p=P)

            def expert_gu(c, r, e, b):
                for s in range(2):
                    for half in range(2):
                        load_tile(sp, c + 2 * s + half, r, halves,
                                  e_gu[bass.ds(e, 1), :, 4 * half:4 * half + 4, bass.ds(b * MB + s * D_FE, MB)]
                                  .rearrange("e p k n -> p (e k) n"))

            def expert_down(c, r, e, b):
                for half in range(2):
                    load_tile(sp, c + half, r, doubles,
                              e_down[bass.ds(e, 1), :, bass.ds(b * 4 + 2 * half, 2), :]
                              .rearrange("e p k n -> p (e k) n"))

            def experts(first):
                with sp.Fori(0, N_EXP) as e:
                    r0 = e * N_MB + first * N_MB
                    expert_gu(T_MOE, r0, e, 0)
                    with sp.Fori(1, N_MB) as b:
                        r = r0 + b - 1
                        expert_gu(T_MOE + 4, r, e, b)
                        expert_down(T_MOE + 8, r, e, b - 1)
                    expert_down(T_MOE + 4, r0 + (N_MB - 1), e, N_MB - 1)

            experts(0)
            sp.wait_ge(passes_ready, 1)
            passes = sp.value_load(passes_t[0:1, 0:1], min_val=1, max_val=2)
            with sp.If(passes > 1):
                experts(N_EXP)
            square(T_GATE[1], passes * (N_EXP * N_MB), ple_w_gate[1])

            for t in range(TT):
                sp.wait_ge(out_ready, t + 1)
                sp.dma_start(out[0, t * P:(t + 1) * P, :], xn[:, t, :]).then_inc(out_landed, 16)
            sp.wait_ge(out_landed, 16 * TT)

        N_VEC_DMAS = 10

        @block.gpsimd
        def _(pool):
            pool.dma_start(cst[:, P:], consts[:, P:]).then_inc(rest_landed, 16)
            for l in range(DEPTH):
                pool.dma_start(lam_row[:, l, :, :].rearrange("p a n -> p (a n)"),
                               diff_lambda[l:l + 1].rearrange("o a n -> o (a n)").broadcast_to([P, 4 * DH])
                               ).then_inc(misc_landed, 16)
                pool.dma_start(w_g2[0:RANK, l, :], gla_w_gate2[l]).then_inc(misc_landed, 16)
                pool.dma_start(b_gate[:, l, :], gla_b_gate[l:l + 1, :].broadcast_to([P, P])).then_inc(misc_landed, 16)
                pool.dma_start(pt[:, l, :, :], p[l, 0].rearrange("(t p) n -> p t n", p=P)).then_inc(misc_landed, 16)
            pool.dma_start(rw[:, :, :], router_w[0].rearrange("(k p) n -> p k n", p=P)).then_inc(misc_landed, 16)
            pool.wait_ge(mixlo_ready, 4 * DEPTH)
            pool.dma_start(g_row[:, :], norm_ffn_g[1:2, :].broadcast_to([P, D])).then_inc(grow_landed, 16)
            pool.wait_ge(xg_ready, 2)
            pool.dma_start(g_row[:, :], final_norm_g.rearrange("(a n) -> a n", a=1).broadcast_to([P, D])
                           ).then_inc(frow_landed, 16)

        N_MISC = 4 * DEPTH + 1

        @block.scalar
        def _(act):
            steps = [0]

            def link(ins):
                steps[0] += 1
                ins.then_inc(act_step, 1)
                act.wait_ge(act_step, steps[0])

            act.dma_start(ident, consts[:, 0:P]).then_inc(ident_landed, 16)
            for first, src in ((V_MIX, norm_mix_g), (V_FFN, norm_ffn_g), (V_PLE, ple_norm_g), (V_CB, conv_b),
                               (V_LG, conv_ln_g), (V_LB, conv_ln_b), (V_SUB, diff_subln_g)):
                n = src.shape[1] // P
                act.dma_start(vrows[first:first + n, :, :], src.rearrange("l (r n) -> r l n", n=P)).then_inc(vec_landed, 16)
            for half in range(2):
                act.dma_start(vrows[V_GLA:V_GLA + 1, :, half * GLA_DV:(half + 1) * GLA_DV],
                              gla_norm_g.rearrange("(a l) n -> a l n", a=1)).then_inc(vec_landed, 16)
            act.dma_start(vrows[V_TAP:V_TAP + 2 * TAPS, :, :],
                          conv_w.rearrange("l a (r n) -> (a r) l n", n=P)).then_inc(vec_landed, 16)

            def norm_stats(q):
                if 1 <= q <= 4 or q == 6:
                    act.wait_ge(h_updated, 10 if q == 6 else h_half(q, 1))
                for t in range(TT):
                    nc.scalar.activation(z[:, 1, C_DQ:C_DQ + D], h[:, t, :], ACT.Square,
                                         accum_out=sumsq[:, t:t + 1]).then_inc(sumsq_ready, 1)
                    act.wait_ge(sumsq_ready, 2 * q + t + 1)
                nc.scalar.activation(std, sumsq, ACT.Sqrt, bias=eps_t[:, 0:1], scale=1.0 / D).then_inc(std_ready, 1)

            def norm_hi(q, l, first, half):
                for k in range(4 * half, 4 * half + 4):
                    act.wait_ge(xnT_ready, 4 * q + k // 2 + 1)
                    nc.scalar.activation(x_parts(q, k)[0], xT(q, k), ACT.Copy,
                                         scale=vcol[:, l, first + k:first + k + 1]).then_inc(xhi_ready, 1)

            def in_proj(l):
                for b, (c0, c1) in enumerate(IN_BLOCKS):
                    c = T_IN[l] + 2 * b
                    split_hi(act, c + 3)
                    act.wait_ge(tile_used, c + 2)
                    s = 2 * (b % 2)
                    if b == 0:
                        act.wait_ge(rstd_ready, 3 * l + 1)
                    parts = ([(0, C_G, ACT.Copy), (C_G, c1, ACT.Sigmoid)] if b == 0 else
                             [(c0, C_GZ, ACT.Silu), (C_GZ, c1, ACT.Copy)] if c0 == C_GR else [(c0, c1, ACT.Copy)])
                    for p0, p1, func in parts:
                        for t in range(TT):
                            ins = nc.scalar.activation(z[:, t, p0:p1], ps[:, s + t, p0 - c0:p1 - c0], func,
                                                       scale=rstd[:, t:t + 1])
                        ins.then_inc(z_ready, 1)
                    split_hi(act, c + 4)
                    if b == 2:
                        act.wait_ge(uT_ready, l + 1)
                        nc.scalar.activation(uT[:, :, TAPS - 1:], ps[:, 4, :].rearrange("p (j n) -> p j n", j=2),
                                             ACT.Copy).then_inc(uT_copied, 1)

            def exps(l, t):
                act.wait_ge(neg_max_ready, TT * l + t + 1)
                for i in range(2 * HEADS):
                    nc.scalar.activation(probs[:, i, 0:P * (t + 1)], probs[:, i, 0:P * (t + 1)], ACT.Exp,
                                         bias=neg_max[:, i:i + 1], accum_out=row_sum[:, i:i + 1]).then_inc(exp_ready, 1)

            def probs_T(l, t):
                for kt in range(t + 1):
                    act.wait_ge(aT_ready, TT * l + t + 1)
                    nc.scalar.activation(aT[:, kt, :], ps[:, 4 + kt, :], ACT.Copy).then_inc(aT_copied, 1)

            def o_square(l, t):
                act.wait_ge(o_ready, TT * l + t + 1)
                nc.scalar.activation(osq[:, :], ps[:, 6, :], ACT.Square).then_inc(osq_ready, 1)

            def o_std_(l, t):
                act.wait_ge(oss_ready, TT * l + t + 1)
                nc.scalar.activation(o_std, o_ss, ACT.Sqrt, bias=eps_t[:, 0:1], scale=1.0 / DV).then_inc(ostd_ready, 1)

            def o_split(l, t):
                act.wait_ge(onT_ready, TT * l + t + 1)
                nc.scalar.activation(x_hi[:, 2:6, t * P:(t + 1) * P], ps[:, 4, :].rearrange("p (j n) -> p j n", j=4),
                                     ACT.Copy, scale=vcol[:, l, V_SUB:V_SUB + 1]).then_inc(mixhi_ready, 1)

            def mixer(l):
                for t in range(TT):
                    act.wait_ge(qkT_ready, 4 * l + t + 1)
                    nc.scalar.activation(qT[:, :, t * P:(t + 1) * P], ps[:, 4 + t, :].rearrange("p (j n) -> p j n", j=4),
                                         ACT.Copy).then_inc(qT_copied, 1)
                act.wait_ge(yc_ready, l + 1)
                nc.scalar.activation(ysq[:, :, :], yc[:, :, :], ACT.Square).then_inc(ysq_ready, 1)
                act.wait_ge(var_ready, l + 1)
                nc.scalar.activation(ysq[:, 0, :], ps[:, 7, SEQ:2 * SEQ], ACT.Sqrt, bias=eps_t[:, 0:1]).then_inc(ystd_ready, 1)
                if l == 0:
                    act.wait_ge(setup_done, 3)
                    nc.scalar.activation(lam_exp[:, :, :], lam_exp[:, :, :], ACT.Exp).then_inc(vec_ready, 1)
                act.wait_ge(gT_ready, l + 1)
                nc.scalar.activation(gqT[:, :], ps[:, 7, 0:SEQ], ACT.Copy, scale=GLA_DK ** -0.5).then_inc(gT_copied, 1)
                nc.scalar.activation(gzT[0:RANK, :], ps[0:RANK, 7, SEQ:2 * SEQ], ACT.Copy).then_inc(gT_copied, 1)
                exps(l, 0)
                act.wait_ge(yn_ready, l + 1)
                for j in range(2):
                    nc.scalar.activation(yc[:, j, :], yc[:, j, :], ACT.Silu, bias=vcol[:, l, V_LB + j:V_LB + j + 1],
                                         scale=vcol[:, l, V_LG + j:V_LG + j + 1]).then_inc(y_ready, 1)
                act.wait_ge(y_ready, 2 * l + 2)
                nc.scalar.activation(x_hi[:, 0:2, :], yc[:, :, :], ACT.Copy).then_inc(mixhi_ready, 1)
                act.wait_ge(gbias_ready, l + 1)
                link(nc.scalar.activation(g_abs[:, :, :], g_pre[:, :, :], ACT.Abs))
                link(nc.scalar.activation(g_abs[:, :, :], g_abs[:, :, :], ACT.Exp, scale=-1.0))
                nc.scalar.activation(g_abs[:, :, :], g_abs[:, :, :], ACT.Ln, bias=1.0).then_inc(gln_ready, 1)
                probs_T(l, 0)
                act.wait_ge(rev_ready, l + 1)
                nc.scalar.activation(g_exp[:, :, :], ps[:, 7, 0:SEQ].rearrange("p (t n) -> p t n", t=2), ACT.Exp,
                                     scale=1.0 / TAU).then_inc(gexp_ready, 1)
                nc.scalar.activation(decay[:, :], ps[:, 7, SEQ:SEQ + 4], ACT.Exp, scale=1.0 / TAU).then_inc(gexp_ready, 1)
                exps(l, 1)
                o_square(l, 0)
                o_std_(l, 0)
                o_split(l, 0)
                probs_T(l, 1)
                act.wait_ge(go_ready, l + 1)
                nc.scalar.activation(osq[:, :], ps[:, 7, :], ACT.Square).then_inc(gsq_ready, 1)
                act.wait_ge(gss_ready, l + 1)
                nc.scalar.activation(g_std, g_ss, ACT.Sqrt, bias=eps_t[:, 0:1], scale=1.0 / GLA_DV).then_inc(gstd_ready, 1)
                o_square(l, 1)
                o_std_(l, 1)
                act.wait_ge(gonT_ready, l + 1)
                nc.scalar.activation(x_hi[:, 6:8, :], ps[:, 7, :].rearrange("p (j n) -> p j n", j=2), ACT.Copy,
                                     scale=vcol[:, l, V_GLA:V_GLA + 1]).then_inc(mixhi_ready, 1)
                o_split(l, 1)
                act.wait_ge(pT_ready, l + 1)
                nc.scalar.activation(p_hi[:, :, :], ps[:, 5, :].rearrange("p (j n) -> p j n", j=2), ACT.Copy).then_inc(phi_ready, 1)

            def up_copy(l):
                act.wait_ge(tile_used, T_UP[l] + 1)
                nc.scalar.activation(up[:, :, :], ps[:, 0:4, :].rearrange("p (t m) n -> p t (m n)", t=2),
                                     ACT.Copy).then_inc(up_ready, 1)

            def ple_gate(l, r):
                for b in range(2):
                    c = T_GATE[l] + 2 * b
                    if l == 0:
                        split_hi(act, c + 3)
                    elif b == 0:
                        split_hi(act, c + 3, r)
                    act.wait_ge(tile_used, nth(c + 1, r))
                    if b == 0:
                        act.wait_ge(rstd_ready, 3 * l + 3)
                    else:
                        act.wait_ge(h_updated, 4 * l + 5)
                    for t in range(TT):
                        ins = nc.scalar.activation(gate[:, t, :], ps[:, 4 * l + 2 * b + t, :], ACT.Sigmoid,
                                                   scale=rstd[:, t:t + 1])
                    ins.then_inc(gate_ready, 1)
                    if l == 0:
                        if b == 1:
                            norm_hi(3, 1, V_MIX, 0)
                        split_hi(act, c + 4)

            act.wait_ge(vecT_ready, 1)
            nc.scalar.activation(vcol[:, :, :], ps[:, 0:2, 0:V_ROWS], ACT.Copy).then_inc(vec_ready, 1)
            act.wait_ge(vec_ready, 1)
            norm_hi(0, 0, V_MIX, 0)
            split_hi(act, 0)
            norm_hi(0, 0, V_MIX, 1)
            split_hi(act, 1)
            split_hi(act, 2)
            act.wait_ge(setup_done, 1)
            act.wait_ge(x_landed, 16)
            norm_stats(0)
            for l in range(DEPTH):
                if l:
                    norm_hi(3, 1, V_MIX, 1)
                    norm_stats(3)
                in_proj(l)
                mixer(l)
                for c in range(T_OUT[l], T_OUT[l] + 3):
                    split_hi(act, c + 3)
                norm_hi(3 * l + 1, l, V_FFN, 0)
                split_hi(act, T_OUT[l] + 6)
                norm_hi(3 * l + 1, l, V_FFN, 1)
                norm_stats(3 * l + 1)
                if l == 0:
                    def ffn_gate():
                        for t in range(TT):
                            ins = nc.scalar.activation(silu_g[:, t * FB:(t + 1) * FB], ps[:, t, 0:FB], ACT.Silu,
                                                       scale=rstd[:, t:t + 1])
                        ins.then_inc(f_silu, 1)

                    def ffn_T(b):
                        act.wait_ge(f_T, b + 1)
                        nc.scalar.activation(ff_hi[:, :], ps[:, 2, :], ACT.Copy).then_inc(f_hi, 1)

                    act.wait_ge(tile_used, T_FFN + 2)
                    act.wait_ge(rstd_ready, 2)
                    ffn_gate()
                    with act.Fori(0, (N_FB - 1) // 2) as i:
                        for s in range(2):
                            c = T_FFN + 2 + 3 * s
                            split_hi(act, c + 1, i)
                            split_hi(act, c + 2, i)
                            ffn_T(i * 2 + s)
                            split_hi(act, c + 3, i)
                            act.wait_ge(tile_used, nth(c + 1, i))
                            ffn_gate()
                    split_hi(act, T_UP[0])
                    split_hi(act, T_UP[0] + 1)
                    ffn_T(N_FB - 1)
                    split_hi(act, T_UP[0] + 2)
                    for half in range(2):
                        norm_hi(2, 0, V_PLE, half)
                    split_hi(act, T_UP[0] + 3)
                    norm_stats(2)
                    up_copy(0)
                    ple_gate(0, None)

            nc.scalar.activation(rw_hi[:, :, :], rw[:, :, :], ACT.Copy).then_inc(rw_hi_ready, 1)
            up_copy(1)
            split_hi(act, T_UP[1] + 3)
            act.wait_ge(chosen_ready, 1)
            nc.scalar.activation(e_gate[:, :, 1:1 + N_EXP], e_gate[:, :, 1:1 + N_EXP], ACT.Exp).then_inc(lexp_ready, 1)
            act.wait_ge(passes_ready, 1)
            passes = act.value_load(passes_t[0:1, 0:1], min_val=1, max_val=2)

            def expert_rows_hi(n):
                for half in range(2):
                    act.wait_ge(m_gathered, n * 2 + (half + 1))
                    nc.scalar.activation(xe_hi[:, 4 * half:4 * half + 4, :],
                                         ps[:, 6 + half, :].rearrange("p (k n) -> p k n", k=4), ACT.Copy).then_inc(m_xhi, 1)

            def expert_out_hi(r):
                act.wait_ge(tile_used, nth(T_MOE - 1, r))
                for half in range(2):
                    nc.scalar.activation(y_hi[:, 512 * half:512 * half + 512], ps[:, 4 + half, :],
                                         ACT.Copy).then_inc(m_yhi, 1)

            expert_rows_hi(0)
            with act.Fori(0, passes) as ps_i:
                with act.Fori(0, N_EXP) as e:
                    n = ps_i * N_EXP + e
                    r0 = n * N_MB

                    def gate_of(c, r):
                        act.wait_ge(tile_used, nth(c, r))
                        nc.scalar.activation(silu_g[:, :], ps[:, 0, :], ACT.Silu).then_inc(m_silu, 1)

                    def upper_T(m):
                        act.wait_ge(m_T, m)
                        nc.scalar.activation(ff_hi[:, :], ps[:, 2, :], ACT.Copy).then_inc(m_hi, 1)

                    expert_out_hi(r0)
                    split_hi(act, T_MOE + 3, r0)
                    gate_of(T_MOE + 1, r0)
                    split_hi(act, T_MOE + 4, r0)
                    split_hi(act, T_MOE + 5, r0)
                    with act.Fori(1, N_MB) as b:
                        r = r0 + b - 1
                        split_hi(act, T_MOE + 6, r)
                        upper_T(r0 + b)
                        split_hi(act, T_MOE + 7, r)
                        gate_of(T_MOE + 5, r)
                        for c in range(8, 12):
                            split_hi(act, T_MOE + c, r)
                    r1 = r0 + N_MB
                    upper_T(r1)
                    split_hi(act, T_MOE + 0, r1)
                    expert_rows_hi(n + 1)
                    act.wait_ge(m_pickT, n + 1)
                    nc.scalar.activation(pickT[:, :], ps[:, 3, 0:SEQ], ACT.Copy).then_inc(m_pickT_copied, 1)
                    split_hi(act, T_MOE + 1, r1)
                    split_hi(act, T_MOE + 2, r1)
            expert_out_hi(passes * (N_EXP * N_MB))
            for half in range(2):
                norm_hi(5, 1, V_PLE, half)
            act.wait_ge(m_added, passes * (2 * N_EXP) + 2)
            norm_stats(5)
            ple_gate(1, passes * (N_EXP * N_MB))
            norm_stats(6)

        @block.vector
        def _(dve):
            steps = [0]

            def link(ins):
                steps[0] += 1
                ins.then_inc(dve_step, 1)
                dve.wait_ge(dve_step, steps[0])

            def norm_rstd(q):
                dve.wait_ge(std_ready, q + 1)
                nc.vector.reciprocal(rstd, std).then_inc(rstd_ready, 1)

            def norm_lo(q, l, first, half):
                for k in range(4 * half, 4 * half + 4):
                    dve.wait_ge(xhi_ready, 8 * q + 2 * (k // 2) + 2)
                    hi, lo = x_parts(q, k)
                    nc.vector.scalar_tensor_tensor(
                        out=lo, in0=xT(q, k), scalar=vcol[:, l, first + k:first + k + 1], in1=hi.bitcast(F32),
                        op0=ALU.mult, op1=ALU.subtract).then_inc(xlo_ready, 1)

            def taps(l, first, last):
                for n in range(first, min(last, 2 * TAPS)):
                    tap, j = n // 2, n % 2
                    w = vcol[:, l, V_TAP + n:V_TAP + n + 1]
                    src = uT[:, j, tap:tap + SEQ]
                    if tap == 0:
                        ins = nc.vector.tensor_scalar(yc[:, j, :], src, w, vcol[:, l, V_CB + j:V_CB + j + 1],
                                                      ALU.mult, ALU.add)
                    else:
                        dve.wait_ge(tap_done, 2 * TAPS * l + n - 1)
                        ins = nc.vector.scalar_tensor_tensor(out=yc[:, j, :], in0=src, scalar=w, in1=yc[:, j, :],
                                                             op0=ALU.mult, op1=ALU.add)
                    ins.then_inc(tap_done, 1)

            def rope(l):
                dve.wait_ge(z_ready, 8 * l + Z_DONE[2])
                qk = z[:, :, C_DQ:C_DV].rearrange("p t (g d) -> p t g d", d=DH)
                x1, x2 = qk[:, :, :, 0:8], qk[:, :, :, 8:16]
                cos = cst[:, K_COS:K_COS + 16].rearrange("p (t o n) -> p t o n", t=2, o=1).broadcast_to([P, TT, 16, 8])
                sin = cst[:, K_SIN:K_SIN + 16].rearrange("p (t o n) -> p t o n", t=2, o=1).broadcast_to([P, TT, 16, 8])
                for i, (a, b) in enumerate(((x1, cos), (x2, sin), (x2, cos), (x1, sin))):
                    for t in range(TT):
                        ins = nc.vector.tensor_tensor(rot[:, i, t], a[:, t], b[:, t], ALU.mult)
                link(ins)
                for t in range(TT):
                    nc.vector.tensor_tensor(x1[:, t], rot[:, 0, t], rot[:, 1, t], ALU.subtract).then_inc(rope_done, 1)
                    nc.vector.tensor_tensor(x2[:, t], rot[:, 2, t], rot[:, 3, t], ALU.add).then_inc(rope_done, 1)

            def in_proj(l):
                n = 0
                for b in range(len(IN_BLOCKS)):
                    c = T_IN[l] + 2 * b
                    split_lo(dve, c + 3)
                    if b >= 3:
                        taps(l, n, n + 10)
                        n += 10
                    if b == 1:
                        dve.wait_ge(z_ready, 8 * l + Z_DONE[0])
                        nc.vector.tensor_tensor(z[:, :, 0:C_G], z[:, :, 0:C_G], z[:, :, C_G:2 * C_G],
                                                ALU.mult).then_inc(u_ready, 1)
                    split_lo(dve, c + 4)
                    if b == 3:
                        rope(l)
                    if b == 2:
                        dve.wait_ge(uT_copied, l + 1)
                    if b >= 2:
                        taps(l, n, n + 10)
                        n += 10
                    if b == 2 and l == 0:
                        lambda_dots()
                taps(l, n, 2 * TAPS)

            def mask_scores(l, t):
                dve.wait_ge(scores_ready, TT * l + t + 1)
                n = P * (t + 1)
                mask = cst[:, K_MASK + t * SEQ:K_MASK + t * SEQ + n].rearrange("p (o n) -> p o n", o=1).broadcast_to([P, HEADS, n])
                for c in range(2):
                    s = ps[:, 2 * c:2 * c + 2, :].rearrange("p b (i n) -> p (b i) n", i=2)[:, :, 0:n]
                    nc.vector.scalar_tensor_tensor(out=probs[:, HEADS * c:HEADS * c + HEADS, 0:n], in0=s,
                                                   scalar=DH ** -0.5, in1=mask, op0=ALU.mult,
                                                   op1=ALU.add).then_inc(masked_ready, 1)
                dve.wait_ge(masked_ready, 2 * TT * l + 2 * t + 2)
                nc.vector.tensor_reduce(neg_max, probs[:, :, 0:n], AX.X, ALU.max, negate=True).then_inc(neg_max_ready, 1)

            def differences(l, t):
                n = P * (t + 1)
                dve.wait_ge(exp_ready, 2 * HEADS * (TT * l + t + 1))
                link(nc.vector.reciprocal(row_inv, row_sum))
                link(nc.vector.tensor_scalar(row_inv[:, HEADS:], row_inv[:, HEADS:], neg_lam[:, l:l + 1], None, ALU.mult))
                for i in range(HEADS):
                    link(nc.vector.tensor_scalar(probs[:, HEADS + i, 0:n], probs[:, HEADS + i, 0:n],
                                                 row_inv[:, HEADS + i:HEADS + i + 1], None, ALU.mult))
                    nc.vector.scalar_tensor_tensor(out=probs[:, i, 0:n], in0=probs[:, i, 0:n], scalar=row_inv[:, i:i + 1],
                                                   in1=probs[:, HEADS + i, 0:n], op0=ALU.mult,
                                                   op1=ALU.add).then_inc(a_ready, 1)

            def o_sums(l, t):
                dve.wait_ge(osq_ready, TT * l + t + 1)
                nc.vector.tensor_reduce(o_ss, osq[:, :].rearrange("p (j n) -> p j n", j=HEADS), AX.X,
                                        ALU.add).then_inc(oss_ready, 1)

            def o_scale(l, t):
                dve.wait_ge(ostd_ready, TT * l + t + 1)
                link(nc.vector.reciprocal(o_inv, o_std))
                nc.vector.tensor_tensor(on[:, :].rearrange("p (j n) -> p j n", j=HEADS),
                                        ps[:, 6, :].rearrange("p (j n) -> p j n", j=HEADS),
                                        o_inv.rearrange("p (j o) -> p j o", o=1).broadcast_to([P, HEADS, DV]),
                                        ALU.mult).then_inc(on_ready, 1)

            def lower_mix(l, part, chunks, src, scale, cols=slice(0, SEQ)):
                dve.wait_ge(mixhi_ready, 4 * l + part + 1)
                hi = x_hi[:, chunks, cols].bitcast(F32)
                if scale is None:
                    ins = nc.vector.tensor_tensor(x_lo[:, chunks, cols], src, hi, ALU.subtract)
                else:
                    ins = nc.vector.scalar_tensor_tensor(out=x_lo[:, chunks, cols], in0=src, scalar=scale, in1=hi,
                                                         op0=ALU.mult, op1=ALU.subtract)
                ins.then_inc(mixlo_ready, 1)

            def mixer(l):
                for t in range(TT):
                    dve.wait_ge(qkT_ready, 4 * l + 2 + t + 1)
                    nc.vector.tensor_copy(kT[:, :, t * P:(t + 1) * P],
                                          ps[:, 6 + t, :].rearrange("p (j n) -> p j n", j=4)).then_inc(kT_copied, 1)
                dve.wait_ge(mean_ready, l + 1)
                both = lambda a: a.rearrange("p (o n) -> p o n", o=1).broadcast_to([P, 2, SEQ])
                nc.vector.tensor_tensor(yc[:, :, :], yc[:, :, :], both(ps[:, 7, 0:SEQ]), ALU.subtract).then_inc(yc_ready, 1)
                mask_scores(l, 0)
                dve.wait_ge(ystd_ready, l + 1)
                link(nc.vector.reciprocal(ysq[:, 1, :], ysq[:, 0, :]))
                nc.vector.tensor_tensor(yc[:, :, :], yc[:, :, :], both(ysq[:, 1, :]), ALU.mult).then_inc(yn_ready, 1)
                lower_mix(l, 0, slice(0, 2), yc[:, :, :], None)
                if l == 0:
                    lambdas()
                dve.wait_ge(gpre_ready, l + 1)
                nc.vector.tensor_tensor(g_pre[:, :, :], ps[:, 7, 0:SEQ].rearrange("p (t n) -> p t n", t=2),
                                        b_gate[:, l, :].rearrange("p (o n) -> p o n", o=1).broadcast_to([P, TT, P]),
                                        ALU.add).then_inc(gbias_ready, 1)
                differences(l, 0)
                dve.wait_ge(gln_ready, l + 1)
                nc.vector.scalar_tensor_tensor(out=log_a[:, :, :], in0=g_pre[:, :, :], scalar=0.0, in1=g_abs[:, :, :],
                                               op0=ALU.min, op1=ALU.subtract).then_inc(la_ready, 1)
                dve.wait_ge(aT_ready, TT * l + 1)
                mask_scores(l, 1)
                dve.wait_ge(gexp_ready, 2 * l + 2)
                link(nc.vector.tensor_tensor(z[:, :, C_GK:C_GV], z[:, :, C_GK:C_GV], g_exp[:, :, :], ALU.mult))
                for half in range(2):
                    nc.vector.tensor_scalar(kx_half[:, :, half, :], z[:, :, C_GK:C_GV], cst[:, K_HALF + half:K_HALF + half + 1],
                                            None, ALU.mult).then_inc(kx_ready, 1)
                o_sums(l, 0)
                o_scale(l, 0)
                for c in range(4):
                    if c % 2 == 0:
                        dve.wait_ge(kv_ready, 2 * l + c // 2 + 1)
                        nc.vector.tensor_tensor(
                            state[:, c:c + 2, :] if c == 0 else kv[:, :, :],
                            ps[:, 7, :].rearrange("p (j n) -> p j n", j=2),
                            cst[:, K_BD:K_BD + 256].rearrange("p (o n) -> p o n", o=1).broadcast_to([P, 2, 256]),
                            ALU.mult).then_inc(kv_masked, 1)
                        dve.wait_ge(kv_masked, 2 * l + c // 2 + 1)
                    if c:
                        nc.vector.scalar_tensor_tensor(
                            out=state[:, c, :], in0=state[:, c - 1, :], scalar=decay[:, c:c + 1],
                            in1=state[:, 1, :] if c == 1 else kv[:, c % 2, :], op0=ALU.mult,
                            op1=ALU.add).then_inc(state_ready, 1)
                        dve.wait_ge(state_ready, 3 * l + c)
                lower_mix(l, 1, slice(2, 6), ps[:, 4, :].rearrange("p (j n) -> p j n", j=4), vcol[:, l, V_SUB:V_SUB + 1],
                          slice(0, P))
                differences(l, 1)
                dve.wait_ge(gsq_ready, l + 1)
                heads = lambda a: a.rearrange("p (j n) -> p j n", n=GLA_DV)
                nc.vector.tensor_reduce(g_ss, heads(osq[:, :]), AX.X, ALU.add).then_inc(gss_ready, 1)
                dve.wait_ge(gstd_ready, l + 1)
                link(nc.vector.reciprocal(g_inv, g_std))
                link(nc.vector.tensor_tensor(heads(silu_g[:, :]), heads(ps[:, 7, :]),
                                             g_inv.rearrange("p (j o) -> p j o", o=1).broadcast_to([P, 8, GLA_DV]), ALU.mult))
                nc.vector.tensor_tensor(silu_g[:, :].rearrange("p (t n) -> p t n", t=2),
                                        silu_g[:, :].rearrange("p (t n) -> p t n", t=2), z[:, :, C_GR:C_GZ],
                                        ALU.mult).then_inc(gon_ready, 1)
                o_sums(l, 1)
                o_scale(l, 1)
                lower_mix(l, 2, slice(6, 8), ps[:, 7, :].rearrange("p (j n) -> p j n", j=2), vcol[:, l, V_GLA:V_GLA + 1])
                lower_mix(l, 3, slice(2, 6), ps[:, 4, :].rearrange("p (j n) -> p j n", j=4), vcol[:, l, V_SUB:V_SUB + 1],
                          slice(P, SEQ))
                dve.wait_ge(phi_ready, l + 1)
                nc.vector.tensor_tensor(p_lo[:, :, :], ps[:, 5, :].rearrange("p (j n) -> p j n", j=2),
                                        p_hi[:, :, :].bitcast(F32), ALU.subtract).then_inc(plo_ready, 1)

            def out_proj(l):
                for b in range(2):
                    c = T_OUT[l] + 2 * b
                    split_lo(dve, c + 3)
                    if b:
                        norm_lo(3 * l + 1, l, V_FFN, 0)
                    dve.wait_ge(tile_used, c + 2)
                    hb = h[:, :, 512 * b:512 * b + 512]
                    nc.vector.tensor_tensor(hb, hb, ps[:, 2 * b:2 * b + 2, :], ALU.add).then_inc(h_updated, 1)
                    if b:
                        norm_lo(3 * l + 1, l, V_FFN, 1)
                    split_lo(dve, c + 4)
                norm_rstd(3 * l + 1)

            def ple_add(l, r):
                for b in range(2):
                    c = T_GATE[l] + 2 * b
                    if l == 0 or b == 0:
                        split_lo(dve, c + 3, r)
                    dve.wait_ge(gate_ready, 2 * l + b + 1)
                    link(nc.vector.tensor_tensor(gate[:, :, :], gate[:, :, :], up[:, :, 512 * b:512 * b + 512], ALU.mult))
                    hb = h[:, :, 512 * b:512 * b + 512]
                    nc.vector.tensor_tensor(hb, hb, gate[:, :, :], ALU.add).then_inc(h_updated, 1)
                    if l == 0:
                        if b:
                            norm_lo(3, 1, V_MIX, 0)
                        split_lo(dve, c + 4)

            def lambda_dots():
                dve.wait_ge(misc_landed, 16 * N_MISC)
                for l in range(DEPTH):
                    link(nc.vector.tensor_tensor(lam_mul[:, l, :, :], lam_row[:, l, 0::2, :], lam_row[:, l, 1::2, :],
                                                 ALU.mult))
                    nc.vector.tensor_reduce(lam_exp[:, l, :], lam_mul[:, l, :, :], AX.X, ALU.add).then_inc(setup_done, 1)

            def lambdas():
                dve.wait_ge(vec_ready, 2)
                for l in range(DEPTH):
                    lam_init = 0.8 - 0.6 * math.exp(-0.3 * l)
                    link(nc.vector.scalar_tensor_tensor(out=neg_lam[:, l:l + 1], in0=lam_exp[:, l, 1:2], scalar=-lam_init,
                                                        in1=lam_exp[:, l, 0:1], op0=ALU.add, op1=ALU.subtract))
                    link(nc.vector.tensor_scalar(vcol[:, l, V_SUB:V_SUB + 1], vcol[:, l, V_SUB:V_SUB + 1],
                                                 1.0 - lam_init, None, ALU.mult))

            nc.vector.memset(eps_t[:, :], EPS).then_inc(setup_done, 1)
            link(nc.vector.memset(e_gate[:, :, :], 0.0))
            link(nc.vector.memset(slot_of[:, :, :], 0.0))
            link(nc.vector.memset(uT[:, :, :], 0.0))
            link(nc.vector.memset(zeros[:, :].bitcast(F32), 0.0))
            norm_lo(0, 0, V_MIX, 0)
            split_lo(dve, 0)
            norm_lo(0, 0, V_MIX, 1)
            split_lo(dve, 1)
            split_lo(dve, 2)
            norm_rstd(0)
            for l in range(DEPTH):
                if l:
                    norm_lo(3, 1, V_MIX, 1)
                    norm_rstd(3)
                in_proj(l)
                mixer(l)
                out_proj(l)
                if l == 0:
                    def ffn_mult(b):
                        dve.wait_ge(f_silu, b + 1)
                        for t in range(TT):
                            cols = slice(t * FB, (t + 1) * FB)
                            ins = nc.vector.scalar_tensor_tensor(out=ff[:, cols], in0=silu_g[:, cols], scalar=rstd[:, t:t + 1],
                                                                 in1=ps[:, t, FB:2 * FB], op0=ALU.mult, op1=ALU.mult)
                        ins.then_inc(f_act, 1)

                    def ffn_T(b):
                        dve.wait_ge(f_hi, b + 1)
                        nc.vector.tensor_tensor(ff_lo[:, :], ps[:, 2, :], ff_hi[:, :].bitcast(F32),
                                                ALU.subtract).then_inc(f_lo, 1)

                    dve.wait_ge(rstd_ready, 2)
                    ffn_mult(0)
                    with dve.Fori(0, (N_FB - 1) // 2) as i:
                        for s in range(2):
                            c = T_FFN + 2 + 3 * s
                            split_lo(dve, c + 1, i)
                            split_lo(dve, c + 2, i)
                            ffn_T(i * 2 + s)
                            split_lo(dve, c + 3, i)
                            ffn_mult(i * 2 + (1 + s))
                    split_lo(dve, T_UP[0])
                    split_lo(dve, T_UP[0] + 1)
                    ffn_T(N_FB - 1)
                    dve.wait_ge(tile_used, T_UP[0])
                    for b in range(2):
                        hb = h[:, :, 512 * b:512 * b + 512]
                        nc.vector.tensor_tensor(hb, hb, ps[:, 4 + b:8:2, :], ALU.add).then_inc(h_updated, 1)
                    split_lo(dve, T_UP[0] + 2)
                    for half in range(2):
                        norm_lo(2, 0, V_PLE, half)
                    split_lo(dve, T_UP[0] + 3)
                    norm_rstd(2)
                    ple_add(0, None)

            split_lo(dve, T_UP[1] + 3)
            dve.wait_ge(rw_hi_ready, 1)
            nc.vector.tensor_tensor(rw_lo[:, :, :], rw[:, :, :], rw_hi[:, :, :].bitcast(F32), ALU.subtract).then_inc(rw_lo_ready, 1)
            dve.wait_ge(rstd_ready, 5)
            dve.wait_ge(logit_ready, 1)
            for t in range(TT):
                link(nc.vector.tensor_scalar(logit[:, t, :], ps[:, 4, t * N_EXP:(t + 1) * N_EXP], rstd[:, t:t + 1], None,
                                             ALU.mult))
            for t in range(TT):
                own = logit[:, t, :].rearrange("p (e o) -> p e o", o=1).broadcast_to([P, N_EXP, N_EXP])
                other = logit[:, t, :].rearrange("p (o e) -> p o e", o=1).broadcast_to([P, N_EXP, N_EXP])
                sq = lambda a: a.rearrange("p (a b) -> p a b", a=N_EXP)
                link(nc.vector.tensor_tensor(sq(cmp_a[:, t, :]), own, other, ALU.is_lt))
                link(nc.vector.tensor_tensor(sq(cmp_b[:, t, :]), own, other, ALU.is_equal))
                link(nc.vector.tensor_tensor(cmp_b[:, t, :], cmp_b[:, t, :], cst[:, K_TIE:K_TIE + 64], ALU.mult))
                link(nc.vector.tensor_tensor(cmp_a[:, t, :], cmp_a[:, t, :], cmp_b[:, t, :], ALU.add))
                link(nc.vector.tensor_reduce(chosen[:, t, :], sq(cmp_a[:, t, :]), AX.X, ALU.add))
                link(nc.vector.tensor_reduce(top[:, t:t + 1], logit[:, t, :], AX.X, ALU.max))
                link(nc.vector.tensor_scalar(e_gate[:, t, 1:1 + N_EXP], logit[:, t, :], top[:, t:t + 1], None, ALU.subtract))
            nc.vector.tensor_scalar(chosen[:, :, :], chosen[:, :, :], 1.5, None, ALU.is_lt).then_inc(chosen_ready, 1)
            dve.wait_ge(chosen_ready, 1)
            dve.wait_ge(grow_landed, 16)
            for t in range(TT):
                nc.vector.scalar_tensor_tensor(out=xn[:, t, :], in0=h[:, t, :], scalar=rstd[:, t:t + 1], in1=g_row[:, :],
                                               op0=ALU.mult, op1=ALU.mult).then_inc(xg_ready, 1)
            dve.wait_ge(lexp_ready, 1)
            eg = e_gate[:, :, 1:1 + N_EXP]
            link(nc.vector.tensor_tensor(eg, eg, chosen[:, :, :], ALU.mult))
            link(nc.vector.tensor_reduce(gsum, eg, AX.X, ALU.add))
            link(nc.vector.reciprocal(gsum, gsum))
            for t in range(TT):
                link(nc.vector.tensor_scalar(e_gate[:, t, 1 + N_EXP:], eg[:, t, :], gsum[:, t:t + 1], None, ALU.mult))
                link(nc.vector.tensor_copy(eg[:, t, :], e_gate[:, t, 1 + N_EXP:]))
            dve.wait_ge(rank_ready, 1)
            for t in range(TT):
                link(nc.vector.scalar_tensor_tensor(out=slot_of[:, t, 0:N_EXP], in0=ps[:, 5, t * N_EXP:(t + 1) * N_EXP],
                                                    scalar=1.0, in1=chosen[:, t, :], op0=ALU.add, op1=ALU.mult))
                link(nc.vector.tensor_scalar(slot_of[:, t, N_EXP:2 * N_EXP], slot_of[:, t, 0:N_EXP], -1.0 - P, None, ALU.add))
                link(nc.vector.tensor_scalar(slot_of[:, t, 0:N_EXP], slot_of[:, t, 0:N_EXP], -1.0, None, ALU.add))
            link(nc.vector.tensor_reduce(count_max, ps[:, 5, 2 * N_EXP:3 * N_EXP], AX.X, ALU.max))
            nc.vector.tensor_scalar(passes_t[:, :], count_max, P + 0.5, 1.0, ALU.is_gt, ALU.add).then_inc(passes_ready, 1)
            dve.wait_ge(passes_ready, 1)
            nc.vector.memset(pickT[:, :].bitcast(F32), 0.0).then_inc(m_pickT_copied, 1)
            for free in (m_act, m_lo):
                dve.sem_inc(free, 1)

            def picks(n):
                for t in range(TT):
                    nc.vector.tensor_scalar(pick[:, t, :], cst[:, K_IOTA:K_IOTA + P], slot_of[:, t, bass.ds(n, 1)], None,
                                            ALU.is_equal).then_inc(m_pick, 1)

            def expert_rows_lo(n):
                for half in range(2):
                    dve.wait_ge(m_xhi, n * 2 + (half + 1))
                    nc.vector.tensor_tensor(xe_lo[:, 4 * half:4 * half + 4, :],
                                            ps[:, 6 + half, :].rearrange("p (k n) -> p k n", k=4),
                                            xe_hi[:, 4 * half:4 * half + 4, :].bitcast(F32),
                                            ALU.subtract).then_inc(m_xlo, 1)

            def expert_out_lo(n):
                for half in range(2):
                    dve.wait_ge(m_yhi, n * 2 + (half + 1))
                    cols = slice(512 * half, 512 * half + 512)
                    nc.vector.tensor_tensor(y_lo[:, cols], ps[:, 4 + half, :], y_hi[:, cols].bitcast(F32),
                                            ALU.subtract).then_inc(m_ylo, 1)

            def add_rows(n):
                for t, bank in ((1, 4), (0, 6)):
                    dve.wait_ge(m_scattered, n * 2 + (2 - t))
                    nc.vector.scalar_tensor_tensor(
                        out=h[:, t, :], in0=ps[:, bank:bank + 2, :].rearrange("p b n -> p (b n)"),
                        scalar=e_gate[:, t, bass.ds(n, 1)], in1=h[:, t, :], op0=ALU.mult,
                        op1=ALU.add).then_inc(m_added, 1)

            picks(0)
            passes = dve.value_load(passes_t[0:1, 0:1], min_val=1, max_val=2)
            expert_rows_lo(0)
            with dve.Fori(0, passes) as ps_i:
                with dve.Fori(0, N_EXP) as e:
                    n = ps_i * N_EXP + e
                    r0 = n * N_MB

                    def mult(m, c, r):
                        dve.wait_ge(tile_used, nth(c, r))
                        dve.wait_ge(m_silu, m)
                        nc.vector.tensor_tensor(ff[:, :], silu_g[:, :], ps[:, 1, :], ALU.mult).then_inc(m_act, 1)

                    def lower_T(m):
                        dve.wait_ge(m_hi, m)
                        nc.vector.tensor_tensor(ff_lo[:, :], ps[:, 2, :], ff_hi[:, :].bitcast(F32),
                                                ALU.subtract).then_inc(m_lo, 1)

                    expert_out_lo(n)
                    for c in range(3, 6):
                        split_lo(dve, T_MOE + c, r0)
                    mult(r0 + 1, T_MOE + 3, r0)
                    add_rows(n)
                    dve.wait_ge(m_pickT, n + 1)
                    picks(n + 1)
                    with dve.Fori(1, N_MB) as b:
                        r = r0 + b - 1
                        split_lo(dve, T_MOE + 6, r)
                        lower_T(r0 + b)
                        for c in range(7, 11):
                            split_lo(dve, T_MOE + c, r)
                        mult(r0 + b + 1, T_MOE + 7, r)
                        split_lo(dve, T_MOE + 11, r)
                    r1 = r0 + N_MB
                    lower_T(r1)
                    split_lo(dve, T_MOE + 0, r1)
                    expert_rows_lo(n + 1)
                    split_lo(dve, T_MOE + 1, r1)
                    split_lo(dve, T_MOE + 2, r1)
            expert_out_lo(passes * N_EXP)
            add_rows(passes * N_EXP)
            for half in range(2):
                norm_lo(5, 1, V_PLE, half)
            norm_rstd(5)
            ple_add(1, passes * (N_EXP * N_MB))
            norm_rstd(6)
            dve.wait_ge(frow_landed, 16)
            dve.wait_ge(rstd_ready, 7)
            for t in range(TT):
                nc.vector.scalar_tensor_tensor(out=xn[:, t, :], in0=h[:, t, :], scalar=rstd[:, t:t + 1],
                                               in1=g_row[:, :], op0=ALU.mult, op1=ALU.mult).then_inc(out_ready, 1)

        @block.tensor
        def _(pe):
            def transpose(dst, src, n=P):
                return nc.tensor.transpose(dst, src, ident[0:n, 0:n])

            def norm_T(q, half):
                if 1 <= q <= 4:
                    pe.wait_ge(h_updated, h_half(q, half))
                for k in range(4 * half, 4 * half + 4):
                    for t in range(TT):
                        ins = transpose(xT(q, k)[:, t * P:(t + 1) * P], h[:, t, k * P:(k + 1) * P])
                    if k % 2:
                        ins.then_inc(xnT_ready, 1)

            def x_ready(q, half):
                pe.wait_ge(xlo_ready, 8 * q + 4 * (half + 1))

            def tile(c, r=None):
                pe.wait_ge(lo_ready, nth(c, r))
                return w_hi[:, c % SPLIT, :], w_lo[:, c % SPLIT, :]

            def columns(c, r, bank, width, half, x_of):
                wh, wl = tile(c, r)
                wh, wl = (w[:, 0:4 * width].rearrange("p (k n) -> p k n", k=4) for w in (wh, wl))
                for kk in range(4):
                    k = 4 * half + kk
                    for t in range(TT):
                        xh, xl = (a[:, t * P:(t + 1) * P] for a in x_of(k))
                        ins = products(ps[:, bank + t, 0:width], xh, xl, wh[:, kk, :], wl[:, kk, :],
                                       k == 0, k == KC - 1)
                ins.then_inc(tile_used, 1)

            def rows_tile(c, r, bank, xh, xl, start, stop, between=None):
                wh, wl = tile(c, r)
                wh, wl = (w.rearrange("p (k m n) -> p k m n", k=2, m=2) for w in (wh, wl))
                for k in range(2):
                    for t in range(TT):
                        for m in range(2):
                            ins = products(ps[:, bank + 2 * t + m, :], xh[:, k, t * P:(t + 1) * P],
                                           xl[:, k, t * P:(t + 1) * P], wh[:, k, m, :], wl[:, k, m, :],
                                           start and k == 0, stop and k == 1)
                    if between and k == 0:
                        between()
                ins.then_inc(tile_used, 1)

            def in_proj(l):
                q = 3 * l
                x_ready(q, 0)
                for b, (c0, c1) in enumerate(IN_BLOCKS):
                    if b >= 2:
                        pe.wait_ge(z_ready, 8 * l + Z_DONE[b - 2])
                    for half in range(2):
                        columns(T_IN[l] + 2 * b + half, None, 2 * (b % 2), c1 - c0, half, lambda k: x_parts(q, k))
                        if b == 0 and half == 0:
                            if l:
                                norm_T(3, 1)
                            x_ready(q, 1)
                    if b == 2:
                        pe.wait_ge(u_ready, l + 1)
                        for j in range(2):
                            for t in range(TT):
                                ins = transpose(ps[:, 4, j * SEQ + t * P:j * SEQ + (t + 1) * P],
                                                z[:, t, j * P:(j + 1) * P])
                        ins.then_inc(uT_ready, 1)

            def scores(l, t):
                if t:
                    pe.wait_ge(masked_ready, 2 * TT * l + 2)
                else:
                    pe.wait_ge(z_ready, 8 * l + 8)
                    pe.wait_ge(qT_copied, 2 * l + 2)
                    pe.wait_ge(kT_copied, 2 * l + 2)
                n = P * (t + 1)
                for c in range(2):
                    for i in range(HEADS):
                        ins = nc.tensor.matmul(ps[:, 2 * c + i // 2, (i % 2) * SEQ:(i % 2) * SEQ + n],
                                               qT[c * DH:(c + 1) * DH, i, t * P:(t + 1) * P],
                                               kT[c * DH:(c + 1) * DH, i, 0:n], start=True, stop=True)
                ins.then_inc(scores_ready, 1)

            def probs_T(l, t):
                pe.wait_ge(a_ready, HEADS * (TT * l + t + 1))
                for kt in range(t + 1):
                    for i in range(HEADS):
                        ins = transpose(ps[:, 4 + kt, i * P:(i + 1) * P], probs[:, i, kt * P:(kt + 1) * P])
                ins.then_inc(aT_ready, 1)

            def values(l, t):
                pe.wait_ge(aT_copied, 3 * l + (1 if t == 0 else 3))
                if t:
                    pe.wait_ge(on_ready, TT * l + 1)
                for i in range(HEADS):
                    for kt in range(t + 1):
                        ins = nc.tensor.matmul(ps[:, 6, i * DV:(i + 1) * DV], aT[:, kt, i * P:(i + 1) * P],
                                               z[:, kt, C_DV + i * DV:C_DV + (i + 1) * DV],
                                               start=kt == 0, stop=kt == t)
                ins.then_inc(o_ready, 1)

            def o_T(l, t):
                pe.wait_ge(on_ready, TT * l + t + 1)
                for i in range(HEADS):
                    ins = transpose(ps[:, 4, i * P:(i + 1) * P], on[:, i * DV:(i + 1) * DV])
                ins.then_inc(onT_ready, 1)

            def mixer(l):
                pe.wait_ge(rope_done, 4 * (l + 1))
                pe.wait_ge(uT_copied, l + 1)
                for s, c0 in enumerate((C_DQ, C_DK)):
                    for t in range(TT):
                        for i in range(HEADS):
                            ins = transpose(ps[:, 4 + 2 * s + t, i * P:(i + 1) * P], z[:, t, c0 + i * P:c0 + (i + 1) * P])
                        ins.then_inc(qkT_ready, 1)
                pe.wait_ge(tap_done, 2 * TAPS * (l + 1))
                pe.wait_ge(kT_copied, 2 * l + 2)
                for j in range(2):
                    ins = nc.tensor.matmul(ps[:, 7, 0:SEQ], cst[:, K_MEAN:K_MEAN + P], yc[:, j, :], start=j == 0, stop=j == 1)
                ins.then_inc(mean_ready, 1)
                scores(l, 0)
                pe.wait_ge(ysq_ready, l + 1)
                for j in range(2):
                    ins = nc.tensor.matmul(ps[:, 7, SEQ:2 * SEQ], cst[:, K_MEAN:K_MEAN + P], ysq[:, j, :], start=j == 0, stop=j == 1)
                ins.then_inc(var_ready, 1)
                pe.wait_ge(ystd_ready, l + 1)
                for t in range(TT):
                    transpose(ps[:, 7, t * P:(t + 1) * P], z[:, t, C_GQ:C_GK])
                for t in range(TT):
                    ins = transpose(ps[0:RANK, 7, SEQ + t * P:SEQ + (t + 1) * P], z[:, t, C_GZ:D_IN])
                ins.then_inc(gT_ready, 1)
                pe.wait_ge(gT_copied, 2 * l + 2)
                for t in range(TT):
                    ins = nc.tensor.matmul(ps[:, 7, t * P:(t + 1) * P], gzT[0:RANK, t * P:(t + 1) * P], w_g2[0:RANK, l, :],
                                           start=True, stop=True)
                ins.then_inc(gpre_ready, 1)
                scores(l, 1)
                probs_T(l, 0)
                pe.wait_ge(la_ready, l + 1)
                for t in range(TT):
                    nc.tensor.matmul(ps[:, 7, t * P:(t + 1) * P], cst[:, K_REV:K_REV + P], log_a[:, t, :], start=True, stop=True)
                for t in range(TT):
                    ins = nc.tensor.matmul(ps[:, 7, SEQ + 2 * t:SEQ + 2 * t + 2], log_a[:, t, :], cst[:, K_HALF:K_HALF + 2],
                                           start=True, stop=True)
                ins.then_inc(rev_ready, 1)
                values(l, 0)
                for t in range(TT):
                    pe.wait_ge(kx_ready, 2 * l + 2)
                    if t:
                        pe.wait_ge(kv_masked, 2 * l + 1)
                    for half in range(2):
                        ins = nc.tensor.matmul(ps[:, 7, half * 256:half * 256 + 256], kx_half[:, t, half, :],
                                               z[:, t, C_GV:C_GR], start=True, stop=True)
                    ins.then_inc(kv_ready, 1)
                    if t == 0:
                        o_T(l, 0)
                pe.wait_ge(state_ready, 3 * (l + 1))
                for t in range(TT):
                    for half in range(2):
                        ins = nc.tensor.matmul(ps[half * CHUNK:(half + 1) * CHUNK, 7, t * 256:t * 256 + 256],
                                               gqT[:, t * P + half * CHUNK:t * P + (half + 1) * CHUNK],
                                               state[:, 2 * t + half, :], start=True, stop=True)
                ins.then_inc(go_ready, 1)
                pe.wait_ge(mixlo_ready, 4 * l + 2)
                probs_T(l, 1)
                values(l, 1)
                pe.wait_ge(gon_ready, l + 1)
                for j in range(2):
                    for t in range(TT):
                        ins = transpose(ps[:, 7, j * SEQ + t * P:j * SEQ + (t + 1) * P],
                                        silu_g[:, t * 256 + j * P:t * 256 + (j + 1) * P])
                ins.then_inc(gonT_ready, 1)
                o_T(l, 1)
                for j in range(2):
                    for t in range(TT):
                        ins = transpose(ps[:, 5, j * SEQ + t * P:j * SEQ + (t + 1) * P], pt[:, l, t, j * P:(j + 1) * P])
                ins.then_inc(pT_ready, 1)

            def square(first, r, x_of, bank=0, next_norm=None):
                for b in range(2):
                    for half in range(2):
                        columns(first + 2 * b + half, r, bank + 2 * b, 512, half, x_of)
                        if b == 1 and half == 0 and next_norm is not None:
                            norm_T(next_norm, 0)

            def up_proj(l, between=None):
                rows_tile(T_UP[l], None, 0, p_hi, p_lo, True, True, between)

            pe.wait_ge(ident_landed, 16)
            pe.wait_ge(x_landed, 16)
            for half in range(2):
                norm_T(0, half)
            pe.wait_ge(vec_landed, 16 * N_VEC_DMAS)
            for l in range(DEPTH):
                ins = transpose(ps[:, l, 0:V_ROWS], vrows[0:V_ROWS, l, :], V_ROWS)
            ins.then_inc(vecT_ready, 1)
            pe.wait_ge(vec_ready, 1)
            pe.wait_ge(rest_landed, 16)
            for l in range(DEPTH):
                in_proj(l)
                if l == 0:
                    pe.wait_ge(misc_landed, 16 * N_MISC)
                mixer(l)
                pe.wait_ge(mixlo_ready, 4 * (l + 1))
                pe.wait_ge(plo_ready, l + 1)
                square(T_OUT[l], None, mix_part, 0, 3 * l + 1)
                if l == 0:
                    def gate_up(c, r):
                        for half in range(2):
                            columns(c + half, r, 0, 512, half, lambda k: x_parts(1, k))
                            if r is None and half == 0:
                                norm_T(1, 1)
                                x_ready(1, 1)

                    def ffn_T(b):
                        pe.wait_ge(f_act, b + 1)
                        for k in range(2):
                            for t in range(TT):
                                ins = transpose(ps[:, 2, k * SEQ + t * P:k * SEQ + (t + 1) * P],
                                                ff[:, t * FB + k * P:t * FB + (k + 1) * P])
                        ins.then_inc(f_T, 1)

                    def down(c, r, b, stop):
                        pe.wait_ge(f_lo, b + 1)
                        rows_tile(c, r, 4, ff_hi[:, :].rearrange("p (k n) -> p k n", k=2),
                                  ff_lo[:, :].rearrange("p (k n) -> p k n", k=2), False, stop)

                    x_ready(1, 0)
                    gate_up(T_FFN, None)
                    for b in range(4):
                        nc.tensor.matmul(ps[:, 4 + b, :], x_hi[:, 0, 0:P], zeros[:, :], start=True, stop=False)
                    ffn_T(0)
                    with pe.Fori(0, (N_FB - 1) // 2) as i:
                        for s in range(2):
                            b = i * 2 + (1 + s)
                            gate_up(T_FFN + 2 + 3 * s, i)
                            down(T_FFN + 4 + 3 * s, i, b - 1, False)
                            ffn_T(b)
                    down(T_UP[0] - 1, None, N_FB - 1, True)
                    def norm_2_T():
                        pe.wait_ge(h_updated, h_half(2, 1))
                        for half in range(2):
                            norm_T(2, half)

                    up_proj(0, norm_2_T)
                    for half in range(2):
                        x_ready(2, half)
                    pe.wait_ge(up_ready, 1)
                    square(T_GATE[0], None, lambda k: x_parts(2, k), 0, 3)
            norm_T(4, 1)
            up_proj(1)
            x_ready(4, 1)
            pe.wait_ge(rw_lo_ready, 1)
            for t in range(TT):
                n = 0
                for k in range(KC):
                    for a in x_parts(4, k):
                        for w in (rw_hi, rw_lo):
                            ins = nc.tensor.matmul(ps[:, 4, t * N_EXP:(t + 1) * N_EXP], a[:, t * P:(t + 1) * P],
                                                   w[:, k, :], start=n == 0, stop=n == 4 * KC - 1)
                            n += 1
            ins.then_inc(logit_ready, 1)
            pe.wait_ge(chosen_ready, 1)
            nc.tensor.matmul(ps[:, 5, 0:N_EXP], cst[:, K_RANK:K_RANK + P], chosen[:, 0, :], start=True, stop=True)
            nc.tensor.matmul(ps[:, 5, N_EXP:2 * N_EXP], cst[:, K_ONES:K_ONES + P], chosen[:, 0, :], start=True, stop=False)
            nc.tensor.matmul(ps[:, 5, N_EXP:2 * N_EXP], cst[:, K_RANK:K_RANK + P], chosen[:, 1, :], start=False, stop=True)
            nc.tensor.matmul(ps[:, 5, 2 * N_EXP:3 * N_EXP], cst[:, K_ONES:K_ONES + P], chosen[:, 0, :], start=True, stop=False)
            nc.tensor.matmul(ps[:, 5, 2 * N_EXP:3 * N_EXP], cst[:, K_ONES:K_ONES + P], chosen[:, 1, :], start=False,
                             stop=True).then_inc(rank_ready, 1)
            pe.wait_ge(xg_ready, 2)
            pe.wait_ge(passes_ready, 1)
            passes = pe.value_load(passes_t[0:1, 0:1], min_val=1, max_val=2)

            def gather(n):
                pe.wait_ge(m_pick, n * 2 + 2)
                for k in range(KC):
                    for t in range(TT):
                        ins = nc.tensor.matmul(ps[:, 6 + k // 4, (k % 4) * P:(k % 4 + 1) * P],
                                               xn[:, t, k * P:(k + 1) * P], pick[:, t, :], start=t == 0, stop=t == 1)
                    if k % 4 == 3:
                        ins.then_inc(m_gathered, 1)

            def scatter(n):
                pe.wait_ge(m_pickT_copied, n + 1)
                pe.wait_ge(m_ylo, n * 2 + 2)
                for t, bank in ((1, 4), (0, 6)):
                    for m in range(2):
                        cols = slice(512 * m, 512 * m + 512)
                        nc.tensor.matmul(ps[:, bank + m, :], pickT[:, t * P:(t + 1) * P], y_hi[:, cols],
                                         start=True, stop=False)
                        ins = nc.tensor.matmul(ps[:, bank + m, :], pickT[:, t * P:(t + 1) * P], y_lo[:, cols],
                                               start=False, stop=True)
                    ins.then_inc(m_scattered, 1)

            gather(0)
            with pe.Fori(0, passes) as ps_i:
                with pe.Fori(0, N_EXP) as e:
                    n = ps_i * N_EXP + e
                    r0 = n * N_MB

                    def gate_up(c, r, m):
                        pe.wait_ge(m_act, m + 1)
                        for s in range(2):
                            for half in range(2):
                                wh, wl = tile(c + 2 * s + half, r)
                                wh, wl = (w.rearrange("p (k n) -> p k n", k=4) for w in (wh, wl))
                                for kk in range(4):
                                    k = 4 * half + kk
                                    ins = products(ps[:, s, :], xe_hi[:, k, :], xe_lo[:, k, :], wh[:, kk, :], wl[:, kk, :],
                                                   k == 0, k == KC - 1)
                                ins.then_inc(tile_used, 1)

                    def act_T(m):
                        pe.wait_ge(m_act, m + 2)
                        pe.wait_ge(m_lo, m + 1)
                        for k in range(4):
                            ins = transpose(ps[:, 2, k * P:(k + 1) * P], ff[:, k * P:(k + 1) * P])
                        ins.then_inc(m_T, 1)

                    def down(c, r, m, stop):
                        pe.wait_ge(m_lo, m + 2)
                        for half in range(2):
                            wh, wl = tile(c + half, r)
                            wh, wl = (w.rearrange("p (k m n) -> p k m n", k=2, m=2) for w in (wh, wl))
                            for kk in range(2):
                                k = 2 * half + kk
                                for s in range(2):
                                    ins = products(ps[:, 4 + s, :], ff_hi[:, k * P:(k + 1) * P], ff_lo[:, k * P:(k + 1) * P],
                                                   wh[:, kk, s, :], wl[:, kk, s, :], False, stop and k == 3)
                            ins.then_inc(tile_used, 1)

                    pe.wait_ge(m_xlo, n * 2 + 2)
                    gate_up(T_MOE, r0, r0)
                    scatter(n)
                    for t in range(TT):
                        ins = transpose(ps[:, 3, t * P:(t + 1) * P], pick[:, t, :])
                    ins.then_inc(m_pickT, 1)
                    act_T(r0)
                    pe.wait_ge(m_added, n * 2 + 1)
                    for m in range(2):
                        nc.tensor.matmul(ps[:, 4 + m, :], xe_hi[:, 0, :], zeros[:, :], start=True, stop=False)
                    with pe.Fori(1, N_MB) as b:
                        r = r0 + b - 1
                        gate_up(T_MOE + 4, r, r0 + b)
                        down(T_MOE + 8, r, r, False)
                        act_T(r0 + b)
                    pe.wait_ge(m_added, n * 2 + 2)
                    gather(n + 1)
                    down(T_MOE + 4, r0 + (N_MB - 1), r0 + (N_MB - 1), True)
            scatter(passes * N_EXP)
            for t in (1, 0):
                pe.wait_ge(m_added, passes * (2 * N_EXP) + (2 - t))
                for k in range(KC):
                    ins = transpose(xT(5, k)[:, t * P:(t + 1) * P], h[:, t, k * P:(k + 1) * P])
                    if t == 0 and k % 2:
                        ins.then_inc(xnT_ready, 1)
            for half in range(2):
                x_ready(5, half)
            square(T_GATE[1], passes * (N_EXP * N_MB), lambda k: x_parts(5, k), 4)


_INS = ["x", "p", "norm_mix_g", "w_in", "conv_w", "conv_b", "conv_ln_g", "conv_ln_b", "diff_lambda", "diff_subln_g",
        "gla_w_gate2", "gla_b_gate", "gla_norm_g", "w_out", "norm_ffn_g", "ffn_w_gu", "ffn_w_down", "router_w",
        "moe_w_gu", "moe_w_down", "ple_w_up", "ple_w_gate", "ple_norm_g", "final_norm_g"]


def kernel(**inputs):
    import concourse.bacc as bacc
    from concourse.bass_utils import run_bass_kernel_spmd

    nc = bacc.Bacc("TRN2", target_bir_lowering=False, num_devices=1)
    arrays, args = {}, []
    for name in _INS:
        arrays[name + "_d"] = np.ascontiguousarray(inputs[name])
    arrays["consts_d"] = constants()
    for name, a in arrays.items():
        args.append(nc.dram_tensor(name, a.shape, mybir.dt.from_np(a.dtype), kind="ExternalInput").ap())
    args.append(nc.dram_tensor("out_d", (1, SEQ, D), F32, kind="ExternalOutput").ap())
    build(nc, *args)
    r = run_bass_kernel_spmd(nc, [arrays], core_ids=[0])
    return r.results[0]["out_d"]
```

```python
import math
from contextlib import ExitStack

import numpy as np

import concourse.bass as bass
from concourse import mybir

P = 128
F32 = mybir.dt.float32
F32R = mybir.dt.float32r
I32 = mybir.dt.int32
ALU = mybir.AluOpType
ACT = mybir.ActivationFunctionType
AX = mybir.AxisListType

D = 1024
SEQ = 256
DEPTH = 2
TT = SEQ // P
KC = D // P
CHUNK = 64
CONV_CH = 256
TAPS = 31
HEADS = 4
DH = 64
DV = 128
GLA_HEADS = 4
GLA_DK = 32
GLA_DV = 64
RANK = 16
TAU = 16.0
ROT = 16
D_FF = 2816
N_EXP = 8
D_FE = 3584
PLE = 256
EPS = 1e-6

C_A, C_G, C_DQ, C_DK, C_DV = 0, 256, 512, 1024, 1536
C_GQ, C_GK, C_GV, C_GR, C_GZ = 2048, 2176, 2304, 2560, 2816
D_IN = 2832
IN_BLOCKS = [(C_A, C_DQ), (C_DQ, C_DK), (C_DK, C_DV), (C_GR, D_IN), (C_DV, C_GQ), (C_GQ, C_GR)]
B_RZ = 3

RING = 6
SPLIT = 3
TILE = 2048

V_MIX, V_FFN, V_PLE, V_CB, V_LG, V_LB, V_SUB, V_GLA, V_TAP = 0, 8, 16, 24, 26, 28, 30, 31, 32
V_ROWS = V_TAP + 2 * TAPS

FB = 256
N_FB = D_FF // FB
MB = 512
N_MB = D_FE // MB
T_IN = [0, 54]
T_OUT = [12, 66]
T_FFN = 16
T_UP = [49, 70]
T_GATE = [50, 71]
T_MOE = 71
E_TILES = 6 * N_MB
assert T_FFN + 3 * N_FB == T_UP[0] and E_TILES % RING == 0

K_ID, K_IOTA, K_RANK, K_REV, K_ONES, K_MEAN = (P * i for i in range(6))
K_MASK = 6 * P
K_BD = K_MASK + P
K_COS = K_BD + 256
K_SIN = K_COS + TT * 8
K_HALF = K_SIN + TT * 8
K_TIE = K_HALF + 2
K_FOLD = K_TIE + 64
K_END = K_FOLD + 8


def constants():
    c = np.zeros((P, K_END), np.float32)
    i = np.arange(P)
    c[:, K_ID:K_ID + P] = np.eye(P)
    c[:, K_IOTA:K_IOTA + P] = i[None, :]
    c[:, K_RANK:K_RANK + P] = i[:, None] < i[None, :]
    c[:, K_REV:K_REV + P] = (i[:, None] > i[None, :]) & (i[:, None] // CHUNK == i[None, :] // CHUNK)
    c[:, K_ONES:K_ONES + P] = 1.0
    c[:, K_MEAN:K_MEAN + P] = 1.0 / CONV_CH
    c[:, K_MASK:K_MASK + P] = np.where(i < CHUNK, -1e30, 0.0)[None, :]
    c[:, K_BD:K_BD + 256] = i[:, None] // GLA_DK == np.arange(256)[None, :] // GLA_DV
    freq = np.float32(500000.0) ** (-np.arange(0, ROT, 2, dtype=np.float32) / np.float32(ROT))
    ang = np.arange(SEQ, dtype=np.float32)[:, None] * freq[None, :].astype(np.float32)
    for t in range(TT):
        c[:, K_COS + 8 * t:K_COS + 8 * t + 8] = np.cos(ang[t * P:(t + 1) * P])
        c[:, K_SIN + 8 * t:K_SIN + 8 * t + 8] = np.sin(ang[t * P:(t + 1) * P])
    c[:, K_HALF] = i < CHUNK
    c[:, K_HALF + 1] = i >= CHUNK
    e = np.arange(N_EXP)
    c[:, K_TIE:K_TIE + 64] = (e[None, :] < e[:, None]).reshape(1, 64)
    c[:, K_FOLD:K_FOLD + 8] = i[:, None] % N_EXP == e[None, :]
    return c


def build(nc, x, p, norm_mix_g, w_in, conv_w, conv_b, conv_ln_g, conv_ln_b, diff_lambda, diff_subln_g,
          gla_w_gate2, gla_b_gate, gla_norm_g, w_out, norm_ffn_g, ffn_w_gu, ffn_w_down, router_w,
          moe_w_gu, moe_w_down, ple_w_up, ple_w_gate, ple_norm_g, final_norm_g, consts, out):
    with ExitStack() as ctx:
        def sb(name, shape, dt=F32):
            return ctx.enter_context(nc.sbuf_tensor(name, [P] + shape, dt))

        def sem(name):
            return ctx.enter_context(nc.semaphore(name))

        raw = sb("raw", [RING, TILE])
        w_hi = sb("w_hi", [SPLIT, TILE], F32R)
        w_lo = sb("w_lo", [SPLIT, TILE], F32R)
        cst = sb("cst", [K_END])
        h = sb("h", [TT, D])
        with nc.sbuf_tensor("xb_hi", [P, KC, SEQ], F32R) as xb_hi:
            pass
        xn = sb("xn", [TT, D])
        x_hi = sb("x_hi", [KC, SEQ], F32R)
        x_lo = sb("x_lo", [KC, SEQ], F32R)
        with (nc.sbuf_tensor("z_front", [P, C_DV], F32), nc.sbuf_tensor("xb_lo0", [P, 4, SEQ], F32R) as xb_lo0,
              nc.sbuf_tensor("z_mid", [P, D_IN - 4 * SEQ], F32), nc.sbuf_tensor("xb_lo1", [P, 4, SEQ], F32R) as xb_lo1):
            pass
        z = sb("z", [TT, D_IN])
        uT = sb("uT", [2, TAPS - 1 + SEQ])
        yc = sb("yc", [2, SEQ])
        ysq = sb("ysq", [2, SEQ])
        probs = sb("probs", [2 * HEADS, SEQ])
        aT = sb("aT", [TT, HEADS * P])
        vcol = sb("vcol", [DEPTH, V_ROWS])
        lam_mul = sb("lam_mul", [DEPTH, 2, DH])
        lam_exp = sb("lam_exp", [DEPTH, 2])
        neg_lam = sb("neg_lam", [DEPTH])
        neg_max = sb("neg_max", [TT, 2 * HEADS])
        row_sum = sb("row_sum", [TT, 2 * HEADS])
        factor = sb("factor", [TT, HEADS])
        o_eps = sb("o_eps", [TT, HEADS])
        w_g2 = sb("w_g2", [DEPTH, P])
        b_gate = sb("b_gate", [DEPTH, P])
        gqT = sb("gqT", [SEQ])
        gzT = sb("gzT", [SEQ])
        decay = sb("decay", [4])
        kx_half = sb("kx_half", [TT, 2, P])
        kv = sb("kv", [2, 256])
        state = sb("state", [4, 256])
        pt = sb("pt", [DEPTH, TT, PLE])
        p_hi = sb("p_hi", [2, SEQ], F32R)
        p_lo = sb("p_lo", [2, SEQ], F32R)
        ff_hi = sb("ff_hi", [512], F32R)
        ff_lo = sb("ff_lo", [512], F32R)
        zeros = sb("zeros", [512], F32R)
        rw = sb("rw", [KC, N_EXP])
        rw_parts = sb("rw_parts", [KC, 2 * N_EXP], F32R)
        small = sb("small", [64])
        eps_t = sb("eps_t", [1])
        logit = sb("logit", [TT, N_EXP])
        chosen = sb("chosen", [TT, N_EXP])
        e_gate = sb("e_gate", [TT, 1 + 2 * N_EXP])
        slot_of = sb("slot_of", [TT, 1 + 2 * N_EXP])
        passes_t = sb("passes_t", [1], I32)
        pickT = sb("pickT", [SEQ], F32R)
        vrows = kx_half[:, :, :, :].rearrange("p t a n -> p (t a) n")[:, 0:DEPTH, :]
        lam_row = kv[:, :, :].rearrange("p l (a n) -> p l a n", a=4)
        qT = xn[:, 0, :].rearrange("p (j n) -> p j n", j=HEADS)
        kT = xn[:, 1, :].rearrange("p (j n) -> p j n", j=HEADS)
        on, osq = z[:, 0, C_DQ:C_DK], z[:, 1, C_DQ:C_DK]
        log_a, g_exp = (z[:, 0, i:i + 256].rearrange("p (t n) -> p t n", t=TT) for i in (0, 256))
        g_pre, g_abs = (z[:, 1, i:i + 256].rearrange("p (t n) -> p t n", t=TT) for i in (0, 256))
        silu_g, ff = z[:, 0, 0:512], z[:, 1, 0:512]
        g_row = z[:, 0, 512:512 + D]
        pick = z[:, 1, 512:768].rearrange("p (t n) -> p t n", t=TT)
        cmp_a, cmp_b = (z[:, 1, i:i + 128].rearrange("p (t n) -> p t n", t=TT) for i in (768, 896))
        up = probs[:, :, :].rearrange("p (t a) n -> p t (a n)", t=TT)
        gate = aT
        rot = state[:, :, :].rearrange("p i (t g n) -> p i t g n", t=TT, g=16)
        xe_hi, xe_lo = (a[:, 0:4, :].rearrange("p k (m n) -> p (k m) n", m=2) for a in (x_hi, x_lo))
        y_hi, y_lo = (a[:, 4:8, :].rearrange("p k n -> p (k n)") for a in (x_hi, x_lo))
        ps = ctx.enter_context(nc.psum_tensor("ps", [P, 8, 512], F32))

        def x_parts(q, k):
            if q in (0, 3, 5):
                return x_hi[:, k, :], x_lo[:, k, :]
            return xb_hi[:, k, :], (xb_lo0, xb_lo1)[k // 4][:, k % 4, :]

        def xT(q, k):
            bank = k // 2 + (0 if q in (3, 5) else 4)
            return ps[:, bank, (k % 2) * SEQ:(k % 2 + 1) * SEQ]

        def h_half(q, half):
            return 2 * q - 1 + half

        ident = cst[:, K_ID:K_ID + P]
        sumsq, std, rstd = small[:, 0:2], small[:, 2:4], small[:, 4:6]
        o_ss, o_std, o_inv = small[:, 32:36], small[:, 36:40], small[:, 40:44]
        g_ss, g_std, g_inv = small[:, 44:52], small[:, 52:60], small[:, 8:16]
        half_sq, rest_sq, part_ms = small[:, 32:34], small[:, 34:36], small[:, 36:38]
        top, gsum, count_max = small[:, 60:62], small[:, 62:64], small[:, 6:7]

        raw_landed = [sem(f"raw_landed{i}") for i in range(RING)]
        up_landed = [sem(f"up_landed{i}") for i in range(RING)]
        hi_ready, lo_ready, tile_used = sem("hi_ready"), sem("lo_ready"), sem("tile_used")
        x_landed, ident_landed, rest_landed, vec_landed = (
            sem("x_landed"), sem("ident_landed"), sem("rest_landed"), sem("vec_landed"))
        misc_landed, grow_landed, frow_landed = sem("misc_landed"), sem("grow_landed"), sem("frow_landed")
        dve_step, act_step = sem("dve_step"), sem("act_step")
        vecT_ready, vec_ready, setup_done = sem("vecT_ready"), sem("vec_ready"), sem("setup_done")
        gain_landed, gainT_ready, gain_ready = sem("gain_landed"), sem("gainT_ready"), sem("gain_ready")
        sumsq_ready, std_ready, rstd_ready = sem("sumsq_ready"), sem("std_ready"), sem("rstd_ready")
        xnT_ready, xhi_ready, xlo_ready = sem("xnT_ready"), sem("xhi_ready"), sem("xlo_ready")
        h_updated = sem("h_updated")
        z_ready, u_ready, uT_ready, uT_copied = sem("z_ready"), sem("u_ready"), sem("uT_ready"), sem("uT_copied")
        tap_done, rope_done = sem("tap_done"), sem("rope_done")
        qkT_ready, qT_copied, kT_copied = sem("qkT_ready"), sem("qT_copied"), sem("kT_copied")
        mean_ready, yc_ready, ysq_ready, var_ready = sem("mean_ready"), sem("yc_ready"), sem("ysq_ready"), sem("var_ready")
        ystd_ready, yn_ready, y_ready = sem("ystd_ready"), sem("yn_ready"), sem("y_ready")
        scores_ready, neg_max_ready, exp_ready = sem("scores_ready"), sem("neg_max_ready"), sem("exp_ready")
        a_ready, aT_ready, aT_copied = sem("a_ready"), sem("aT_ready"), sem("aT_copied")
        o_ready, osq_ready, oss_ready, ostd_ready = sem("o_ready"), sem("osq_ready"), sem("oss_ready"), sem("ostd_ready")
        on_ready, onT_ready = sem("on_ready"), sem("onT_ready")
        gzT_ready, gzT_copied, gqT_ready, gqT_copied = sem("gzT_ready"), sem("gzT_copied"), sem("gqT_ready"), sem("gqT_copied")
        gpre_ready, gbias_ready = sem("gpre_ready"), sem("gbias_ready")
        gln_ready, la_ready, rev_ready, gexp_ready = sem("gln_ready"), sem("la_ready"), sem("rev_ready"), sem("gexp_ready")
        kx_ready, kv_ready, kv_masked, state_ready = sem("kx_ready"), sem("kv_ready"), sem("kv_masked"), sem("state_ready")
        go_ready, gsq_ready, gss_ready, gstd_ready = sem("go_ready"), sem("gsq_ready"), sem("gss_ready"), sem("gstd_ready")
        gon_ready, gonT_ready = sem("gon_ready"), sem("gonT_ready")
        mixhi_ready, mixlo_ready = sem("mixhi_ready"), sem("mixlo_ready")
        pT_ready, phi_ready, plo_ready, up_ready, gate_ready = (
            sem("pT_ready"), sem("phi_ready"), sem("plo_ready"), sem("up_ready"), sem("gate_ready"))
        f_silu, f_act, f_T, f_hi, f_lo = sem("f_silu"), sem("f_act"), sem("f_T"), sem("f_hi"), sem("f_lo")
        logitT_ready, logitT_copied = sem("logitT_ready"), sem("logitT_copied")
        logit_ready, rank_ready, lexp_ready, chosen_ready = sem("logit_ready"), sem("rank_ready"), sem("lexp_ready"), sem("chosen_ready")
        passes_ready, xg_ready, rw_hi_ready, rw_lo_ready = (
            sem("passes_ready"), sem("xg_ready"), sem("rw_hi_ready"), sem("rw_lo_ready"))
        m_pick, m_gathered, m_xhi, m_xlo = sem("m_pick"), sem("m_gathered"), sem("m_xhi"), sem("m_xlo")
        m_pickT, m_pickT_copied = sem("m_pickT"), sem("m_pickT_copied")
        m_silu, m_act, m_T, m_hi, m_lo = sem("m_silu"), sem("m_act"), sem("m_T"), sem("m_hi"), sem("m_lo")
        m_yhi, m_ylo, m_scattered, m_added = sem("m_yhi"), sem("m_ylo"), sem("m_scattered"), sem("m_added")
        part_ready = sem("part_ready")
        out_landed, out_ready = sem("out_landed"), sem("out_ready")

        def nth(c, r):
            return c + 1 if r is None else r * RING + (c + 1)

        def load_tile(sp, c, r, dst_of, src):
            if c >= RING or r is not None:
                sp.wait_ge(lo_ready, nth(c - RING, r))
            sp.dma_start(dst_of(raw[:, c % RING, :]), src).then_inc(raw_landed[c % RING], 16)

        def split_hi(act, c, r=None):
            f = c - T_FFN
            if 0 <= f < 3 * N_FB - 1 and (f < 2 or (f - 2) % 3 != 2):
                if r is None:
                    act.wait_ge(up_landed[c % RING], 16 * (f // RING + 1))
                else:
                    act.wait_ge(up_landed[c % RING], r * 16 + 16 * (f // RING + 1))
            if r is None:
                act.wait_ge(raw_landed[c % RING], 16 * (c // RING + 1))
            else:
                act.wait_ge(raw_landed[c % RING], r * 16 + 16 * (c // RING + 1))
            if c >= SPLIT or r is not None:
                act.wait_ge(tile_used, nth(c - SPLIT, r))
            w = tile_width(c)
            nc.scalar.activation(w_hi[:, c % SPLIT, 0:w], raw[:, c % RING, 0:w], ACT.Copy).then_inc(hi_ready, 1)

        def split_lo(dve, c, r=None):
            dve.wait_ge(hi_ready, nth(c, r))
            w = tile_width(c)
            nc.vector.tensor_tensor(w_lo[:, c % SPLIT, 0:w], raw[:, c % RING, 0:w],
                                    w_hi[:, c % SPLIT, 0:w].bitcast(F32), ALU.subtract).then_inc(lo_ready, 1)

        def tile_width(c):
            narrow = any(c in (t + 2 * B_RZ, t + 2 * B_RZ + 1) for t in T_IN)
            return 4 * (D_IN - C_GR) if narrow else TILE

        def products(acc, xh, xl, wh, wl, start, stop):
            nc.tensor.matmul(acc, xh, wh, start=start, stop=False)
            nc.tensor.matmul(acc, xh, wl, start=False, stop=False)
            return nc.tensor.matmul(acc, xl, wh, start=False, stop=stop)

        Z_DONE = [2, 3, 4, 6, 7, 8]
        halves = lambda t: t.rearrange("p (k n) -> p k n", k=4)
        doubles = lambda t: t.rearrange("p (k n) -> p k n", k=2)
        MIX_TILES = ((0, 1), (1, 1), (0, 0), (1, 0))
        O_BANK, OT_BANK = (4, 6), (3, 4)

        def score(t, c, i):
            if t == 0:
                return ps[:, 6 + c, i * P:(i + 1) * P]
            return ps[:, (0, 6)[c] + i // 2, (i % 2) * SEQ:(i % 2 + 1) * SEQ]

        block = ctx.enter_context(nc.Block())

        N_VEC_DMAS = 9
        @block.sync
        def _(sp):
            def rows(c, r, w, cols):
                n = cols[1] - cols[0]
                load_tile(sp, c, r, lambda t: t[:, 0:4 * n].rearrange("p (k n) -> p k n", k=4),
                          w[:, :, cols[0]:cols[1]])

            def in_proj(l):
                w = w_in[l].rearrange("(k p) n -> p k n", p=P)
                for b, cols in enumerate(IN_BLOCKS):
                    for half in range(2):
                        rows(T_IN[l] + 2 * b + half, None, w[:, 4 * half:4 * half + 4, :], cols)

            def square(first, r, w, tiles=((0, 0), (0, 1), (1, 0), (1, 1))):
                w = w.rearrange("(k p) n -> p k n", p=P)
                for i, (b, half) in enumerate(tiles):
                    rows(first + i, r, w[:, 4 * half:4 * half + 4, :], (512 * b, 512 * b + 512))

            def up_proj(l):
                load_tile(sp, T_UP[l], None, doubles, ple_w_up[l].rearrange("(k p) n -> p k n", p=P))

            f_gu = ffn_w_gu[0].rearrange("(k p) (s n) -> p k s n", p=P, s=2)
            f_down = ffn_w_down[0].rearrange("(k p) n -> p k n", p=P)

            def ffn_gu(c, r, b):
                for half in range(2):
                    load_tile(sp, c + half, r, lambda t: t.rearrange("p (k s n) -> p k s n", k=4, s=2)[:, :, 0, :],
                              f_gu[:, 4 * half:4 * half + 4, 0, bass.ds(b * FB, FB)])
                    dst = raw[:, (c + half) % RING, :].rearrange("p (k s n) -> p k s n", k=4, s=2)[:, :, 1, :]
                    sp.dma_start(dst, f_gu[:, 4 * half:4 * half + 4, 1, bass.ds(b * FB, FB)]
                                 ).then_inc(up_landed[(c + half) % RING], 16)

            def ffn_down(c, r, b):
                load_tile(sp, c, r, doubles, f_down[:, bass.ds(b * 2, 2), :])

            assert V_MIX == 0
            sp.dma_start(vrows[0:KC, :, :], norm_mix_g.rearrange("l (r n) -> r l n", n=P)).then_inc(gain_landed, 16)
            sp.dma_start(h[:, :, :], x[0].rearrange("(t p) n -> p t n", p=P)).then_inc(x_landed, 16)
            in_proj(0)
            square(T_OUT[0], None, w_out[0], MIX_TILES)
            ffn_gu(T_FFN, None, 0)
            with sp.Fori(0, (N_FB - 1) // 2) as i:
                for s in range(2):
                    ffn_gu(T_FFN + 2 + 3 * s, i, i * 2 + (1 + s))
                    ffn_down(T_FFN + 4 + 3 * s, i, i * 2 + s)
            c = T_UP[0] - 1
            load_tile(sp, c, None, lambda t: doubles(t)[:, 0, :], f_down[:, 2 * N_FB - 2, :])
            sp.dma_start(doubles(raw[:, c % RING, :])[:, 1, :], f_down[:, 2 * N_FB - 1, :]).then_inc(up_landed[c % RING], 16)
            up_proj(0)
            square(T_GATE[0], None, ple_w_gate[0])
            in_proj(1)
            square(T_OUT[1], None, w_out[1], MIX_TILES)
            up_proj(1)

            e_gu = moe_w_gu[0].rearrange("e (k p) n -> e p k n", p=P)
            e_down = moe_w_down[0].rearrange("e (k p) n -> e p k n", p=P)

            def expert_gu(c, r, e, b):
                for s in range(2):
                    for half in range(2):
                        load_tile(sp, c + 2 * s + half, r, halves,
                                  e_gu[bass.ds(e, 1), :, 4 * half:4 * half + 4, bass.ds(b * MB + s * D_FE, MB)]
                                  .rearrange("e p k n -> p (e k) n"))

            def expert_down(c, r, e, b):
                for half in range(2):
                    load_tile(sp, c + half, r, doubles,
                              e_down[bass.ds(e, 1), :, bass.ds(b * 4 + 2 * half, 2), :]
                              .rearrange("e p k n -> p (e k) n"))

            def experts(first):
                with sp.Fori(0, N_EXP) as e:
                    r0 = e * N_MB + first * N_MB
                    expert_gu(T_MOE, r0, e, 0)
                    with sp.Fori(1, N_MB) as b:
                        r = r0 + b - 1
                        expert_gu(T_MOE + 4, r, e, b)
                        expert_down(T_MOE + 8, r, e, b - 1)
                    expert_down(T_MOE + 4, r0 + (N_MB - 1), e, N_MB - 1)

            experts(0)
            sp.wait_ge(passes_ready, 1)
            passes = sp.value_load(passes_t[0:1, 0:1], min_val=1, max_val=2)
            with sp.If(passes > 1):
                experts(N_EXP)
            square(T_GATE[1], passes * (N_EXP * N_MB), ple_w_gate[1])

            for t in range(TT):
                sp.wait_ge(out_ready, t + 1)
                sp.dma_start(out[0, t * P:(t + 1) * P, :], xn[:, t, :]).then_inc(out_landed, 16)
            sp.wait_ge(out_landed, 16 * TT)

        @block.gpsimd
        def _(pool):
            pool.wait_ge(x_landed, 16)
            pool.dma_start(cst[:, P:], consts[:, P:]).then_inc(rest_landed, 16)
            for first, src in ((V_FFN, norm_ffn_g), (V_PLE, ple_norm_g), (V_CB, conv_b),
                               (V_LG, conv_ln_g), (V_LB, conv_ln_b), (V_SUB, diff_subln_g)):
                n = src.shape[1] // P
                pool.dma_start(vrows[first:first + n, :, :], src.rearrange("l (r n) -> r l n", n=P)).then_inc(vec_landed, 16)
            for half in range(2):
                pool.dma_start(vrows[V_GLA:V_GLA + 1, :, half * GLA_DV:(half + 1) * GLA_DV],
                               gla_norm_g.rearrange("(a l) n -> a l n", a=1)).then_inc(vec_landed, 16)
            pool.dma_start(vrows[V_TAP:V_TAP + 2 * TAPS, :, :],
                           conv_w.rearrange("l a (r n) -> (a r) l n", n=P)).then_inc(vec_landed, 16)
            for l in range(DEPTH):
                pool.dma_start(lam_row[:, l, :, :].rearrange("p a n -> p (a n)"),
                               diff_lambda[l:l + 1].rearrange("o a n -> o (a n)").broadcast_to([P, 4 * DH])
                               ).then_inc(misc_landed, 16)
                pool.dma_start(w_g2[0:RANK, l, :], gla_w_gate2[l]).then_inc(misc_landed, 16)
                pool.dma_start(b_gate[:, l, :], gla_b_gate[l:l + 1, :].broadcast_to([P, P])).then_inc(misc_landed, 16)
                pool.dma_start(pt[:, l, :, :], p[l, 0].rearrange("(t p) n -> p t n", p=P)).then_inc(misc_landed, 16)
            pool.dma_start(rw[:, :, :], router_w[0].rearrange("(k p) n -> p k n", p=P)).then_inc(misc_landed, 16)
            pool.wait_ge(mixlo_ready, 4 * DEPTH)
            pool.dma_start(g_row[:, :], norm_ffn_g[1:2, :].broadcast_to([P, D])).then_inc(grow_landed, 16)
            pool.wait_ge(xg_ready, 2)
            pool.dma_start(g_row[:, :], final_norm_g.rearrange("(a n) -> a n", a=1).broadcast_to([P, D])
                           ).then_inc(frow_landed, 16)

        N_MISC = 4 * DEPTH + 1

        @block.scalar
        def _(act):
            steps = [0]

            def link(ins):
                steps[0] += 1
                ins.then_inc(act_step, 1)
                act.wait_ge(act_step, steps[0])

            act.dma_start(ident, consts[:, 0:P]).then_inc(ident_landed, 16)

            def norm_stats(q):
                if 1 <= q <= 4:
                    act.wait_ge(h_updated, h_half(q, 1))
                for t in range(TT):
                    nc.scalar.activation(z[:, 1, C_DQ:C_DQ + D], h[:, t, :], ACT.Square,
                                         accum_out=sumsq[:, t:t + 1]).then_inc(sumsq_ready, 1)
                    act.wait_ge(sumsq_ready, 2 * q + t + 1)
                nc.scalar.activation(std, sumsq, ACT.Sqrt, bias=eps_t[:, 0:1], scale=1.0 / D).then_inc(std_ready, 1)

            def norm_hi(q, l, first, half):
                for k in range(4 * half, 4 * half + 4):
                    act.wait_ge(xnT_ready, 4 * q + k // 2 + 1)
                    nc.scalar.activation(x_parts(q, k)[0], xT(q, k), ACT.Copy,
                                         scale=vcol[:, l, first + k:first + k + 1]).then_inc(xhi_ready, 1)

            def in_proj(l):
                for b, (c0, c1) in enumerate(IN_BLOCKS):
                    c = T_IN[l] + 2 * b
                    if b == 4:
                        act.wait_ge(gzT_ready, l + 1)
                        nc.scalar.activation(gzT[0:RANK, :], ps[0:RANK, 5, SEQ:2 * SEQ], ACT.Copy).then_inc(gzT_copied, 1)
                    split_hi(act, c + 3)
                    if b == 1:
                        if l == 0:
                            act.wait_ge(vecT_ready, 1)
                            nc.scalar.activation(vcol[:, 0, KC:], ps[:, 6, KC:V_ROWS], ACT.Copy)
                            nc.scalar.activation(vcol[:, 1, :], ps[:, 7, 0:V_ROWS], ACT.Copy).then_inc(vec_ready, 1)
                        act.wait_ge(uT_ready, l + 1)
                        nc.scalar.activation(uT[:, :, TAPS - 1:], ps[:, 4, :].rearrange("p (j n) -> p j n", j=2),
                                             ACT.Copy).then_inc(uT_copied, 1)
                    if b == 2:
                        act.wait_ge(pT_ready, l + 1)
                        nc.scalar.activation(p_hi[:, :, :], ps[:, 5, :].rearrange("p (j n) -> p j n", j=2),
                                             ACT.Copy).then_inc(phi_ready, 1)
                    if b == 4:
                        act.wait_ge(gbias_ready, l + 1)
                        link(nc.scalar.activation(g_abs[:, :, :], g_pre[:, :, :], ACT.Abs))
                        link(nc.scalar.activation(g_abs[:, :, :], g_abs[:, :, :], ACT.Exp, scale=-1.0))
                        exps(l, 0)
                        nc.scalar.activation(g_abs[:, :, :], g_abs[:, :, :], ACT.Ln, bias=1.0).then_inc(gln_ready, 1)
                    if b == 5:
                        act.wait_ge(rev_ready, l + 1)
                        nc.scalar.activation(g_exp[:, :, :], ps[:, 5, 0:SEQ].rearrange("p (t n) -> p t n", t=2), ACT.Exp,
                                             scale=1.0 / TAU).then_inc(gexp_ready, 1)
                        nc.scalar.activation(decay[:, :], ps[:, 5, SEQ:SEQ + 4], ACT.Exp, scale=1.0 / TAU).then_inc(gexp_ready, 1)
                        probs_T(l, 0)
                        exps(l, 1)
                    act.wait_ge(tile_used, c + 2)
                    s = 2 * (b % 2)
                    if b == 0:
                        act.wait_ge(rstd_ready, 3 * l + 1)
                    parts = ([(0, C_G, ACT.Copy), (C_G, c1, ACT.Sigmoid)] if b == 0 else
                             [(c0, C_GZ, ACT.Silu), (C_GZ, c1, ACT.Copy)] if b == B_RZ else [(c0, c1, ACT.Copy)])
                    for p0, p1, func in parts:
                        for t in range(TT):
                            ins = nc.scalar.activation(z[:, t, p0:p1], ps[:, s + t, p0 - c0:p1 - c0], func,
                                                       scale=rstd[:, t:t + 1])
                        ins.then_inc(z_ready, 1)
                    if b < 5:
                        split_hi(act, c + 4)
                    if b == B_RZ:
                        for t, bank in ((0, 5), (1, 6)):
                            act.wait_ge(qkT_ready, 4 * l + t + 1)
                            nc.scalar.activation(qT[:, :, t * P:(t + 1) * P], ps[:, bank, :].rearrange("p (j n) -> p j n", j=4),
                                                 ACT.Copy, scale=DH ** -0.5).then_inc(qT_copied, 1)
                        for t, bank in ((0, 7), (1, 4)):
                            act.wait_ge(qkT_ready, 4 * l + 2 + t + 1)
                            nc.scalar.activation(kT[:, :, t * P:(t + 1) * P], ps[:, bank, :].rearrange("p (j n) -> p j n", j=4),
                                                 ACT.Copy).then_inc(kT_copied, 1)
                        if l == 0:
                            act.wait_ge(misc_landed, 16 * N_MISC)
                            nc.scalar.activation(rw_parts[:, :, 0:N_EXP], rw[:, :, :], ACT.Copy).then_inc(rw_hi_ready, 1)
                            act.wait_ge(setup_done, 3)
                            nc.scalar.activation(lam_exp[:, :, :], lam_exp[:, :, :], ACT.Exp).then_inc(vec_ready, 1)

            def exps(l, t):
                n = P * (t + 1)
                for c in range(2):
                    act.wait_ge(neg_max_ready, 3 * l + t + (c if t else 0) + 1)
                    for i in range(HEADS):
                        m = HEADS * c + i
                        nc.scalar.activation(probs[:, m, 0:n], score(t, c, i), ACT.Exp, bias=neg_max[:, t, m:m + 1],
                                             accum_out=row_sum[:, t, m:m + 1]).then_inc(exp_ready, 1)

            def probs_T(l, t):
                for kt in range(t + 1):
                    act.wait_ge(aT_ready, TT * l + t + 1)
                    nc.scalar.activation(aT[:, kt, :], ps[:, (4, 0)[t] + kt, :], ACT.Copy).then_inc(aT_copied, 1)

            def o_square(l, t):
                act.wait_ge(o_ready, TT * l + t + 1)
                if t:
                    act.wait_ge(ostd_ready, TT * l + 1)
                for i in range(HEADS):
                    nc.scalar.activation(osq[:, i * DV:(i + 1) * DV], ps[:, O_BANK[t], i * DV:(i + 1) * DV], ACT.Square,
                                         accum_out=o_ss[:, i:i + 1]).then_inc(osq_ready, 1)

            def o_std_(l, t):
                act.wait_ge(oss_ready, TT * l + t + 1)
                nc.scalar.activation(o_std, o_ss, ACT.Sqrt).then_inc(ostd_ready, 1)

            def o_split(l, t):
                act.wait_ge(onT_ready, TT * l + t + 1)
                nc.scalar.activation(x_hi[:, 2:6, t * P:(t + 1) * P], ps[:, OT_BANK[t], :].rearrange("p (j n) -> p j n", j=4),
                                     ACT.Copy, scale=vcol[:, l, V_SUB:V_SUB + 1]).then_inc(mixhi_ready, 1)

            def mixer(l):
                act.wait_ge(gqT_ready, l + 1)
                nc.scalar.activation(gqT[:, :], ps[:, 2, 0:SEQ], ACT.Copy, scale=GLA_DK ** -0.5).then_inc(gqT_copied, 1)
                o_square(l, 0)
                probs_T(l, 1)
                o_std_(l, 0)
                o_square(l, 1)
                o_std_(l, 1)
                o_split(l, 0)
                act.wait_ge(osq_ready, 2 * HEADS * (l + 1))
                act.wait_ge(go_ready, l + 1)
                nc.scalar.activation(osq[:, :], ps[:, 7, :], ACT.Square).then_inc(gsq_ready, 1)
                o_split(l, 1)
                act.wait_ge(gss_ready, l + 1)
                nc.scalar.activation(g_std, g_ss, ACT.Sqrt, bias=eps_t[:, 0:1], scale=1.0 / GLA_DV).then_inc(gstd_ready, 1)
                act.wait_ge(gonT_ready, l + 1)
                nc.scalar.activation(x_hi[:, 6:8, :], ps[:, 6, :].rearrange("p (j n) -> p j n", j=2), ACT.Copy,
                                     scale=vcol[:, l, V_GLA:V_GLA + 1]).then_inc(mixhi_ready, 1)
                split_hi(act, T_OUT[l] + 2)
                act.wait_ge(yc_ready, l + 1)
                nc.scalar.activation(ysq[:, :, :], yc[:, :, :], ACT.Square).then_inc(ysq_ready, 1)
                act.wait_ge(var_ready, l + 1)
                nc.scalar.activation(ysq[:, 0, :], ps[:, 5, SEQ:2 * SEQ], ACT.Sqrt, bias=eps_t[:, 0:1]).then_inc(ystd_ready, 1)
                link(nc.scalar.activation(g_std, g_ss, ACT.Silu))
                split_hi(act, T_OUT[l] + 3)
                act.wait_ge(yn_ready, l + 1)
                for j in range(2):
                    nc.scalar.activation(yc[:, j, :], yc[:, j, :], ACT.Silu, bias=vcol[:, l, V_LB + j:V_LB + j + 1],
                                         scale=vcol[:, l, V_LG + j:V_LG + j + 1]).then_inc(y_ready, 1)
                act.wait_ge(y_ready, 2 * l + 2)
                nc.scalar.activation(x_hi[:, 0:2, :], yc[:, :, :], ACT.Copy).then_inc(mixhi_ready, 1)

            def up_copy(l):
                act.wait_ge(tile_used, T_UP[l] + 1)
                nc.scalar.activation(up[:, :, :], ps[:, 0:4, :].rearrange("p (t m) n -> p t (m n)", t=2),
                                     ACT.Copy).then_inc(up_ready, 1)

            def ple_gate(l, r):
                for b in range(2):
                    c = T_GATE[l] + 2 * b
                    if l == 0:
                        split_hi(act, c + 3)
                    elif b == 0:
                        split_hi(act, c + 3, r)
                    if (l, b) == (0, 1):
                        norm_hi(3, 1, V_MIX, 0)
                    act.wait_ge(tile_used, nth(c + 1, r))
                    if b == 0:
                        act.wait_ge(rstd_ready, 3 * l + 3)
                    else:
                        act.wait_ge(h_updated, 4 * l + 5)
                    for t in range(TT):
                        nc.scalar.activation(gate[:, t, :], ps[:, 4 + 2 * b + t, :], ACT.Sigmoid,
                                             scale=rstd[:, t:t + 1]).then_inc(gate_ready, 1)
                    if l == 1 and b == 0:
                        act.wait_ge(h_updated, 9)
                        for t in range(TT):
                            nc.scalar.activation(z[:, 1, C_DQ + 512 * t:C_DQ + 512 * (t + 1)], h[:, t, 0:512], ACT.Square,
                                                 accum_out=half_sq[:, t:t + 1]).then_inc(sumsq_ready, 1)
                    if l == 0:
                        split_hi(act, c + 4)

            act.wait_ge(gainT_ready, 1)
            nc.scalar.activation(vcol[:, 0, 0:KC], ps[:, 0, 0:KC], ACT.Copy).then_inc(gain_ready, 1)
            act.wait_ge(gain_ready, 1)
            norm_hi(0, 0, V_MIX, 0)
            split_hi(act, 0)
            norm_hi(0, 0, V_MIX, 1)
            split_hi(act, 1)
            split_hi(act, 2)
            act.wait_ge(setup_done, 1)
            act.wait_ge(x_landed, 16)
            norm_stats(0)
            for l in range(DEPTH):
                if l:
                    norm_hi(3, 1, V_MIX, 1)
                    norm_stats(3)
                in_proj(l)
                mixer(l)
                split_hi(act, T_OUT[l] + 4)
                norm_hi(3 * l + 1, l, V_FFN, 0)
                split_hi(act, T_OUT[l] + 5)
                split_hi(act, T_OUT[l] + 6)
                norm_hi(3 * l + 1, l, V_FFN, 1)
                norm_stats(3 * l + 1)
                if l == 0:
                    def ffn_gate():
                        for t in range(TT):
                            ins = nc.scalar.activation(silu_g[:, t * FB:(t + 1) * FB], ps[:, t, 0:FB], ACT.Silu,
                                                       scale=rstd[:, t:t + 1])
                        ins.then_inc(f_silu, 1)

                    def ffn_T(b):
                        act.wait_ge(f_T, b + 1)
                        nc.scalar.activation(ff_hi[:, :], ps[:, 2, :], ACT.Copy).then_inc(f_hi, 1)

                    act.wait_ge(tile_used, T_FFN + 2)
                    act.wait_ge(rstd_ready, 2)
                    ffn_gate()
                    with act.Fori(0, (N_FB - 1) // 2) as i:
                        for s in range(2):
                            c = T_FFN + 2 + 3 * s
                            split_hi(act, c + 1, i)
                            split_hi(act, c + 2, i)
                            ffn_T(i * 2 + s)
                            split_hi(act, c + 3, i)
                            act.wait_ge(tile_used, nth(c + 1, i))
                            ffn_gate()
                    split_hi(act, T_UP[0])
                    ffn_T(N_FB - 1)
                    split_hi(act, T_UP[0] + 1)
                    split_hi(act, T_UP[0] + 2)
                    for half in range(2):
                        norm_hi(2, 0, V_PLE, half)
                    split_hi(act, T_UP[0] + 3)
                    up_copy(0)
                    norm_stats(2)
                    ple_gate(0, None)

            act.wait_ge(logitT_ready, 1)
            nc.scalar.activation(gzT[0:2 * N_EXP, :], ps[0:2 * N_EXP, 4, 0:SEQ], ACT.Copy).then_inc(logitT_copied, 1)
            act.wait_ge(chosen_ready, 2)
            nc.scalar.activation(e_gate[:, :, 1:1 + N_EXP], e_gate[:, :, 1:1 + N_EXP], ACT.Exp).then_inc(lexp_ready, 1)
            split_hi(act, T_UP[1] + 3)
            up_copy(1)
            act.wait_ge(passes_ready, 1)
            passes = act.value_load(passes_t[0:1, 0:1], min_val=1, max_val=2)

            def expert_rows_hi(n):
                for half in range(2):
                    act.wait_ge(m_gathered, n * 2 + (half + 1))
                    nc.scalar.activation(xe_hi[:, 4 * half:4 * half + 4, :],
                                         ps[:, 6 + half, :].rearrange("p (k n) -> p k n", k=4), ACT.Copy).then_inc(m_xhi, 1)

            def expert_out_hi(r):
                act.wait_ge(tile_used, nth(T_MOE - 1, r))
                for half in range(2):
                    nc.scalar.activation(y_hi[:, 512 * half:512 * half + 512], ps[:, 4 + half, :],
                                         ACT.Copy).then_inc(m_yhi, 1)

            expert_rows_hi(0)
            with act.Fori(0, passes) as ps_i:
                with act.Fori(0, N_EXP) as e:
                    n = ps_i * N_EXP + e
                    r0 = n * N_MB

                    def gate_of(c, r):
                        act.wait_ge(tile_used, nth(c, r))
                        nc.scalar.activation(silu_g[:, :], ps[:, 0, :], ACT.Silu).then_inc(m_silu, 1)

                    def upper_T(m):
                        act.wait_ge(m_T, m)
                        nc.scalar.activation(ff_hi[:, :], ps[:, 2, :], ACT.Copy).then_inc(m_hi, 1)

                    split_hi(act, T_MOE + 3, r0)
                    gate_of(T_MOE + 1, r0)
                    split_hi(act, T_MOE + 4, r0)
                    split_hi(act, T_MOE + 5, r0)
                    with act.Fori(1, N_MB) as b:
                        r = r0 + b - 1
                        split_hi(act, T_MOE + 6, r)
                        upper_T(r0 + b)
                        split_hi(act, T_MOE + 7, r)
                        gate_of(T_MOE + 5, r)
                        for c in range(8, 12):
                            split_hi(act, T_MOE + c, r)
                    r1 = r0 + N_MB
                    upper_T(r1)
                    split_hi(act, T_MOE + 0, r1)
                    expert_rows_hi(n + 1)
                    act.wait_ge(m_pickT, n + 1)
                    nc.scalar.activation(pickT[:, :], ps[:, 3, 0:SEQ], ACT.Copy).then_inc(m_pickT_copied, 1)
                    split_hi(act, T_MOE + 1, r1)
                    expert_out_hi(r1)
                    split_hi(act, T_MOE + 2, r1)
            for half in range(2):
                norm_hi(5, 1, V_PLE, half)
            act.wait_ge(m_added, passes * (2 * N_EXP) + 2)
            norm_stats(5)
            ple_gate(1, passes * (N_EXP * N_MB))
            act.wait_ge(sumsq_ready, 14)
            link(nc.scalar.activation(std, half_sq, ACT.Sqrt, bias=eps_t[:, 0:1], scale=1.0 / D))
            for t in range(TT):
                act.wait_ge(h_updated, 10 + t)
                link(nc.scalar.activation(z[:, 1, C_DQ + 512 * t:C_DQ + 512 * (t + 1)], h[:, t, 512:], ACT.Square,
                                          accum_out=rest_sq[:, t:t + 1]))
                act.wait_ge(part_ready, 1)
                nc.scalar.activation(std[:, t:t + 1], rest_sq[:, t:t + 1], ACT.Sqrt, bias=part_ms[:, t:t + 1],
                                     scale=1.0 / D).then_inc(std_ready, 1)

        @block.vector
        def _(dve):
            steps = [0]

            def link(ins):
                steps[0] += 1
                ins.then_inc(dve_step, 1)
                dve.wait_ge(dve_step, steps[0])

            def norm_rstd(q):
                dve.wait_ge(std_ready, q + 1)
                nc.vector.reciprocal(rstd, std).then_inc(rstd_ready, 1)

            def norm_lo(q, l, first, half):
                for k in range(4 * half, 4 * half + 4):
                    dve.wait_ge(xhi_ready, 8 * q + 2 * (k // 2) + 2)
                    hi, lo = x_parts(q, k)
                    nc.vector.scalar_tensor_tensor(
                        out=lo, in0=xT(q, k), scalar=vcol[:, l, first + k:first + k + 1], in1=hi.bitcast(F32),
                        op0=ALU.mult, op1=ALU.subtract).then_inc(xlo_ready, 1)

            def taps(l, first, last):
                for n in range(first, min(last, 2 * TAPS)):
                    tap, j = n // 2, n % 2
                    w = vcol[:, l, V_TAP + n:V_TAP + n + 1]
                    src = uT[:, j, tap:tap + SEQ]
                    if tap == 0:
                        ins = nc.vector.tensor_scalar(yc[:, j, :], src, w, vcol[:, l, V_CB + j:V_CB + j + 1],
                                                      ALU.mult, ALU.add)
                    else:
                        dve.wait_ge(tap_done, 2 * TAPS * l + n - 1)
                        ins = nc.vector.scalar_tensor_tensor(out=yc[:, j, :], in0=src, scalar=w, in1=yc[:, j, :],
                                                             op0=ALU.mult, op1=ALU.add)
                    ins.then_inc(tap_done, 1)

            def rope(l):
                dve.wait_ge(z_ready, 8 * l + Z_DONE[2])
                qk = z[:, :, C_DQ:C_DV].rearrange("p t (g d) -> p t g d", d=DH)
                x1, x2 = qk[:, :, :, 0:8], qk[:, :, :, 8:16]
                cos = cst[:, K_COS:K_COS + 16].rearrange("p (t o n) -> p t o n", t=2, o=1).broadcast_to([P, TT, 16, 8])
                sin = cst[:, K_SIN:K_SIN + 16].rearrange("p (t o n) -> p t o n", t=2, o=1).broadcast_to([P, TT, 16, 8])
                for i, (a, b) in enumerate(((x1, cos), (x2, sin), (x2, cos), (x1, sin))):
                    for t in range(TT):
                        ins = nc.vector.tensor_tensor(rot[:, i, t], a[:, t], b[:, t], ALU.mult)
                link(ins)
                for t in range(TT):
                    nc.vector.tensor_tensor(x1[:, t], rot[:, 0, t], rot[:, 1, t], ALU.subtract).then_inc(rope_done, 1)
                    nc.vector.tensor_tensor(x2[:, t], rot[:, 2, t], rot[:, 3, t], ALU.add).then_inc(rope_done, 1)

            TAPS_FIRST, TAPS_SECOND = (0, 8, 8, 4, 8, 2), (0, 10, 0, 5, 0, 4)

            def in_proj(l):
                n = 0
                for b in range(len(IN_BLOCKS)):
                    c = T_IN[l] + 2 * b
                    if b == 4:
                        dve.wait_ge(gpre_ready, l + 1)
                        nc.vector.tensor_tensor(g_pre[:, :, :], ps[:, 5, 0:SEQ].rearrange("p (t n) -> p t n", t=2),
                                                b_gate[:, l, :].rearrange("p (o n) -> p o n", o=1).broadcast_to([P, TT, P]),
                                                ALU.add).then_inc(gbias_ready, 1)
                    if b == 5:
                        row_max(l, 1)
                    split_lo(dve, c + 3)
                    if b == 0:
                        dve.wait_ge(z_ready, 8 * l + Z_DONE[0])
                        nc.vector.tensor_tensor(z[:, :, 0:C_G], z[:, :, 0:C_G], z[:, :, C_G:2 * C_G],
                                                ALU.mult).then_inc(u_ready, 1)
                    if b == 2:
                        dve.wait_ge(phi_ready, l + 1)
                        nc.vector.tensor_tensor(p_lo[:, :, :], ps[:, 5, :].rearrange("p (j n) -> p j n", j=2),
                                                p_hi[:, :, :].bitcast(F32), ALU.subtract).then_inc(plo_ready, 1)
                    if b == 4:
                        row_max(l, 0)
                    if b == 1:
                        dve.wait_ge(uT_copied, l + 1)
                    taps(l, n, n + TAPS_FIRST[b])
                    n += TAPS_FIRST[b]
                    if b == 5:
                        differences(l, 1)
                    if b == 4:
                        dve.wait_ge(gln_ready, l + 1)
                        nc.vector.scalar_tensor_tensor(out=log_a[:, :, :], in0=g_pre[:, :, :], scalar=0.0, in1=g_abs[:, :, :],
                                                       op0=ALU.min, op1=ALU.subtract).then_inc(la_ready, 1)
                    if b == 2:
                        rope(l)
                    if b < 5:
                        split_lo(dve, c + 4)
                    if b == 1 and l == 0:
                        lambda_dots()
                    if b == 4:
                        if l == 0:
                            lambdas()
                        differences(l, 0)
                    taps(l, n, n + TAPS_SECOND[b])
                    n += TAPS_SECOND[b]
                return n

            def row_max(l, t):
                n = P * (t + 1)
                for c in range(t + 1):
                    dve.wait_ge(scores_ready, 3 * l + t + c + 1)
                    if t:
                        bank = (0, 6)[c]
                        src, dst = ps[:, bank:bank + 2, :].rearrange("p b (i n) -> p (b i) n", i=2), neg_max[:, t, HEADS * c:HEADS * c + HEADS]
                    else:
                        src, dst = ps[:, 6:8, :].rearrange("p b (i n) -> p (b i) n", i=HEADS), neg_max[:, t, :]
                    nc.vector.tensor_reduce(dst, src, AX.X, ALU.max, negate=True).then_inc(neg_max_ready, 1)

            def differences(l, t):
                n = P * (t + 1)
                dve.wait_ge(exp_ready, 2 * HEADS * (TT * l + t + 1))
                s0, s1 = row_sum[:, t, 0:HEADS], row_sum[:, t, HEADS:]
                link(nc.vector.reciprocal(factor[:, t, :], s1))
                link(nc.vector.scalar_tensor_tensor(out=factor[:, t, :], in0=factor[:, t, :], scalar=neg_lam[:, l:l + 1], in1=s0,
                                                    op0=ALU.mult, op1=ALU.mult))
                for i in range(HEADS):
                    nc.vector.scalar_tensor_tensor(out=probs[:, i, 0:n], in0=probs[:, HEADS + i, 0:n],
                                                   scalar=factor[:, t, i:i + 1], in1=probs[:, i, 0:n], op0=ALU.mult,
                                                   op1=ALU.add).then_inc(a_ready, 1)
                link(nc.vector.scalar_tensor_tensor(out=o_eps[:, t, :], in0=s0, scalar=EPS, in1=s0,
                                                    op0=ALU.mult, op1=ALU.mult))

            def o_sums(l, t):
                dve.wait_ge(osq_ready, HEADS * (TT * l + t + 1))
                nc.vector.scalar_tensor_tensor(out=o_ss, in0=o_ss, scalar=1.0 / DV, in1=o_eps[:, t, :], op0=ALU.mult,
                                               op1=ALU.add).then_inc(oss_ready, 1)

            def o_scale(l, t):
                dve.wait_ge(ostd_ready, TT * l + t + 1)
                link(nc.vector.reciprocal(o_inv, o_std))
                if t:
                    dve.wait_ge(onT_ready, TT * l + 1)
                nc.vector.tensor_tensor(on[:, :].rearrange("p (j n) -> p j n", j=HEADS),
                                        ps[:, O_BANK[t], :].rearrange("p (j n) -> p j n", j=HEADS),
                                        o_inv.rearrange("p (j o) -> p j o", o=1).broadcast_to([P, HEADS, DV]),
                                        ALU.mult).then_inc(on_ready, 1)

            def lower_mix(l, part, chunks, src, scale, cols=slice(0, SEQ)):
                dve.wait_ge(mixhi_ready, 4 * l + part + 1)
                hi = x_hi[:, chunks, cols].bitcast(F32)
                if scale is None:
                    ins = nc.vector.tensor_tensor(x_lo[:, chunks, cols], src, hi, ALU.subtract)
                else:
                    ins = nc.vector.scalar_tensor_tensor(out=x_lo[:, chunks, cols], in0=src, scalar=scale, in1=hi,
                                                         op0=ALU.mult, op1=ALU.subtract)
                ins.then_inc(mixlo_ready, 1)

            def lower_o(l, t, part):
                lower_mix(l, part, slice(2, 6), ps[:, OT_BANK[t], :].rearrange("p (j n) -> p j n", j=4),
                          vcol[:, l, V_SUB:V_SUB + 1], slice(t * P, (t + 1) * P))

            def mixer(l, n):
                dve.wait_ge(gexp_ready, 2 * l + 2)
                dve.wait_ge(z_ready, 8 * l + 8)
                link(nc.vector.tensor_tensor(z[:, :, C_GK:C_GV], z[:, :, C_GK:C_GV], g_exp[:, :, :], ALU.mult))
                for half in range(2):
                    nc.vector.tensor_scalar(kx_half[:, :, half, :], z[:, :, C_GK:C_GV], cst[:, K_HALF + half:K_HALF + half + 1],
                                            None, ALU.mult).then_inc(kx_ready, 1)
                o_sums(l, 0)
                taps(l, n, n + 2)
                n += 2
                for c in range(4):
                    if c % 2 == 0:
                        dve.wait_ge(kv_ready, 2 * l + c // 2 + 1)
                        nc.vector.tensor_tensor(
                            state[:, c:c + 2, :] if c == 0 else kv[:, :, :],
                            ps[:, 3 - c // 2, :].rearrange("p (j n) -> p j n", j=2),
                            cst[:, K_BD:K_BD + 256].rearrange("p (o n) -> p o n", o=1).broadcast_to([P, 2, 256]),
                            ALU.mult).then_inc(kv_masked, 1)
                        dve.wait_ge(kv_masked, 2 * l + c // 2 + 1)
                    if c:
                        nc.vector.scalar_tensor_tensor(
                            out=state[:, c, :], in0=state[:, c - 1, :], scalar=decay[:, c:c + 1],
                            in1=state[:, 1, :] if c == 1 else kv[:, c % 2, :], op0=ALU.mult,
                            op1=ALU.add).then_inc(state_ready, 1)
                        dve.wait_ge(state_ready, 3 * l + c)
                    if c == 1:
                        o_scale(l, 0)
                    if c == 2:
                        o_sums(l, 1)
                taps(l, n, n + 1)
                o_scale(l, 1)
                taps(l, n + 1, n + 2)
                lower_o(l, 0, 0)
                dve.wait_ge(gsq_ready, l + 1)
                heads = lambda a: a.rearrange("p (j n) -> p j n", n=GLA_DV)
                nc.vector.tensor_reduce(g_ss, heads(osq[:, :]), AX.X, ALU.add).then_inc(gss_ready, 1)
                lower_o(l, 1, 1)
                taps(l, n + 2, n + 4)
                dve.wait_ge(gstd_ready, l + 1)
                link(nc.vector.reciprocal(g_inv, g_std))
                link(nc.vector.tensor_tensor(heads(silu_g[:, :]), heads(ps[:, 7, :]),
                                             g_inv.rearrange("p (j o) -> p j o", o=1).broadcast_to([P, 8, GLA_DV]), ALU.mult))
                nc.vector.tensor_tensor(silu_g[:, :].rearrange("p (t n) -> p t n", t=2),
                                        silu_g[:, :].rearrange("p (t n) -> p t n", t=2), z[:, :, C_GR:C_GZ],
                                        ALU.mult).then_inc(gon_ready, 1)
                taps(l, n + 4, 2 * TAPS)
                lower_mix(l, 2, slice(6, 8), ps[:, 6, :].rearrange("p (j n) -> p j n", j=2), vcol[:, l, V_GLA:V_GLA + 1])
                dve.wait_ge(mean_ready, l + 1)
                both = lambda a: a.rearrange("p (o n) -> p o n", o=1).broadcast_to([P, 2, SEQ])
                nc.vector.tensor_tensor(yc[:, :, :], yc[:, :, :], both(ps[:, 5, 0:SEQ]), ALU.subtract).then_inc(yc_ready, 1)
                split_lo(dve, T_OUT[l] + 2)
                dve.wait_ge(ystd_ready, l + 1)
                link(nc.vector.reciprocal(ysq[:, 1, :], ysq[:, 0, :]))
                nc.vector.tensor_tensor(yc[:, :, :], yc[:, :, :], both(ysq[:, 1, :]), ALU.mult).then_inc(yn_ready, 1)
                split_lo(dve, T_OUT[l] + 3)
                lower_mix(l, 3, slice(0, 2), yc[:, :, :], None)

            def out_proj(l):
                split_lo(dve, T_OUT[l] + 4)
                for b in range(2):
                    dve.wait_ge(tile_used, T_OUT[l] + 3 + b)
                    hb = h[:, :, 512 * b:512 * b + 512]
                    nc.vector.tensor_tensor(hb, hb, ps[:, 2 * b:2 * b + 2, :], ALU.add).then_inc(h_updated, 1)
                    if b == 0:
                        norm_lo(3 * l + 1, l, V_FFN, 0)
                split_lo(dve, T_OUT[l] + 5)
                norm_lo(3 * l + 1, l, V_FFN, 1)
                split_lo(dve, T_OUT[l] + 6)
                norm_rstd(3 * l + 1)

            def ple_add(l, r):
                for b in range(2):
                    c = T_GATE[l] + 2 * b
                    if l == 0 or b == 0:
                        split_lo(dve, c + 3, r)
                    if (l, b) == (0, 1):
                        norm_lo(3, 1, V_MIX, 0)
                    for t in range(TT):
                        dve.wait_ge(gate_ready, 4 * l + 2 * b + t + 1)
                        link(nc.vector.tensor_tensor(gate[:, t, :], gate[:, t, :], up[:, t, 512 * b:512 * b + 512], ALU.mult))
                        hb = h[:, t, 512 * b:512 * b + 512]
                        ins = nc.vector.tensor_tensor(hb, hb, gate[:, t, :], ALU.add)
                        if t or (l, b) == (1, 1):
                            ins.then_inc(h_updated, 1)
                    if (l, b) == (1, 0):
                        dve.wait_ge(sumsq_ready, 14)
                        nc.vector.tensor_scalar(part_ms, half_sq, 1.0 / D, EPS, ALU.mult, ALU.add).then_inc(part_ready, 1)
                    if l == 0:
                        split_lo(dve, c + 4)

            def lambda_dots():
                dve.wait_ge(misc_landed, 16 * N_MISC)
                for l in range(DEPTH):
                    link(nc.vector.tensor_tensor(lam_mul[:, l, :, :], lam_row[:, l, 0::2, :], lam_row[:, l, 1::2, :],
                                                 ALU.mult))
                    nc.vector.tensor_reduce(lam_exp[:, l, :], lam_mul[:, l, :, :], AX.X, ALU.add).then_inc(setup_done, 1)

            def lambdas():
                dve.wait_ge(rw_hi_ready, 1)
                nc.vector.tensor_tensor(rw_parts[:, :, N_EXP:], rw[:, :, :], rw_parts[:, :, 0:N_EXP].bitcast(F32),
                                        ALU.subtract).then_inc(rw_lo_ready, 1)
                dve.wait_ge(vec_ready, 2)
                for l in range(DEPTH):
                    lam_init = 0.8 - 0.6 * math.exp(-0.3 * l)
                    link(nc.vector.scalar_tensor_tensor(out=neg_lam[:, l:l + 1], in0=lam_exp[:, l, 1:2], scalar=-lam_init,
                                                        in1=lam_exp[:, l, 0:1], op0=ALU.add, op1=ALU.subtract))
                    link(nc.vector.tensor_scalar(vcol[:, l, V_SUB:V_SUB + 1], vcol[:, l, V_SUB:V_SUB + 1],
                                                 1.0 - lam_init, None, ALU.mult))

            nc.vector.memset(eps_t[:, :], EPS).then_inc(setup_done, 1)
            link(nc.vector.memset(e_gate[:, :, :], 0.0))
            link(nc.vector.memset(slot_of[:, :, :], 0.0))
            link(nc.vector.memset(uT[:, :, :], 0.0))
            link(nc.vector.memset(zeros[:, :].bitcast(F32), 0.0))
            norm_lo(0, 0, V_MIX, 0)
            split_lo(dve, 0)
            norm_lo(0, 0, V_MIX, 1)
            split_lo(dve, 1)
            split_lo(dve, 2)
            norm_rstd(0)
            for l in range(DEPTH):
                if l:
                    norm_lo(3, 1, V_MIX, 1)
                    norm_rstd(3)
                mixer(l, in_proj(l))
                out_proj(l)
                if l == 0:
                    def ffn_mult(b):
                        dve.wait_ge(f_silu, b + 1)
                        for t in range(TT):
                            cols = slice(t * FB, (t + 1) * FB)
                            ins = nc.vector.scalar_tensor_tensor(out=ff[:, cols], in0=silu_g[:, cols], scalar=rstd[:, t:t + 1],
                                                                 in1=ps[:, t, FB:2 * FB], op0=ALU.mult, op1=ALU.mult)
                        ins.then_inc(f_act, 1)

                    def ffn_T(b):
                        dve.wait_ge(f_hi, b + 1)
                        nc.vector.tensor_tensor(ff_lo[:, :], ps[:, 2, :], ff_hi[:, :].bitcast(F32),
                                                ALU.subtract).then_inc(f_lo, 1)

                    dve.wait_ge(rstd_ready, 2)
                    ffn_mult(0)
                    with dve.Fori(0, (N_FB - 1) // 2) as i:
                        for s in range(2):
                            c = T_FFN + 2 + 3 * s
                            split_lo(dve, c + 1, i)
                            split_lo(dve, c + 2, i)
                            ffn_T(i * 2 + s)
                            split_lo(dve, c + 3, i)
                            ffn_mult(i * 2 + (1 + s))
                    split_lo(dve, T_UP[0])
                    ffn_T(N_FB - 1)
                    split_lo(dve, T_UP[0] + 1)
                    dve.wait_ge(tile_used, T_UP[0])
                    for b in range(2):
                        hb = h[:, :, 512 * b:512 * b + 512]
                        nc.vector.tensor_tensor(hb, hb, ps[:, 4 + b:8:2, :], ALU.add).then_inc(h_updated, 1)
                    split_lo(dve, T_UP[0] + 2)
                    for half in range(2):
                        norm_lo(2, 0, V_PLE, half)
                    split_lo(dve, T_UP[0] + 3)
                    norm_rstd(2)
                    ple_add(0, None)

            def spread(a, n):
                return a.rearrange("p (t o) -> p t o", o=1).broadcast_to([P, TT, n])

            def expert_rows(t):
                nc.vector.scalar_tensor_tensor(out=xn[:, t, :], in0=h[:, t, :], scalar=rstd[:, t:t + 1], in1=g_row[:, :],
                                               op0=ALU.mult, op1=ALU.mult).then_inc(xg_ready, 1)

            dve.wait_ge(rstd_ready, 5)
            dve.wait_ge(grow_landed, 16)
            dve.wait_ge(logitT_ready, 1)
            expert_rows(0)
            dve.wait_ge(logit_ready, 1)
            link(nc.vector.tensor_tensor(logit[:, :, :], ps[:, 5, 0:TT * N_EXP].rearrange("p (t e) -> p t e", t=TT),
                                         spread(rstd, N_EXP), ALU.mult))
            square_of = lambda a: a.rearrange("p t (a b) -> p t a b", a=N_EXP)
            sq_a, sq_b = square_of(cmp_a[:, :, 0:64]), square_of(cmp_b[:, :, 0:64])
            own = logit[:, :, :].rearrange("p t (e o) -> p t e o", o=1).broadcast_to([P, TT, N_EXP, N_EXP])
            other = logit[:, :, :].rearrange("p t (o e) -> p t o e", o=1).broadcast_to([P, TT, N_EXP, N_EXP])
            ties = cst[:, K_TIE:K_TIE + 64].rearrange("p (o a b) -> p o a b", o=1, a=N_EXP).broadcast_to([P, TT, N_EXP, N_EXP])
            nc.vector.tensor_tensor(sq_a, own, other, ALU.is_lt)
            link(nc.vector.tensor_tensor(sq_b, own, other, ALU.is_equal))
            link(nc.vector.tensor_tensor(sq_b, sq_b, ties, ALU.mult))
            link(nc.vector.tensor_tensor(sq_a, sq_a, sq_b, ALU.add))
            link(nc.vector.tensor_reduce(chosen[:, :, :], sq_a, AX.X, ALU.add))
            nc.vector.tensor_scalar(chosen[:, :, :], chosen[:, :, :], 1.5, None, ALU.is_lt).then_inc(chosen_ready, 1)
            expert_rows(1)
            dve.wait_ge(chosen_ready, 1)
            dve.wait_ge(rank_ready, 1)
            link(nc.vector.scalar_tensor_tensor(out=slot_of[:, :, 0:N_EXP], scalar=1.0, in1=chosen[:, :, :],
                                                in0=ps[:, 6, 0:TT * N_EXP].rearrange("p (t e) -> p t e", t=TT),
                                                op0=ALU.add, op1=ALU.mult))
            link(nc.vector.tensor_scalar(slot_of[:, :, N_EXP:2 * N_EXP], slot_of[:, :, 0:N_EXP], -1.0 - P, None, ALU.add))
            link(nc.vector.tensor_scalar(slot_of[:, :, 0:N_EXP], slot_of[:, :, 0:N_EXP], -1.0, None, ALU.add))
            link(nc.vector.tensor_reduce(count_max, ps[:, 6, 2 * N_EXP:3 * N_EXP], AX.X, ALU.max))
            nc.vector.tensor_scalar(passes_t[:, :], count_max, P + 0.5, 1.0, ALU.is_gt, ALU.add).then_inc(passes_ready, 1)
            for free in (m_act, m_lo, m_yhi, m_ylo):
                dve.sem_inc(free, 1)

            def picks(n):
                for t in range(TT):
                    nc.vector.tensor_scalar(pick[:, t, :], cst[:, K_IOTA:K_IOTA + P], slot_of[:, t, bass.ds(n, 1)], None,
                                            ALU.is_equal).then_inc(m_pick, 1)

            def expert_rows_lo(n):
                for half in range(2):
                    dve.wait_ge(m_xhi, n * 2 + (half + 1))
                    nc.vector.tensor_tensor(xe_lo[:, 4 * half:4 * half + 4, :],
                                            ps[:, 6 + half, :].rearrange("p (k n) -> p k n", k=4),
                                            xe_hi[:, 4 * half:4 * half + 4, :].bitcast(F32),
                                            ALU.subtract).then_inc(m_xlo, 1)

            def expert_out_lo(n):
                for half in range(2):
                    dve.wait_ge(m_yhi, n * 2 + (half + 2))
                    cols = slice(512 * half, 512 * half + 512)
                    nc.vector.tensor_tensor(y_lo[:, cols], ps[:, 4 + half, :], y_hi[:, cols].bitcast(F32),
                                            ALU.subtract).then_inc(m_ylo, 1)

            def add_rows(n):
                for t, bank in ((1, 4), (0, 6)):
                    dve.wait_ge(m_scattered, n * 2 + (2 - t))
                    nc.vector.scalar_tensor_tensor(
                        out=h[:, t, :], in0=ps[:, bank:bank + 2, :].rearrange("p b n -> p (b n)"),
                        scalar=e_gate[:, t, bass.ds(n, 1)], in1=h[:, t, :], op0=ALU.mult,
                        op1=ALU.add).then_inc(m_added, 1)

            picks(0)
            eg, eg2 = e_gate[:, :, 1:1 + N_EXP], e_gate[:, :, 1 + N_EXP:]
            link(nc.vector.tensor_reduce(top, logit[:, :, :], AX.X, ALU.max))
            nc.vector.tensor_tensor(eg, logit[:, :, :], spread(top, N_EXP), ALU.subtract).then_inc(chosen_ready, 1)
            nc.vector.memset(pickT[:, :].bitcast(F32), 0.0).then_inc(m_pickT_copied, 1)
            dve.wait_ge(lexp_ready, 1)
            link(nc.vector.tensor_tensor(eg, eg, chosen[:, :, :], ALU.mult))
            link(nc.vector.tensor_reduce(gsum, eg, AX.X, ALU.add))
            link(nc.vector.reciprocal(gsum, gsum))
            link(nc.vector.tensor_tensor(eg2, eg, spread(gsum, N_EXP), ALU.mult))
            link(nc.vector.tensor_copy(eg, eg2))
            dve.wait_ge(passes_ready, 1)
            passes = dve.value_load(passes_t[0:1, 0:1], min_val=1, max_val=2)
            expert_rows_lo(0)
            with dve.Fori(0, passes) as ps_i:
                with dve.Fori(0, N_EXP) as e:
                    n = ps_i * N_EXP + e
                    r0 = n * N_MB

                    def mult(m, c, r):
                        dve.wait_ge(tile_used, nth(c, r))
                        dve.wait_ge(m_silu, m)
                        nc.vector.tensor_tensor(ff[:, :], silu_g[:, :], ps[:, 1, :], ALU.mult).then_inc(m_act, 1)

                    def lower_T(m):
                        dve.wait_ge(m_hi, m)
                        nc.vector.tensor_tensor(ff_lo[:, :], ps[:, 2, :], ff_hi[:, :].bitcast(F32),
                                                ALU.subtract).then_inc(m_lo, 1)

                    for c in range(2, 6):
                        split_lo(dve, T_MOE + c, r0)
                    mult(r0 + 1, T_MOE + 3, r0)
                    add_rows(n)
                    dve.wait_ge(m_pickT, n + 1)
                    picks(n + 1)
                    with dve.Fori(1, N_MB) as b:
                        r = r0 + b - 1
                        split_lo(dve, T_MOE + 6, r)
                        lower_T(r0 + b)
                        for c in range(7, 11):
                            split_lo(dve, T_MOE + c, r)
                        mult(r0 + b + 1, T_MOE + 7, r)
                        split_lo(dve, T_MOE + 11, r)
                    r1 = r0 + N_MB
                    lower_T(r1)
                    split_lo(dve, T_MOE + 0, r1)
                    expert_rows_lo(n + 1)
                    split_lo(dve, T_MOE + 1, r1)
                    expert_out_lo(n)
            for m in range(2):
                dve.wait_ge(m_scattered, passes * (2 * N_EXP) + (m + 1))
                for t in range(TT):
                    cols = slice(512 * m, 512 * m + 512)
                    ins = nc.vector.scalar_tensor_tensor(
                        out=h[:, t, cols], in0=ps[:, (6, 4)[t] + m, :],
                        scalar=e_gate[:, t, bass.ds(passes * N_EXP, 1)], in1=h[:, t, cols], op0=ALU.mult, op1=ALU.add)
                ins.then_inc(m_added, 1)
            for half in range(2):
                norm_lo(5, 1, V_PLE, half)
            split_lo(dve, T_GATE[1] + 2, passes * (N_EXP * N_MB))
            norm_rstd(5)
            ple_add(1, passes * (N_EXP * N_MB))
            dve.wait_ge(frow_landed, 16)
            for t in range(TT):
                dve.wait_ge(std_ready, 7 + t)
                link(nc.vector.reciprocal(rstd[:, t:t + 1], std[:, t:t + 1]))
                nc.vector.scalar_tensor_tensor(out=xn[:, t, :], in0=h[:, t, :], scalar=rstd[:, t:t + 1],
                                               in1=g_row[:, :], op0=ALU.mult, op1=ALU.mult).then_inc(out_ready, 1)

        @block.tensor
        def _(pe):
            def transpose(dst, src, n=P):
                return nc.tensor.transpose(dst, src, ident[0:n, 0:n])

            def norm_T(q, half):
                if 1 <= q <= 4:
                    pe.wait_ge(h_updated, h_half(q, half))
                if q == 3:
                    pe.wait_ge(up_ready, 1)
                for k in range(4 * half, 4 * half + 4):
                    for t in range(TT):
                        ins = transpose(xT(q, k)[:, t * P:(t + 1) * P], h[:, t, k * P:(k + 1) * P])
                    if k % 2:
                        ins.then_inc(xnT_ready, 1)

            def x_ready(q, half):
                pe.wait_ge(xlo_ready, 8 * q + 4 * (half + 1))

            def tile(c, r=None):
                pe.wait_ge(lo_ready, nth(c, r))
                return w_hi[:, c % SPLIT, :], w_lo[:, c % SPLIT, :]

            def columns(c, r, bank, width, half, x_of, between=None, order=range(4), first=None, at=1):
                wh, wl = tile(c, r)
                wh, wl = (w[:, 0:4 * width].rearrange("p (k n) -> p k n", k=4) for w in (wh, wl))
                first = half == 0 if first is None else first
                for n, kk in enumerate(order):
                    for t in range(TT):
                        xh, xl = (a[:, t * P:(t + 1) * P] for a in x_of(4 * half + kk))
                        ins = products(ps[:, bank + t, 0:width], xh, xl, wh[:, kk, :], wl[:, kk, :],
                                       first and n == 0, not first and n == 3)
                    if n == at and between:
                        between()
                ins.then_inc(tile_used, 1)

            def rows_tile(c, r, bank, xh, xl, start, stop, between=None):
                wh, wl = tile(c, r)
                wh, wl = (w.rearrange("p (k m n) -> p k m n", k=2, m=2) for w in (wh, wl))
                for k in range(2):
                    for t in range(TT):
                        for m in range(2):
                            ins = products(ps[:, bank + 2 * t + m, :], xh[:, k, t * P:(t + 1) * P],
                                           xl[:, k, t * P:(t + 1) * P], wh[:, k, m, :], wl[:, k, m, :],
                                           start and k == 0, stop and k == 1)
                        if between and 2 * k + t in between:
                            between[2 * k + t]()
                ins.then_inc(tile_used, 1)

            def in_proj(l):
                q = 3 * l
                x_ready(q, 0)
                for b, (c0, c1) in enumerate(IN_BLOCKS):
                    if b >= 2:
                        pe.wait_ge(z_ready, 8 * l + Z_DONE[b - 2])
                    for half in range(2):
                        if b == 0 and half == 1:
                            x_ready(q, 1)
                        columns(T_IN[l] + 2 * b + half, None, 2 * (b % 2), c1 - c0, half, lambda k: x_parts(q, k),
                                (lambda: norm_T(3, 1)) if l and b == 0 and half == 0 else None)
                        if (l, b, half) == (0, 1, 0):
                            pe.wait_ge(vec_landed, 16 * N_VEC_DMAS)
                            pe.wait_ge(rest_landed, 16)
                            for i in range(DEPTH):
                                ins = transpose(ps[:, 6 + i, 0:V_ROWS], vrows[0:V_ROWS, i, :], V_ROWS)
                            ins.then_inc(vecT_ready, 1)
                        if b == 1 and half == 0:
                            pe.wait_ge(u_ready, l + 1)
                            for j in range(2):
                                for t in range(TT):
                                    ins = transpose(ps[:, 4, j * SEQ + t * P:j * SEQ + (t + 1) * P],
                                                    z[:, t, j * P:(j + 1) * P])
                            ins.then_inc(uT_ready, 1)
                        if b == 2 and half == 0:
                            if l == 0:
                                pe.wait_ge(misc_landed, 16 * N_MISC)
                            for j in range(2):
                                for t in range(TT):
                                    ins = transpose(ps[:, 5, j * SEQ + t * P:j * SEQ + (t + 1) * P],
                                                    pt[:, l, t, j * P:(j + 1) * P])
                            ins.then_inc(pT_ready, 1)
                        if b == B_RZ and half == 1:
                            pe.wait_ge(plo_ready, l + 1)
                            pe.wait_ge(rope_done, 4 * (l + 1))
                            pe.wait_ge(uT_copied, l + 1)
                            for c, banks in ((C_DQ, (5, 6)), (C_DK, (7, 4))):
                                for t in range(TT):
                                    for i in range(HEADS):
                                        ins = transpose(ps[:, banks[t], i * P:(i + 1) * P], z[:, t, c + i * P:c + (i + 1) * P])
                                    ins.then_inc(qkT_ready, 1)
                        if b == 4 and half == 0:
                            pe.wait_ge(z_ready, 8 * l + Z_DONE[B_RZ])
                            pe.wait_ge(qT_copied, 2 * l + 2)
                            for t in range(TT):
                                ins = transpose(ps[0:RANK, 5, SEQ + t * P:SEQ + (t + 1) * P], z[:, t, C_GZ:D_IN])
                            ins.then_inc(gzT_ready, 1)
                            pe.wait_ge(kT_copied, 2 * l + 2)
                            scores(l, 0)
                            pe.wait_ge(gzT_copied, l + 1)
                            for t in range(TT):
                                ins = nc.tensor.matmul(ps[:, 5, t * P:(t + 1) * P], gzT[0:RANK, t * P:(t + 1) * P],
                                                       w_g2[0:RANK, l, :], start=True, stop=True)
                            ins.then_inc(gpre_ready, 1)
                        if b == 5 and half == 0:
                            pe.wait_ge(la_ready, l + 1)
                            for t in range(TT):
                                nc.tensor.matmul(ps[:, 5, t * P:(t + 1) * P], cst[:, K_REV:K_REV + P], log_a[:, t, :],
                                                 start=True, stop=True)
                            for t in range(TT):
                                ins = nc.tensor.matmul(ps[:, 5, SEQ + 2 * t:SEQ + 2 * t + 2], log_a[:, t, :],
                                                       cst[:, K_HALF:K_HALF + 2], start=True, stop=True)
                            ins.then_inc(rev_ready, 1)
                            pe.wait_ge(z_ready, 8 * l + Z_DONE[4])
                            pe.wait_ge(exp_ready, 2 * HEADS * (TT * l + 1))
                            scores(l, 1)
                            probs_T(l, 0)

            def scores(l, t):
                n = P * (t + 1)
                per_bank = 512 // n
                for c in range(2):
                    for i in range(HEADS):
                        nc.tensor.matmul(score(t, c, i), qT[c * DH:(c + 1) * DH, i, t * P:(t + 1) * P],
                                         kT[c * DH:(c + 1) * DH, i, 0:n], start=i % per_bank == 0, stop=False)
                    for i in range(0, HEADS, per_bank):
                        bank = (6 + c) if t == 0 else (0, 6)[c] + i // 2
                        ins = nc.tensor.matmul(ps[:, bank, :].rearrange("p (i n) -> p i n", n=n)[:, :, n - CHUNK:],
                                               cst[0:1, K_MASK:K_MASK + P],
                                               cst[0:1, K_ONES:K_ONES + CHUNK].rearrange("p (o n) -> p o n", o=1)
                                               .broadcast_to([1, per_bank, CHUNK]), start=False, stop=True)
                    if t or c:
                        ins.then_inc(scores_ready, 1)

            def probs_T(l, t):
                pe.wait_ge(a_ready, HEADS * (TT * l + t + 1))
                for kt in range(t + 1):
                    for i in range(HEADS):
                        ins = transpose(ps[:, (4, 0)[t] + kt, i * P:(i + 1) * P], probs[:, i, kt * P:(kt + 1) * P])
                ins.then_inc(aT_ready, 1)

            def values(l, t):
                pe.wait_ge(aT_copied, 3 * l + (1 if t == 0 else 3))
                for i in range(HEADS):
                    for kt in range(t + 1):
                        ins = nc.tensor.matmul(ps[:, O_BANK[t], i * DV:(i + 1) * DV], aT[:, kt, i * P:(i + 1) * P],
                                               z[:, kt, C_DV + i * DV:C_DV + (i + 1) * DV],
                                               start=kt == 0, stop=kt == t)
                ins.then_inc(o_ready, 1)

            def o_T(l, t):
                pe.wait_ge(on_ready, TT * l + t + 1)
                for i in range(HEADS):
                    ins = transpose(ps[:, OT_BANK[t], i * P:(i + 1) * P], on[:, i * DV:(i + 1) * DV])
                ins.then_inc(onT_ready, 1)

            def mixer(l):
                values(l, 0)
                probs_T(l, 1)
                pe.wait_ge(z_ready, 8 * l + 8)
                for t in range(TT):
                    ins = transpose(ps[:, 2, t * P:(t + 1) * P], z[:, t, C_GQ:C_GK])
                ins.then_inc(gqT_ready, 1)
                pe.wait_ge(kx_ready, 2 * l + 2)
                pe.wait_ge(gqT_copied, l + 1)
                for t in range(TT):
                    for half in range(2):
                        ins = nc.tensor.matmul(ps[:, 3 - t, half * 256:half * 256 + 256], kx_half[:, t, half, :],
                                               z[:, t, C_GV:C_GR], start=True, stop=True)
                    ins.then_inc(kv_ready, 1)
                values(l, 1)
                o_T(l, 0)
                pe.wait_ge(state_ready, 3 * (l + 1))
                for t in range(TT):
                    for half in range(2):
                        ins = nc.tensor.matmul(ps[half * CHUNK:(half + 1) * CHUNK, 7, t * 256:t * 256 + 256],
                                               gqT[:, t * P + half * CHUNK:t * P + (half + 1) * CHUNK],
                                               state[:, 2 * t + half, :], start=True, stop=True)
                ins.then_inc(go_ready, 1)
                o_T(l, 1)

            def gla_T(l):
                pe.wait_ge(gon_ready, l + 1)
                for j in range(2):
                    for t in range(TT):
                        ins = transpose(ps[:, 6, j * SEQ + t * P:j * SEQ + (t + 1) * P],
                                        silu_g[:, t * 256 + j * P:t * 256 + (j + 1) * P])
                ins.then_inc(gonT_ready, 1)

            def mean(l):
                pe.wait_ge(tap_done, 2 * TAPS * (l + 1))
                for j in range(2):
                    ins = nc.tensor.matmul(ps[:, 5, 0:SEQ], cst[:, K_MEAN:K_MEAN + P], yc[:, j, :], start=j == 0, stop=j == 1)
                ins.then_inc(mean_ready, 1)

            def variance(l):
                pe.wait_ge(ysq_ready, l + 1)
                for j in range(2):
                    ins = nc.tensor.matmul(ps[:, 5, SEQ:2 * SEQ], cst[:, K_MEAN:K_MEAN + P], ysq[:, j, :], start=j == 0, stop=j == 1)
                ins.then_inc(var_ready, 1)

            def square(first, r, x_of, bank=0, next_norm=None, second_half=None):
                for b in range(2):
                    for half in range(2):
                        if (b, half) == (0, 1) and second_half:
                            second_half()
                        columns(first + 2 * b + half, r, bank + 2 * b, 512, half, x_of,
                                (lambda: norm_T(next_norm, 0)) if b == 1 and half == 0 and next_norm is not None else None,
                                at=2)

            def out_proj(l):
                def part(i, chunks):
                    b, half = MIX_TILES[i]
                    wh, wl = (w.rearrange("p (k n) -> p k n", k=4) for w in tile(T_OUT[l] + i))
                    for kk in chunks:
                        k = 4 * half + kk
                        for t in range(TT):
                            ins = products(ps[:, 2 * b + t, :], x_hi[:, k, t * P:(t + 1) * P], x_lo[:, k, t * P:(t + 1) * P],
                                           wh[:, kk, :], wl[:, kk, :], k == 4, k == 1)
                    return ins

                pe.wait_ge(mixlo_ready, 4 * l + 2)
                part(0, (0, 1))
                gla_T(l)
                part(1, (0,))
                mean(l)
                part(1, (1,))
                variance(l)
                pe.wait_ge(mixlo_ready, 4 * l + 3)
                part(0, (2, 3)).then_inc(tile_used, 1)
                part(1, (2, 3)).then_inc(tile_used, 1)
                part(2, (2, 3))
                pe.wait_ge(mixlo_ready, 4 * l + 4)
                part(2, (0, 1)).then_inc(tile_used, 1)
                part(3, (2, 3))
                norm_T(3 * l + 1, 0)
                part(3, (0, 1)).then_inc(tile_used, 1)

            def up_proj(l, between=None):
                rows_tile(T_UP[l], None, 0, p_hi, p_lo, True, True, between)

            pe.wait_ge(ident_landed, 16)
            pe.wait_ge(gain_landed, 16)
            transpose(ps[:, 0, 0:KC], vrows[0:KC, 0, :], KC).then_inc(gainT_ready, 1)
            pe.wait_ge(x_landed, 16)
            for half in range(2):
                norm_T(0, half)
            for l in range(DEPTH):
                in_proj(l)
                mixer(l)
                out_proj(l)
                if l == 0:
                    def gate_up(c, r):
                        for half in range(2):
                            if r is None and half == 1:
                                x_ready(1, 1)
                            columns(c + half, r, 0, 512, half, lambda k: x_parts(1, k),
                                    (lambda: norm_T(1, 1)) if r is None and half == 0 else None)

                    def ffn_T(b):
                        pe.wait_ge(f_act, b + 1)
                        for k in range(2):
                            for t in range(TT):
                                ins = transpose(ps[:, 2, k * SEQ + t * P:k * SEQ + (t + 1) * P],
                                                ff[:, t * FB + k * P:t * FB + (k + 1) * P])
                        ins.then_inc(f_T, 1)

                    def down(c, r, b, stop):
                        pe.wait_ge(f_lo, b + 1)
                        rows_tile(c, r, 4, ff_hi[:, :].rearrange("p (k n) -> p k n", k=2),
                                  ff_lo[:, :].rearrange("p (k n) -> p k n", k=2), False, stop)

                    x_ready(1, 0)
                    gate_up(T_FFN, None)
                    for b in range(4):
                        nc.tensor.matmul(ps[:, 4 + b, :], x_hi[:, 0, 0:P], zeros[:, :], start=True, stop=False)
                    ffn_T(0)
                    with pe.Fori(0, (N_FB - 1) // 2) as i:
                        for s in range(2):
                            b = i * 2 + (1 + s)
                            gate_up(T_FFN + 2 + 3 * s, i)
                            down(T_FFN + 4 + 3 * s, i, b - 1, False)
                            ffn_T(b)
                    down(T_UP[0] - 1, None, N_FB - 1, True)
                    def norm_2_T():
                        pe.wait_ge(h_updated, h_half(2, 1))
                        for half in range(2):
                            norm_T(2, half)

                    up_proj(0, {1: norm_2_T})
                    x_ready(2, 0)
                    square(T_GATE[0], None, lambda k: x_parts(2, k), 4, 3, lambda: x_ready(2, 1))
            def logits_T(half):
                x_ready(4, half)
                for k in range(4 * half, 4 * half + 4):
                    for i, a in enumerate(x_parts(4, k)):
                        ins = nc.tensor.matmul(ps[0:2 * N_EXP, 4, 0:SEQ], rw_parts[:, k, :], a,
                                               start=k + i == 0, stop=k + i == KC)
                if half:
                    ins.then_inc(logitT_ready, 1)

            def logits():
                pe.wait_ge(logitT_copied, 1)
                for t in range(TT):
                    ins = nc.tensor.matmul(ps[:, 5, t * N_EXP:(t + 1) * N_EXP], gzT[0:2 * N_EXP, t * P:(t + 1) * P],
                                           cst[0:2 * N_EXP, K_FOLD:K_FOLD + N_EXP], start=True, stop=True)
                ins.then_inc(logit_ready, 1)

            def ranks():
                pe.wait_ge(chosen_ready, 1)
                nc.tensor.matmul(ps[:, 6, 0:N_EXP], cst[:, K_RANK:K_RANK + P], chosen[:, 0, :], start=True, stop=True)
                nc.tensor.matmul(ps[:, 6, N_EXP:2 * N_EXP], cst[:, K_ONES:K_ONES + P], chosen[:, 0, :], start=True, stop=False)
                nc.tensor.matmul(ps[:, 6, N_EXP:2 * N_EXP], cst[:, K_RANK:K_RANK + P], chosen[:, 1, :], start=False, stop=True)
                nc.tensor.matmul(ps[:, 6, 2 * N_EXP:3 * N_EXP], cst[:, K_ONES:K_ONES + P], chosen[:, 0, :], start=True, stop=False)
                nc.tensor.matmul(ps[:, 6, 2 * N_EXP:3 * N_EXP], cst[:, K_ONES:K_ONES + P], chosen[:, 1, :], start=False,
                                 stop=True).then_inc(rank_ready, 1)

            pe.wait_ge(rw_lo_ready, 1)
            logits_T(0)
            norm_T(4, 1)
            up_proj(1, {1: lambda: logits_T(1), 2: logits})
            ranks()
            pe.wait_ge(xg_ready, 2)
            pe.wait_ge(passes_ready, 1)
            passes = pe.value_load(passes_t[0:1, 0:1], min_val=1, max_val=2)

            def gather(n):
                pe.wait_ge(m_pick, n * 2 + 2)
                for k in range(KC):
                    for t in range(TT):
                        ins = nc.tensor.matmul(ps[:, 6 + k // 4, (k % 4) * P:(k % 4 + 1) * P],
                                               xn[:, t, k * P:(k + 1) * P], pick[:, t, :], start=t == 0, stop=t == 1)
                    if k % 4 == 3:
                        ins.then_inc(m_gathered, 1)

            def scatter(n):
                pe.wait_ge(m_pickT_copied, n + 1)
                pe.wait_ge(m_ylo, n * 2 + 1)
                for t, bank in ((1, 4), (0, 6)):
                    for m in range(2):
                        cols = slice(512 * m, 512 * m + 512)
                        nc.tensor.matmul(ps[:, bank + m, :], pickT[:, t * P:(t + 1) * P], y_hi[:, cols],
                                         start=True, stop=False)
                        ins = nc.tensor.matmul(ps[:, bank + m, :], pickT[:, t * P:(t + 1) * P], y_lo[:, cols],
                                               start=False, stop=True)
                    ins.then_inc(m_scattered, 1)

            def last_scatter(n):
                pe.wait_ge(m_pickT_copied, n + 1)
                pe.wait_ge(m_xlo, n * 2 + 2)
                for m in range(2):
                    cols = slice(512 * m, 512 * m + 512)
                    pe.wait_ge(m_yhi, n * 2 + m)
                    nc.tensor.matmul(ps[:, 6 + m, :], pickT[:, 0:P], y_hi[:, cols], start=True, stop=False)
                    pe.wait_ge(m_ylo, n * 2 + m)
                    nc.tensor.matmul(ps[:, 6 + m, :], pickT[:, 0:P], y_lo[:, cols], start=False, stop=True)
                    nc.tensor.matmul(ps[:, 4 + m, :], pickT[:, P:2 * P], y_hi[:, cols], start=True, stop=False)
                    nc.tensor.matmul(ps[:, 4 + m, :], pickT[:, P:2 * P], y_lo[:, cols],
                                     start=False, stop=True).then_inc(m_scattered, 1)

            gather(0)
            with pe.Fori(0, passes) as ps_i:
                with pe.Fori(0, N_EXP) as e:
                    n = ps_i * N_EXP + e
                    r0 = n * N_MB

                    def gate_up(c, r, m, expert=None):
                        pe.wait_ge(m_act, m + 1)
                        for s in range(2):
                            for half in range(2):
                                if expert is not None and s == 0:
                                    pe.wait_ge(m_xlo, expert * 2 + (half + 1))
                                wh, wl = tile(c + 2 * s + half, r)
                                wh, wl = (w.rearrange("p (k n) -> p k n", k=4) for w in (wh, wl))
                                for kk in range(4):
                                    k = 4 * half + kk
                                    ins = products(ps[:, s, :], xe_hi[:, k, :], xe_lo[:, k, :], wh[:, kk, :], wl[:, kk, :],
                                                   k == 0, k == KC - 1)
                                ins.then_inc(tile_used, 1)

                    def act_T(m):
                        pe.wait_ge(m_act, m + 2)
                        pe.wait_ge(m_lo, m + 1)
                        for k in range(4):
                            ins = transpose(ps[:, 2, k * P:(k + 1) * P], ff[:, k * P:(k + 1) * P])
                        ins.then_inc(m_T, 1)

                    def down(c, r, m, stop):
                        pe.wait_ge(m_lo, m + 2)
                        for half in range(2):
                            wh, wl = tile(c + half, r)
                            wh, wl = (w.rearrange("p (k m n) -> p k m n", k=2, m=2) for w in (wh, wl))
                            for kk in range(2):
                                k = 2 * half + kk
                                for s in range(2):
                                    ins = products(ps[:, 4 + s, :], ff_hi[:, k * P:(k + 1) * P], ff_lo[:, k * P:(k + 1) * P],
                                                   wh[:, kk, s, :], wl[:, kk, s, :], False, stop and k == 3)
                            ins.then_inc(tile_used, 1)

                    gate_up(T_MOE, r0, r0, n)
                    scatter(n)
                    for t in range(TT):
                        ins = transpose(ps[:, 3, t * P:(t + 1) * P], pick[:, t, :])
                    ins.then_inc(m_pickT, 1)
                    act_T(r0)
                    pe.wait_ge(m_added, n * 2 + 1)
                    for m in range(2):
                        nc.tensor.matmul(ps[:, 4 + m, :], xe_hi[:, 0, :], zeros[:, :], start=True, stop=False)
                    with pe.Fori(1, N_MB) as b:
                        r = r0 + b - 1
                        gate_up(T_MOE + 4, r, r0 + b)
                        down(T_MOE + 8, r, r, False)
                        act_T(r0 + b)
                    pe.wait_ge(m_added, n * 2 + 2)
                    gather(n + 1)
                    down(T_MOE + 4, r0 + (N_MB - 1), r0 + (N_MB - 1), True)
            last_scatter(passes * N_EXP)
            for half in range(2):
                pe.wait_ge(m_added, passes * (2 * N_EXP) + (half + 1))
                norm_T(5, half)
            x_ready(5, 0)
            square(T_GATE[1], passes * (N_EXP * N_MB), lambda k: x_parts(5, k), 4, second_half=lambda: x_ready(5, 1))


_INS = ["x", "p", "norm_mix_g", "w_in", "conv_w", "conv_b", "conv_ln_g", "conv_ln_b", "diff_lambda", "diff_subln_g",
        "gla_w_gate2", "gla_b_gate", "gla_norm_g", "w_out", "norm_ffn_g", "ffn_w_gu", "ffn_w_down", "router_w",
        "moe_w_gu", "moe_w_down", "ple_w_up", "ple_w_gate", "ple_norm_g", "final_norm_g"]


def kernel(**inputs):
    import concourse.bacc as bacc
    from concourse.bass_utils import run_bass_kernel_spmd

    nc = bacc.Bacc("TRN2", target_bir_lowering=False, num_devices=1)
    arrays, args = {}, []
    for name in _INS:
        arrays[name + "_d"] = np.ascontiguousarray(inputs[name])
    arrays["consts_d"] = constants()
    for name, a in arrays.items():
        args.append(nc.dram_tensor(name, a.shape, mybir.dt.from_np(a.dtype), kind="ExternalInput").ap())
    args.append(nc.dram_tensor("out_d", (1, SEQ, D), F32, kind="ExternalOutput").ap())
    build(nc, *args)
    r = run_bass_kernel_spmd(nc, [arrays], core_ids=[0])
    return r.results[0]["out_d"]
```
